# Optimizing a Trainium2 kernel written in Bass

```python
import jax, jax.numpy as jnp
from jax import lax
import numpy as np
import math

D_MODEL = 1024
BATCH = 1
SEQ = 256
DEPTH = 2

CHUNK = 64
EPS = 1e-6
LRU_WIDTH = D_MODEL
LRU_BLOCKS = 16
LRU_BLOCK_DIM = LRU_WIDTH // LRU_BLOCKS
LRU_CONV = 4
LRU_C = 8.0
RET_QK_DIM = 256
RET_V_DIM = 512
RET_HEADS = D_MODEL // RET_QK_DIM
RET_QK = RET_HEADS * RET_QK_DIM
RET_V = RET_HEADS * RET_V_DIM
ROPE_BASE = 10000.0
SC_WIDTH = D_MODEL
SC_CONV = 3
D_FF = 2816
SPLIT_SIZES = (LRU_WIDTH, LRU_WIDTH, RET_QK, RET_QK, RET_V, RET_V,
               SC_WIDTH, SC_WIDTH, SC_WIDTH, 3 * D_MODEL)
MIX_IN = sum(SPLIT_SIZES)


def rmsnorm(x, g):
    xf = x.astype(jnp.float32)
    xf = xf * lax.rsqrt(jnp.mean(xf * xf, axis=-1, keepdims=True) + EPS)
    return xf.astype(x.dtype) * g

def swiglu(u, w_in, w_out):
    gate, up = jnp.split(u @ w_in, 2, axis=-1)
    return (jax.nn.silu(gate) * up) @ w_out

def causal_depthwise_conv(x, w):
    K, C = w.shape
    return lax.conv_general_dilated(
        x, w[:, None, :].astype(x.dtype), window_strides=(1,), padding=[(K - 1, 0)],
        dimension_numbers=("NWC", "WIO", "NWC"), feature_group_count=C)

def _lin_rec_combine(e1, e2):
    a1, b1 = e1
    a2, b2 = e2
    return a1 * a2, a2 * b1 + b2

def rg_lru(x, w_a, b_a, w_x, b_x, lam):
    Bsz, S, W = x.shape
    xf = x.astype(jnp.float32)
    xb = xf.reshape(Bsz, S, LRU_BLOCKS, LRU_BLOCK_DIM)
    r = jax.nn.sigmoid(jnp.einsum("bsgi,gij->bsgj", xb, w_a.astype(jnp.float32)).reshape(Bsz, S, W)
                       + b_a.astype(jnp.float32))
    i = jax.nn.sigmoid(jnp.einsum("bsgi,gij->bsgj", xb, w_x.astype(jnp.float32)).reshape(Bsz, S, W)
                       + b_x.astype(jnp.float32))
    log_a = -LRU_C * r * jax.nn.softplus(-lam.astype(jnp.float32))
    a = jnp.exp(log_a)
    u = jnp.sqrt(-jnp.expm1(2.0 * log_a)) * (i * xf)
    _, h = lax.associative_scan(_lin_rec_combine, (a, u), axis=1)
    return h.astype(x.dtype)

def rope(t, positions):
    half = t.shape[-1] // 2
    inv_freq = jnp.power(ROPE_BASE, -jnp.arange(half, dtype=jnp.float32) / half)
    ang = positions.astype(jnp.float32)[:, None] * inv_freq[None, :]
    cos = jnp.cos(ang)[None, :, None, :]
    sin = jnp.sin(ang)[None, :, None, :]
    t1, t2 = t[..., :half], t[..., half:]
    return jnp.concatenate([t1 * cos - t2 * sin, t1 * sin + t2 * cos], axis=-1)

def retention(q, k, v, positions):
    Bsz, S, H, dk = q.shape
    dv = v.shape[-1]
    N = S // CHUNK
    q = rope(q.astype(jnp.float32), positions)
    k = rope(k.astype(jnp.float32), positions) * (dk ** -0.5)
    v = v.astype(jnp.float32)
    log_g = jnp.log1p(-jnp.power(2.0, -5.0 - jnp.arange(H, dtype=jnp.float32)))
    idx = jnp.arange(CHUNK, dtype=jnp.float32)
    intra_decay = jnp.exp(log_g[:, None, None] * jnp.abs(idx[:, None] - idx[None, :]))
    q_decay = jnp.exp(log_g[:, None] * (idx[None, :] + 1.0))
    k_decay = jnp.exp(log_g[:, None] * (CHUNK - 1.0 - idx[None, :]))
    chunk_decay = jnp.exp(log_g * CHUNK)

    def to_chunks(t):
        return t.reshape(Bsz, N, CHUNK, H, t.shape[-1]).transpose(1, 0, 3, 2, 4)

    qc, kc, vc = to_chunks(q), to_chunks(k), to_chunks(v)
    scores = jnp.einsum("nbhid,nbhjd->nbhij", qc, kc) * intra_decay
    intra = jnp.einsum("nbhij,nbhje->nbhie", scores, vc)

    def step(state, inp):
        qn, kn, vn = inp
        cross = jnp.einsum("bhid,bhde->bhie", qn, state) * q_decay[None, :, :, None]
        state = state * chunk_decay[None, :, None, None] + jnp.einsum(
            "bhjd,bhje->bhde", kn * k_decay[None, :, :, None], vn)
        return state, cross

    state0 = jnp.zeros((Bsz, H, dk, dv), jnp.float32)
    _, cross = lax.scan(step, state0, (qc, kc, vc))
    out = (intra + cross).transpose(1, 0, 3, 2, 4).reshape(Bsz, S, H, dv)
    out = out * lax.rsqrt(jnp.mean(out * out, axis=-1, keepdims=True) + EPS)
    return out

def hybrid_mixer(u, positions, w_in, lru_conv_w, lru_conv_b, lru_w_a, lru_b_a, lru_w_x, lru_b_x,
                 lru_lambda, w_lru_out, w_ret_out, sc_conv_w, w_sc_out, w_out):
    Bsz, S, _ = u.shape
    proj = u @ w_in
    cuts = [int(c) for c in np.cumsum(SPLIT_SIZES)[:-1]]
    xa, ya, q, k, v, g, sb, sc, sh, gates = jnp.split(proj, cuts, axis=-1)
    xa = causal_depthwise_conv(xa, lru_conv_w) + lru_conv_b
    ha = rg_lru(xa, lru_w_a, lru_b_a, lru_w_x, lru_b_x, lru_lambda)
    oa = (ha * jax.nn.gelu(ya)) @ w_lru_out
    ret = retention(q.reshape(Bsz, S, RET_HEADS, RET_QK_DIM),
                    k.reshape(Bsz, S, RET_HEADS, RET_QK_DIM),
                    v.reshape(Bsz, S, RET_HEADS, RET_V_DIM), positions)
    ob = (jax.nn.silu(g) * ret.reshape(Bsz, S, RET_V).astype(u.dtype)) @ w_ret_out
    oc = (sb * causal_depthwise_conv(sc * sh, sc_conv_w)) @ w_sc_out
    ga, gb, gc = jnp.split(jax.nn.sigmoid(gates), 3, axis=-1)
    return (ga * oa + gb * ob + gc * oc) @ w_out

def first_inputs(seed: int = 0) -> dict:
    key = jax.random.key(seed)
    ks = jax.random.split(key, 32)
    L = DEPTH

    def nrm(k, shape, scale):
        return jax.random.normal(k, shape, jnp.float32) * scale

    def gain(k):
        return 1.0 + 0.02 * jax.random.normal(k, (L, D_MODEL), jnp.float32)

    a_target = jax.random.uniform(ks[2], (L, LRU_WIDTH), jnp.float32, minval=0.9, maxval=0.999)
    s = a_target ** (1.0 / LRU_C)
    lru_lambda = jnp.log(s) - jnp.log1p(-s)
    offset = CHUNK * jax.random.randint(ks[3], (), 0, 64, dtype=jnp.int32)
    return {
        "x": nrm(ks[0], (BATCH, SEQ, D_MODEL), 1.0),
        "positions": offset + jnp.arange(SEQ, dtype=jnp.int32),
        "ffn1_pre_g": gain(ks[4]),
        "ffn1_w_in": nrm(ks[5], (L, D_MODEL, 2 * D_FF), D_MODEL ** -0.5),
        "ffn1_w_out": nrm(ks[6], (L, D_FF, D_MODEL), D_FF ** -0.5),
        "ffn1_post_g": gain(ks[7]),
        "mix_pre_g": gain(ks[8]),
        "w_mix_in": nrm(ks[9], (L, D_MODEL, MIX_IN), D_MODEL ** -0.5),
        "lru_conv_w": nrm(ks[10], (L, LRU_CONV, LRU_WIDTH), LRU_CONV ** -0.5),
        "lru_conv_b": nrm(ks[11], (L, LRU_WIDTH), 0.01),
        "lru_w_a": nrm(ks[12], (L, LRU_BLOCKS, LRU_BLOCK_DIM, LRU_BLOCK_DIM), LRU_BLOCK_DIM ** -0.5),
        "lru_b_a": nrm(ks[13], (L, LRU_WIDTH), 0.01),
        "lru_w_x": nrm(ks[14], (L, LRU_BLOCKS, LRU_BLOCK_DIM, LRU_BLOCK_DIM), LRU_BLOCK_DIM ** -0.5),
        "lru_b_x": nrm(ks[15], (L, LRU_WIDTH), 0.01),
        "lru_lambda": lru_lambda,
        "w_lru_out": nrm(ks[16], (L, LRU_WIDTH, D_MODEL), LRU_WIDTH ** -0.5),
        "w_ret_out": nrm(ks[17], (L, RET_V, D_MODEL), RET_V ** -0.5),
        "sc_conv_w": nrm(ks[18], (L, SC_CONV, SC_WIDTH), SC_CONV ** -0.5),
        "w_sc_out": nrm(ks[19], (L, SC_WIDTH, D_MODEL), SC_WIDTH ** -0.5),
        "w_mix_out": nrm(ks[20], (L, D_MODEL, D_MODEL), D_MODEL ** -0.5),
        "mix_post_g": gain(ks[21]),
        "ffn2_pre_g": gain(ks[22]),
        "ffn2_w_in": nrm(ks[23], (L, D_MODEL, 2 * D_FF), D_MODEL ** -0.5),
        "ffn2_w_out": nrm(ks[24], (L, D_FF, D_MODEL), D_FF ** -0.5),
        "ffn2_post_g": gain(ks[25]),
    }

def first_block(x, positions, ffn1_pre_g, ffn1_w_in, ffn1_w_out, ffn1_post_g, mix_pre_g, w_mix_in,
              lru_conv_w, lru_conv_b, lru_w_a, lru_b_a, lru_w_x, lru_b_x, lru_lambda, w_lru_out,
              w_ret_out, sc_conv_w, w_sc_out, w_mix_out, mix_post_g, ffn2_pre_g, ffn2_w_in,
              ffn2_w_out, ffn2_post_g):
    for l in range(DEPTH):
        h = swiglu(rmsnorm(x, ffn1_pre_g[l]), ffn1_w_in[l], ffn1_w_out[l])
        x = x + 0.5 * rmsnorm(h, ffn1_post_g[l])
        h = hybrid_mixer(rmsnorm(x, mix_pre_g[l]), positions, w_mix_in[l], lru_conv_w[l],
                         lru_conv_b[l], lru_w_a[l], lru_b_a[l], lru_w_x[l], lru_b_x[l],
                         lru_lambda[l], w_lru_out[l], w_ret_out[l], sc_conv_w[l], w_sc_out[l],
                         w_mix_out[l])
        x = x + rmsnorm(h, mix_post_g[l])
        h = swiglu(rmsnorm(x, ffn2_pre_g[l]), ffn2_w_in[l], ffn2_w_out[l])
        x = x + 0.5 * rmsnorm(h, ffn2_post_g[l])
    return x


DEPTH_2 = 1

HEAD_DIM = 64
N_HEADS_A = 8
N_KV_A = 2
GROUP_A = N_HEADS_A // N_KV_A
WINDOW_A = 128
N_HEADS_B = 8
DILATED_PATTERNS = ((128, 1), (512, 4), (2048, 16))
WIDTH_A = N_HEADS_A * HEAD_DIM
WIDTH_B = N_HEADS_B * HEAD_DIM
D_MIX = WIDTH_A + WIDTH_B
KV_WIDTH_A = N_KV_A * HEAD_DIM
D_IN_PROJ = WIDTH_A + 2 * KV_WIDTH_A + 3 * WIDTH_B
N_BIAS_HEADS = N_HEADS_A + N_HEADS_B
NUM_BUCKETS = 32
MAX_DISTANCE = 1024
D_FF_2 = 4 * D_MODEL
PLE_DIM = 256
NEG = -1e30


def rmsnorm_2(x, g):
    xf = x.astype(jnp.float32)
    y = xf * lax.rsqrt(jnp.mean(xf * xf, axis=-1, keepdims=True) + EPS)
    return (y * g.astype(jnp.float32)).astype(x.dtype)

def t5_bucket(rel):
    half = NUM_BUCKETS // 2
    max_exact = half // 2
    sign = jnp.where(rel > 0, half, 0)
    n = jnp.abs(rel)
    nf = jnp.maximum(n, 1).astype(jnp.float32)
    large = max_exact + (jnp.log(nf / max_exact) / math.log(MAX_DISTANCE / max_exact)
                         * (half - max_exact)).astype(jnp.int32)
    large = jnp.minimum(large, half - 1)
    return sign + jnp.where(n < max_exact, n, large)

def band_rel(block):
    qi = jnp.arange(block)[:, None]
    ki = jnp.arange(3 * block)[None, :]
    return ki - block - qi

def banded_attention(q, k, v, bias, half_window, block, sink):
    b_, hk, g, L, dh = q.shape
    nb = -(-L // block)
    lp = nb * block
    q = jnp.pad(q, ((0, 0), (0, 0), (0, 0), (0, lp - L), (0, 0)))
    kv_pad = ((0, 0), (0, 0), (block, lp - L + block), (0, 0))
    kp = jnp.pad(k, kv_pad).reshape(b_, hk, nb + 2, block, dh)
    vp = jnp.pad(v, kv_pad).reshape(b_, hk, nb + 2, block, dh)
    kw = jnp.concatenate([kp[:, :, :-2], kp[:, :, 1:-1], kp[:, :, 2:]], axis=3)
    vw = jnp.concatenate([vp[:, :, :-2], vp[:, :, 1:-1], vp[:, :, 2:]], axis=3)
    qb = q.reshape(b_, hk, g, nb, block, dh)
    s = jnp.einsum('bhgnqd,bhnkd->bhgnqk', qb, kw).astype(jnp.float32) * (dh ** -0.5)
    s = s + bias[:, :, None]
    rel = band_rel(block)
    kpos = jnp.arange(nb)[:, None, None] * block + jnp.arange(3 * block)[None, None, :] - block
    valid = (jnp.abs(rel) <= half_window)[None] & (kpos >= 0) & (kpos < L)
    s = jnp.where(valid, s, NEG)
    m = jnp.max(s, axis=-1, keepdims=True)
    if sink is not None:
        sinkb = sink.astype(jnp.float32)[None, :, :, None, None, None]
        m = jnp.maximum(m, sinkb)
    e = jnp.exp(s - m)
    denom = jnp.sum(e, axis=-1, keepdims=True)
    if sink is not None:
        denom = denom + jnp.exp(sinkb - m)
    o = jnp.einsum('bhgnqk,bhnkd->bhgnqd', e, vw.astype(jnp.float32)) / denom
    lse = (jnp.log(denom) + m)[..., 0]
    o = o.reshape(b_, hk, g, lp, dh)[:, :, :, :L].astype(k.dtype)
    lse = lse.reshape(b_, hk, g, lp)[..., :L]
    return o, lse

def windowed_gqa_sink(qa, ka, va, bias_table, sink):
    b_, s_, _ = qa.shape
    q = qa.reshape(b_, s_, N_KV_A, GROUP_A, HEAD_DIM).transpose(0, 2, 3, 1, 4)
    k = ka.reshape(b_, s_, N_KV_A, HEAD_DIM).transpose(0, 2, 1, 3)
    v = va.reshape(b_, s_, N_KV_A, HEAD_DIM).transpose(0, 2, 1, 3)
    bias = bias_table[t5_bucket(band_rel(WINDOW_A))][..., :N_HEADS_A]
    bias = bias.transpose(2, 0, 1).reshape(N_KV_A, GROUP_A, WINDOW_A, 3 * WINDOW_A)
    o, _ = banded_attention(q, k, v, bias.astype(jnp.float32), WINDOW_A, WINDOW_A,
                            sink.reshape(N_KV_A, GROUP_A))
    return o.transpose(0, 3, 1, 2, 4).reshape(b_, s_, WIDTH_A)

def dilated_mixture(qb_, kb_, vb_, bias_table):
    b_, s_, _ = qb_.shape
    to_heads = lambda t: t.reshape(b_, s_, N_HEADS_B, HEAD_DIM).transpose(0, 2, 1, 3)
    q, k, v = to_heads(qb_), to_heads(kb_), to_heads(vb_)
    outs, lses = [], []
    for window, dil in DILATED_PATTERNS:
        half = window // (2 * dil)
        ls = s_ // dil
        sub = lambda t: t.reshape(b_, N_HEADS_B, ls, dil, HEAD_DIM).transpose(0, 1, 3, 2, 4) \
                         .reshape(b_, N_HEADS_B * dil, ls, HEAD_DIM)
        bias = bias_table[t5_bucket(band_rel(half) * dil)][..., N_HEADS_A:]
        bias = jnp.repeat(bias.transpose(2, 0, 1), dil, axis=0)[:, None]
        o, lse = banded_attention(sub(q)[:, :, None], sub(k), sub(v),
                                  bias.astype(jnp.float32), half, half, None)
        o = o.reshape(b_, N_HEADS_B, dil, ls, HEAD_DIM).transpose(0, 1, 3, 2, 4) \
             .reshape(b_, N_HEADS_B, s_, HEAD_DIM)
        lse = lse.reshape(b_, N_HEADS_B, dil, ls).transpose(0, 1, 3, 2).reshape(b_, N_HEADS_B, s_)
        outs.append(o)
        lses.append(lse)
    w = jax.nn.softmax(jnp.stack(lses, axis=0), axis=0)
    o = jnp.sum(w[..., None] * jnp.stack(outs, axis=0).astype(jnp.float32), axis=0).astype(q.dtype)
    return o.transpose(0, 2, 1, 3).reshape(b_, s_, WIDTH_B)

def second_inputs(seed: int = 0) -> dict:
    key = jax.random.key(seed)
    ks = jax.random.split(key, 20)
    nrm = lambda k, shape, scale: (jax.random.normal(k, shape, jnp.float32) * scale)
    gain = lambda k, n: 1.0 + nrm(k, (DEPTH_2, n), 0.02)
    return {
        "x": nrm(ks[0], (BATCH, SEQ, D_MODEL), 1.0),
        "p": nrm(ks[1], (DEPTH_2, BATCH, SEQ, PLE_DIM), 1.0),
        "rel_bias_table": nrm(ks[2], (NUM_BUCKETS, N_BIAS_HEADS), 0.5),
        "g_pre_mix": gain(ks[3], D_MODEL),
        "w_in": nrm(ks[4], (DEPTH_2, D_MODEL, D_IN_PROJ), D_MODEL ** -0.5),
        "sink_a": nrm(ks[5], (DEPTH_2, N_HEADS_A), 0.5),
        "g_out_a": gain(ks[6], WIDTH_A),
        "g_out_b": gain(ks[7], WIDTH_B),
        "w_o": nrm(ks[8], (DEPTH_2, D_MIX, D_MODEL), D_MIX ** -0.5),
        "g_post_mix": gain(ks[9], D_MODEL),
        "g_pre_mlp": gain(ks[10], D_MODEL),
        "w_up": nrm(ks[11], (DEPTH_2, D_MODEL, D_FF_2), D_MODEL ** -0.5),
        "w_down": nrm(ks[12], (DEPTH_2, D_FF_2, D_MODEL), D_FF_2 ** -0.5),
        "g_post_mlp": gain(ks[13], D_MODEL),
        "w_ple_proj": nrm(ks[14], (DEPTH_2, PLE_DIM, D_MODEL), PLE_DIM ** -0.5),
        "w_ple_gate": nrm(ks[15], (DEPTH_2, D_MODEL, D_MODEL), D_MODEL ** -0.5),
        "b_ple_gate": nrm(ks[16], (DEPTH_2, D_MODEL), 0.02),
        "g_post_ple": gain(ks[17], D_MODEL),
    }

def second_block(x, p, rel_bias_table, g_pre_mix, w_in, sink_a, g_out_a, g_out_b, w_o,
              g_post_mix, g_pre_mlp, w_up, w_down, g_post_mlp, w_ple_proj, w_ple_gate,
              b_ple_gate, g_post_ple):
    h = x
    offs = np.cumsum([0, WIDTH_A, KV_WIDTH_A, KV_WIDTH_A, WIDTH_B, WIDTH_B, WIDTH_B])
    for i in range(DEPTH_2):
        u = rmsnorm_2(h, g_pre_mix[i])
        proj = jnp.einsum('bsd,de->bse', u, w_in[i])
        qa, ka, va, qb, kb, vb = [proj[..., offs[j]:offs[j + 1]] for j in range(6)]
        o_a = rmsnorm_2(windowed_gqa_sink(qa, ka, va, rel_bias_table, sink_a[i]), g_out_a[i])
        o_b = rmsnorm_2(dilated_mixture(qb, kb, vb, rel_bias_table), g_out_b[i])
        mix = jnp.einsum('bse,ed->bsd', jnp.concatenate([o_a, o_b], axis=-1), w_o[i])
        h = h + rmsnorm_2(mix, g_post_mix[i])
        v_ = rmsnorm_2(h, g_pre_mlp[i])
        a = jax.nn.relu(jnp.einsum('bsd,df->bsf', v_, w_up[i]))
        ff = jnp.einsum('bsf,fd->bsd', a * a, w_down[i])
        h = h + rmsnorm_2(ff, g_post_mlp[i])
        gate = jax.nn.sigmoid(jnp.einsum('bsd,de->bse', h, w_ple_gate[i]) + b_ple_gate[i])
        ple = jnp.einsum('bsk,kd->bsd', p[i], w_ple_proj[i])
        h = h + rmsnorm_2(gate * ple, g_post_ple[i])
    return h


def setup_inputs(seed=0):
    out = dict(first_inputs(seed))
    for name, value in second_inputs(seed + 1).items():
        if name != "x":
            out[name + "_2"] = value
    return out


def reference(
    x, positions, ffn1_pre_g, ffn1_w_in, ffn1_w_out, ffn1_post_g, mix_pre_g, w_mix_in,
    lru_conv_w, lru_conv_b, lru_w_a, lru_b_a, lru_w_x, lru_b_x, lru_lambda, w_lru_out,
    w_ret_out, sc_conv_w, w_sc_out, w_mix_out, mix_post_g, ffn2_pre_g, ffn2_w_in, ffn2_w_out,
    ffn2_post_g, p_2, rel_bias_table_2, g_pre_mix_2, w_in_2, sink_a_2, g_out_a_2, g_out_b_2,
    w_o_2, g_post_mix_2, g_pre_mlp_2, w_up_2, w_down_2, g_post_mlp_2, w_ple_proj_2,
    w_ple_gate_2, b_ple_gate_2, g_post_ple_2,
):
    x = first_block(
        x, positions, ffn1_pre_g, ffn1_w_in, ffn1_w_out, ffn1_post_g, mix_pre_g, w_mix_in,
        lru_conv_w, lru_conv_b, lru_w_a, lru_b_a, lru_w_x, lru_b_x, lru_lambda, w_lru_out,
        w_ret_out, sc_conv_w, w_sc_out, w_mix_out, mix_post_g, ffn2_pre_g, ffn2_w_in,
        ffn2_w_out, ffn2_post_g,
    )
    return second_block(
        x, p_2, rel_bias_table_2, g_pre_mix_2, w_in_2, sink_a_2, g_out_a_2, g_out_b_2, w_o_2,
        g_post_mix_2, g_pre_mlp_2, w_up_2, w_down_2, g_post_mlp_2, w_ple_proj_2, w_ple_gate_2,
        b_ple_gate_2, g_post_ple_2,
    )


_drawn_inputs = setup_inputs


def setup_inputs(seed=0):
    import zlib

    import numpy as np

    out = dict(_drawn_inputs(seed))
    spreads = {}
    factors = {'lru_b_a': 8.0,
     'lru_b_x': 8.0,
     'ffn2_pre_g': 3.499,
     'ffn2_post_g': 4.916,
     'g_pre_mix_2': 3.913,
     'sink_a_2': 8.0,
     'g_out_a_2': 33.301,
     'g_out_b_2': 34.359,
     'g_post_mix_2': 17.157,
     'g_pre_mlp_2': 20.73,
     'g_post_mlp_2': 26.655,
     'b_ple_gate_2': 38.738,
     'g_post_ple_2': 36.418}
    for name, (base, spread) in spreads.items():
        noise = np.random.default_rng([zlib.crc32(name.encode()), seed]).standard_normal(out[name].shape)
        drawn = base * np.exp(spread * noise) if base else spread * noise
        out[name] = __import__('jax').numpy.asarray(drawn.astype(out[name].dtype))
    for name, factor in factors.items():
        out[name] = (out[name] * factor).astype(out[name].dtype)
    return out
```

```python
from contextlib import ExitStack

import numpy as np
import concourse.bass as bass
from concourse import mybir

F32 = mybir.dt.float32
F32R = mybir.dt.float32r
I32 = mybir.dt.int32
ALU = mybir.AluOpType
ACT = mybir.ActivationFunctionType
AX_X = mybir.AxisListType.X
ds = bass.ds

P = 128
S = 256
D = 1024
DEPTH = 2
EPS = 1e-6
CHUNK = 64
HEADS = 4
HV = 512
D_FF = 2816
TT = S // P
KD = D // P
SLOTC = 256

FFN_PAIRS = D_FF // SLOTC
FIRST_PAIRS = 8
LAST_PAIRS = FFN_PAIRS - FIRST_PAIRS
FFN_IN2 = 3 * FIRST_PAIRS
FFN_OUT2 = FFN_IN2 + 2 * LAST_PAIRS
FFN_SLOTS = FFN_OUT2 + LAST_PAIRS + 1
MIX0 = FFN_SLOTS
STAGES = [("xa", 4), ("q", 4), ("k", 4), ("ya", 4), ("ga", 4), ("lru_out", 4), ("v", 8), ("g", 8),
          ("sc", 4), ("sh", 4), ("gb", 4), ("ret_out", 8), ("sb", 4), ("gc", 4), ("sc_out", 4),
          ("mix_out", 4)]
AT = {}
for _name, _n in STAGES:
    AT[_name] = MIX0 + sum(n for m, n in STAGES[:len(AT)])
FFN2 = MIX0 + sum(n for _, n in STAGES)
SLOTS = FFN2 + FFN_SLOTS
RAW, SPLIT = 4, 2
assert SLOTS % RAW == 0 and SLOTS % SPLIT == 0 and SPLIT == 2

MC = {"xa": 0, "ya": 1024, "q": 2048, "k": 3072, "v": 4096, "g": 6144, "sb": 8192, "sc": 9216,
      "sh": 10240, "ga": 11264, "gb": 12288, "gc": 13312}

V_G1, V_GM, V_CW, V_CB, V_BA, V_BX, V_LAM, V_SW, V_G2, NV = 0, 1, 2, 6, 7, 8, 9, 10, 13, 14
V2_GMIX, V2_GOUT, V2_GMLP = DEPTH * NV, DEPTH * NV + 1, DEPTH * NV + 2
NVEC = DEPTH * NV + 3

B_IN, B_O, B_UP, B_DN, B_UP2, B_DN2, B_GATE, B_PLE, B_SLOTS = 0, 9, 13, 21, 29, 37, 45, 49, 50
NHEAD = 16
BIASW = 384
REL = 2 * S - 1


class Signal:

    def __init__(self, sem, per, primed=0):
        self.sem, self.per, self.primed = sem, per, primed

    def at(self, l, k):
        return l * self.per + (self.primed + k)


class Chain:

    def __init__(self, eng, sem):
        self.eng, self.sem, self.n = eng, sem, 0

    def done(self, ins):
        ins.then_inc(self.sem, 1)
        self.n += 1
        self.eng.wait_ge(self.sem, self.n)

    def restart(self):
        if self.n:
            self.eng.sem_clear(self.sem)
            self.n = 0


def constants():
    half = 128
    inv_freq = (10000.0 ** (-np.arange(half, dtype=np.float64) / half)).astype(np.float32)[:, None]
    log_g = np.log1p(-(2.0 ** (-5.0 - np.arange(HEADS))))
    i, j = np.arange(S)[None, :], np.arange(S)[:, None]
    seen = (j // CHUNK) <= (i // CHUNK)
    full = np.exp(log_g[:, None, None] * np.abs(i - j)) * seen / 16.0
    decay = np.concatenate([full[:, :P, :], full[:, P:, P:]], axis=2).transpose(1, 0, 2)
    d = np.arange(S - 1, -S, -1)
    n = np.abs(d)
    large = 8 + (np.log(np.maximum(n, 1).astype(np.float32) / np.float32(8)) / np.float32(np.log(1024 / 8))
                 * np.float32(8)).astype(np.int32)
    bucket = np.where(d > 0, 16, 0) + np.where(n < 8, n, np.minimum(large, 15))
    onehot = (np.arange(32)[:, None] == bucket[None, :]).astype(np.float32)
    times = (n <= 64).astype(int) + (d % 4 == 0) * (n <= 256) + (d % 16 == 0)
    seen_b = np.where(times > 0, np.log(np.maximum(times, 1)), -1e30)
    seen_a = np.where(n <= 128, 0.0, -1e30)
    allowed = np.concatenate([np.tile(seen_a, (8, 1)), np.tile(seen_b, (8, 1))]).astype(np.float32)
    return {"inv_freq": inv_freq, "decay": np.ascontiguousarray(decay.reshape(P, -1)).astype(np.float32),
            "onehot": onehot, "allowed": allowed}


def build(nc, t, out, scratch):
    ctx = ExitStack()
    with ctx:
        def sb(name, shape, dt=F32):
            return ctx.enter_context(nc.sbuf_tensor(name, shape, dt))

        def sem(name):
            return ctx.enter_context(nc.semaphore(name))

        def signal(name, per, primed=0):
            return Signal(sem(name), per, primed)

        x = sb("x", [P, TT, D])
        raw = [sb(f"raw{i}", [P, 2048]) for i in range(RAW)]
        w_hi = [sb(f"w_hi{i}", [P, 2048], F32R) for i in range(SPLIT)]
        w_lo = [sb(f"w_lo{i}", [P, 2048], F32R) for i in range(SPLIT)]
        u_hi = sb("u_hi", [P, KD, S], F32R)
        u_lo = sb("u_lo", [P, KD, S], F32R)
        h_hi = sb("h_hi", [P, 16, S], F32R)
        h_lo = sb("h_lo", [P, 16, S], F32R)
        a0 = sb("a0", [P, 8 * (S + 3)])
        a1, a2, a3, a4, a5 = (sb(f"a{i}", [P, 2048]) for i in range(1, 6))
        act2 = sb("act2", [P, 2, 512])
        mul2 = sb("mul2", [P, 2, 512])
        probs = sb("probs", [P, 2, 384])
        gain_row = sb("gain_row", [P, D])
        decay = sb("decay", [P, HEADS, 384])
        cos2 = sb("cos2", [P, S])
        sin2 = sb("sin2", [P, S])
        ident = sb("ident", [P, P])
        rows = sb("rows", [NVEC, D])
        vec = sb("vec", [P, KD, NVEC])
        lv = sb("lv", [P, KD, NV])
        small = sb("small", [P, 64])
        inv_freq = sb("inv_freq", [P, 1])
        minus_half = sb("minus_half", [P, 4])
        sink = sb("sink", [P, 8])
        soft = sb("soft", [P, 5, 2 * KD])
        ps = ctx.enter_context(nc.psum_tensor("ps", [P, 8, 512], F32))

        def tiles(a):
            return a[:, 0:2048].rearrange("p (k n) -> p k n", n=S)

        xa_pad = a0[:, :].rearrange("p (k n) -> p k n", n=S + 3)
        prod_pad = a0[:, 0:8 * (S + 2)].rearrange("p (k n) -> p k n", n=S + 2)
        scaled = a3[:, :].rearrange("p (t n) -> p t n", t=TT)
        rescaled = a4[:, :].rearrange("p (t n) -> p t n", t=TT)
        lru_w = a2[:, :].rearrange("p (m c n) -> p m c n", m=2, c=KD)
        q_t, k_t = tiles(a3), tiles(a4)
        v_rows = [a0, a1]
        t_half = tiles(a5)
        pre_ss, pre_ms, pre_rs = small[:, 0:4], small[:, 4:8], small[:, 8:12]
        post_ss, post_ms, post_rs = small[:, 12:14], small[:, 14:16], small[:, 16:18]
        ret_ss, ret_ms, ret_rs = small[:, 18:20], small[:, 20:22], small[:, 22:24]

        raw_loaded = [signal(f"raw_loaded{i}", 16 * SLOTS // RAW) for i in range(RAW)]
        heads_done = signal("heads_done", 2 * SLOTS)
        split_done = signal("split_done", SLOTS, RAW)
        slot_used = signal("slot_used", SLOTS)
        x_loaded = sem("x_loaded")
        x_ready = signal("x_ready", 6, TT)
        pre_sum = signal("pre_sum", 6)
        pre_scale = signal("pre_scale", 6)
        pre_scaled = signal("pre_scaled", 6)
        u_turned = signal("u_turned", 3 * KD)
        u_head = signal("u_head", 3 * KD)
        u_ready = signal("u_ready", 3 * KD)
        post_sum = signal("post_sum", 6)
        post_scale = signal("post_scale", 6)
        gain_loaded = signal("gain_loaded", 3 * 16)
        act_ready = signal("act_ready", 2 * FFN_PAIRS, 2)
        mul_ready = signal("mul_ready", 2 * FFN_PAIRS, 2)
        h_ready = signal("h_ready", 2 * FFN_PAIRS)
        lv_ready = signal("lv_ready", 1)
        lru_w_loaded = signal("lru_w_loaded", 4 * 16)
        xa_ready = signal("xa_ready", 4)
        xc_ready = signal("xc_ready", KD)
        lru_gates = signal("lru_gates", KD)
        lru_acts = signal("lru_acts", KD)
        gated_x = signal("gated_x", KD, 2)
        roots_ready = signal("roots_ready", 1)
        q_ready = signal("q_ready", 4)
        k_ready = signal("k_ready", 4)
        gelu_ready = signal("gelu_ready", 4)
        oa_ready = signal("oa_ready", 4)
        ga_ready = signal("ga_ready", 4)
        acc_ready = signal("acc_ready", 4)
        v_ready0 = signal("v_ready0", 2)
        v_ready1 = signal("v_ready1", 2)
        g_ready = signal("g_ready", 8)
        ret_scores = signal("ret_scores", HEADS)
        ret_probs = signal("ret_probs", HEADS)
        ret_out = signal("ret_out", HEADS)
        ret_sum = signal("ret_sum", HEADS)
        ret_scale = signal("ret_scale", HEADS)
        ret_scaled = signal("ret_scaled", HEADS)
        ret_turned = signal("ret_turned", HEADS)
        ret_ready = signal("ret_ready", HEADS, 1)
        sc_ready = signal("sc_ready", 4)
        sh_ready = signal("sh_ready", 4)
        gb_ready = signal("gb_ready", 4)
        ret_added = signal("ret_added", 4)
        oc_ready = signal("oc_ready", 4)
        gc_ready = signal("gc_ready", 4)
        mix_ready = signal("mix_ready", 4)
        vec_loaded, consts_loaded = sem("vec_loaded"), sem("consts_loaded")
        pos_loaded = sem("pos_loaded")
        ident_ready, halves_ready = sem("ident_ready"), sem("halves_ready")
        vec_turned, vec_ready = sem("vec_turned"), sem("vec_ready")
        lam_ready, lam_exp, angles, sines = sem("lam_ready"), sem("lam_exp"), sem("angles"), sem("sines")
        rel_done, rel_ready, rel_stored = sem("rel_done"), sem("rel_ready"), sem("rel_stored")
        act_own, dve_own, pool_own, pool_steps = sem("act_own"), sem("dve_own"), sem("pool_own"), sem("pool_steps")
        b = {n: sem(n) for n in (
            "proj_ready", "ka_swapped", "v_turned", "v_rows_a", "v_rows_b", "bias_loaded0", "bias_loaded1",
            "scored", "logits", "row_max", "exps", "turned", "exps_t", "attended", "den_ready",
            "attn_rows", "attn_sum", "attn_scale", "relu_ready", "sq_ready", "hid_ready", "p_loaded",
            "p_turned", "p_head", "p_ready", "brow_loaded", "gate_in", "gate_ready", "gated", "ple_sum",
            "ple_scale", "out_ready", "out_stored", "sink_loaded")}

        k_major = "l (k p) n -> p (l k) n"
        w_ffn_in = [t["ffn1_w_in"].rearrange(k_major, p=P), t["ffn2_w_in"].rearrange(k_major, p=P)]
        w_ffn_out = [t["ffn1_w_out"].rearrange(k_major, p=P), t["ffn2_w_out"].rearrange(k_major, p=P)]
        w_mix_in = t["w_mix_in"].rearrange(k_major, p=P)
        w_out = {n: t[w].rearrange(k_major, p=P) for n, w in (
            ("lru_out", "w_lru_out"), ("ret_out", "w_ret_out"), ("sc_out", "w_sc_out"), ("mix_out", "w_mix_out"))}
        b_w = {n: t[n + "_2"].rearrange(k_major, p=P)
               for n in ("w_in", "w_o", "w_up", "w_down", "w_ple_gate", "w_ple_proj")}

        def turned(l, i, k):
            first = (0, 2, 1, 0)[i] if l is DEPTH else (0, 2, 2)[i]
            bank = (first + k // 2) % 4
            return ps[:, bank, S * (k % 2):S * (k % 2) + S]

        def bcast(row, n):
            return row.broadcast_to([P, n])

        def col_view(buf, n):
            return buf[n][:, :].rearrange("p (k n) -> p k n", n=SLOTC)

        def row_view(buf, n):
            return buf[n][:, :].rearrange("p (k n) -> p k n", n=D)

        block = ctx.enter_context(nc.Block())

        @block.sync
        def _(sp):
            def load(l, n, src, half=False):
                sp.wait_ge(split_done.sem, split_done.at(l, n - RAW + 1))
                size = src.shape[1] * src.shape[2]
                dst = raw[n % RAW][:, 0:size].rearrange("p (k n) -> p k n", n=src.shape[2])
                sp.dma_start(dst, src).then_inc(raw_loaded[n % RAW].sem, 16)

            def feed_forward(l, which, base):
                w_in, w_o = w_ffn_in[which], w_ffn_out[which]

                def gate_up(n, col):
                    load(l, n, w_in[:, ds(l * KD, KD), ds(col, SLOTC)])
                    load(l, n + 1, w_in[:, ds(l * KD, KD), ds(col + D_FF, SLOTC)])

                with sp.Fori(0, FIRST_PAIRS // 2) as it:
                    for j in range(4):
                        n = base + j
                        sp.wait_ge(split_done.sem, l * SLOTS + it * 4 + (RAW + n - RAW + 1))
                        col = it * (2 * SLOTC) + ((j // 2) * SLOTC + (j % 2) * D_FF)
                        sp.dma_start(col_view(raw, n % RAW), w_in[:, ds(l * KD, KD), ds(col, SLOTC)])\
                          .then_inc(raw_loaded[n % RAW].sem, 16)
                for p in range(FIRST_PAIRS):
                    load(l, base + 2 * FIRST_PAIRS + p, w_o[:, ds(l * 2 * FFN_PAIRS + 2 * p, 2), :])
                for p in range(FIRST_PAIRS, FFN_PAIRS):
                    gate_up(base + FFN_IN2 + 2 * (p - FIRST_PAIRS), p * SLOTC)
                for p in range(FIRST_PAIRS, FFN_PAIRS - 1):
                    load(l, base + FFN_OUT2 + p - FIRST_PAIRS, w_o[:, ds(l * 2 * FFN_PAIRS + 2 * p, 2), :])
                for i in range(2):
                    load(l, base + FFN_SLOTS - 2 + i, w_o[:, ds(l * 2 * FFN_PAIRS + 2 * FFN_PAIRS - 2 + i, 1), :])

            def mixer(l):
                for name, count in STAGES:
                    for j in range(count):
                        n = AT[name] + j
                        if name == "v":
                            src = w_mix_in[:, ds(l * KD + 2 * (j % 4), 2), MC["v"] + D * (j // 4):MC["v"] + D * (j // 4) + D]
                        elif name in MC:
                            src = w_mix_in[:, ds(l * KD, KD), MC[name] + SLOTC * j:MC[name] + SLOTC * (j + 1)]
                        elif name == "ret_out":
                            c = SLOTC * (j // 2)
                            src = w_out[name][:, ds(l * 2 * KD + KD * (j % 2), KD), c:c + SLOTC]
                        elif name == "mix_out":
                            src = w_out[name][:, ds(l * KD + 2 * j, 2), :]
                        else:
                            src = w_out[name][:, ds(l * KD, KD), SLOTC * j:SLOTC * (j + 1)]
                        load(l, n, src)

            sp.sem_inc(split_done.sem, RAW)
            sp.dma_start(x[:, :, :], t["x"].rearrange("b (t p) d -> p (b t) d", p=P)).then_inc(x_loaded, 16)
            with sp.Fori(0, DEPTH) as l:
                feed_forward(l, 0, 0)
                mixer(l)
                feed_forward(l, 1, FFN2)
            l = DEPTH
            for j in range(9):
                load(l, B_IN + j, b_w["w_in"][:, :, SLOTC * j:SLOTC * (j + 1)])
            for j in range(4):
                load(l, B_O + j, b_w["w_o"][:, 2 * j:2 * j + 2, :])
            for part in range(2):
                up, down = (B_UP, B_DN) if part == 0 else (B_UP2, B_DN2)
                for j in range(8):
                    c = SLOTC * (8 * part + j)
                    load(l, up + j, b_w["w_up"][:, :, c:c + SLOTC])
                for j in range(8):
                    k = 2 * (8 * part + j)
                    load(l, down + j, b_w["w_down"][:, k:k + 2, :])
            for j in range(4):
                load(l, B_GATE + j, b_w["w_ple_gate"][:, 2 * j:2 * j + 2, :])
            load(l, B_PLE, b_w["w_ple_proj"][:, 0:2, :])
            for tt in range(TT):
                sp.wait_ge(b["out_ready"], tt + 1)
                sp.dma_start(out.rearrange("b (t p) d -> p (b t) d", p=P)[:, tt, :], x[:, tt, :])\
                  .then_inc(b["out_stored"], 16)
            sp.wait_ge(b["out_stored"], 16 * TT)

        @block.gpsimd
        def _(pool):
            own = Chain(pool, pool_own)

            def until(sig, count):
                pool.wait_ge(sig.sem, count)
                pool.sem_inc(pool_steps, 1)

            def inverse_rms(ss, ms, rs, n, width, sig, l, count, last_sig, by=1.0):
                until(sig, sig.at(l, count))
                own.done(nc.gpsimd.tensor_scalar(ms, ss, 1.0 / (n * by * by), EPS / (by * by), ALU.mult, ALU.add))
                nc.gpsimd.tensor_tensor(rs, ms, minus_half[:, 0:width], ALU.pow).then_inc(last_sig.sem, 1)

            def pre(l, i):
                for tt in range(TT):
                    inverse_rms(pre_ss[:, tt:tt + 1], pre_ms[:, tt:tt + 1], pre_rs[:, tt:tt + 1], D, 1,
                                pre_sum, l, TT * i + tt + 1, pre_scale)

            def post(l, i, by):
                for tt in range(TT):
                    inverse_rms(post_ss[:, tt:tt + 1], post_ms[:, tt:tt + 1], post_rs[:, tt:tt + 1], D, 1,
                                post_sum, l, TT * i + tt + 1, post_scale, by)

            def gain(l, i, src):
                until(x_ready, x_ready.at(l, TT * i))
                pool.dma_start(gain_row[:, :], src).then_inc(gain_loaded.sem, 16)

            def gain_of(name, l):
                return bcast(t[name][ds(l, 1), :], D)

            nc.gpsimd.memset(minus_half[:, :], -0.5).then_inc(halves_ready, 1)
            pool.wait_ge(halves_ready, 1)
            own.done(nc.gpsimd.memset(ident[:, :], 0.0))
            nc.gpsimd.affine_select(out=ident[:, :], in_=ident[:, :], compare_op=ALU.not_equal, fill=1.0,
                                    base=0, pattern=[[-1, P]], channel_multiplier=1).then_inc(ident_ready, 1)
            own.restart()
            with pool.Fori(0, DEPTH) as l:
                until(ret_ready, ret_ready.at(l, 0))
                own.done(nc.gpsimd.memset(a2[:, :], 0.0))
                for m, name in enumerate(("lru_w_a", "lru_w_x")):
                    w = t[name].rearrange("l (c e) i j -> e i (l c) j", e=2)
                    for e in range(2):
                        pool.dma_start(lru_w[64 * e:64 * e + 64, m, :, 64 * e:64 * e + 64],
                                       w[e, :, ds(l * KD, KD), :]).then_inc(lru_w_loaded.sem, 16)
                gain(l, 0, gain_of("ffn1_post_g", l))
                pre(l, 0)
                post(l, 0, 0.5)
                gain(l, 1, gain_of("mix_post_g", l))
                pre(l, 1)
                for h in range(HEADS):
                    inverse_rms(ret_ss, ret_ms, ret_rs, HV, 2, ret_sum, l, h + 1, ret_scale)
                post(l, 1, 1.0)
                gain(l, 2, gain_of("ffn2_post_g", l))
                pre(l, 2)
                post(l, 2, 0.5)
                own.restart()
            l = DEPTH
            gain(l, 0, gain_of("g_post_mix_2", 0))
            pre(l, 0)
            pool.wait_ge(rel_stored, 16)
            def band(h):
                ring = a1 if h % 10 < 5 else a2
                s = (h % 5) * BIASW
                return ring[:, s:s + BIASW]
            for h in range(NHEAD):
                if h >= 10:
                    pool.wait_ge(b["logits"], h - 9)
                elif h == 0:
                    pool.wait_ge(x_ready.sem, x_ready.at(l, 0))
                src = bass.AP(tensor=scratch.tensor, offset=scratch.offset + h * 512, ap=[[1, P], [1, BIASW]])
                pool.dma_start(band(h), src).then_inc(b["bias_loaded0" if h % 2 == 0 else "bias_loaded1"], 16)
                pool.wait_ge(b["bias_loaded0" if h % 2 == 0 else "bias_loaded1"], 16 * (h // 2 + 1))
            pool.wait_ge(b["attn_sum"], 4)
            own.done(nc.gpsimd.tensor_scalar(pre_ms, pre_ss, 1.0 / 512, EPS, ALU.mult, ALU.add))
            nc.gpsimd.tensor_tensor(pre_rs, pre_ms, minus_half[:, :], ALU.pow).then_inc(b["attn_scale"], 1)
            post(l, 0, 1.0)
            gain(l, 1, gain_of("g_post_mlp_2", 0))
            pre(l, 1)
            pool.wait_ge(b["den_ready"], 2)
            pool.dma_start(a1[:, 0:2 * S].rearrange("p (t n) -> p t n", t=TT),
                           t["p_2"].rearrange("l b (t p) n -> p (l b t) n", p=P)).then_inc(b["p_loaded"], 16)
            post(l, 1, 1.0)
            gain(l, 2, gain_of("g_post_ple_2", 0))
            pool.dma_start(a2[:, 0:D], gain_of("b_ple_gate_2", 0)).then_inc(b["brow_loaded"], 16)
            for tt in range(TT):
                pool.wait_ge(b["ple_sum"], tt + 1)
                own.done(nc.gpsimd.tensor_scalar(post_ms[:, tt:tt + 1], post_ss[:, tt:tt + 1], 1.0 / D, EPS,
                                                 ALU.mult, ALU.add))
                nc.gpsimd.tensor_tensor(post_rs[:, tt:tt + 1], post_ms[:, tt:tt + 1], minus_half[:, 0:1], ALU.pow)\
                  .then_inc(b["ple_scale"], 1)

        @block.scalar
        def _(act):
            A = nc.scalar.activation
            own = Chain(act, act_own)

            def head(l, n, size=2048, it=0, first=False):
                r = n % RAW
                act.wait_ge(raw_loaded[r].sem, raw_loaded[r].at(l, 16 * (n // RAW + 1)) + it * 16)
                if not first:
                    act.wait_ge(slot_used.sem, slot_used.at(l, n - 1) + it * 4)
                for i in range(2):
                    part = slice(i * size // 2, (i + 1) * size // 2)
                    A(w_hi[n % SPLIT][:, part], raw[r][:, part], ACT.Copy).then_inc(heads_done.sem, 1)

            def pre(l, i, gains, col):
                for tt in range(TT):
                    act.wait_ge(x_ready.sem, x_ready.at(l, TT * i + tt - 1))
                    A(a5[:, 0:D], x[:, tt, :], ACT.Square, accum_out=pre_ss[:, tt:tt + 1]).then_inc(pre_sum.sem, 1)
                    act.wait_ge(pre_sum.sem, pre_sum.at(l, TT * i + tt + 1))
                u_heads(l, i, gains, col)

            def u_heads(l, i, gains, col):
                for k in range(KD):
                    act.wait_ge(u_turned.sem, u_turned.at(l, KD * i + (k | 1) + 1))
                    A(u_hi[:, k, :], turned(l, i, k), ACT.Copy, scale=gains[:, k, col:col + 1]).then_inc(u_head.sem, 1)

            def post(l, i, slot):
                act.wait_ge(slot_used.sem, slot_used.at(l, slot + 1))
                for tt in range(TT):
                    A(a5[:, 0:D], ps[:, 4 + 2 * tt:6 + 2 * tt, :].rearrange("p a n -> p (a n)"), ACT.Square,
                      accum_out=post_ss[:, tt:tt + 1]).then_inc(post_sum.sem, 1)
                    act.wait_ge(post_sum.sem, post_sum.at(l, TT * i + tt + 1))

            def silu(l, which, base, p, it=0):
                pair = FFN_PAIRS * which + p
                n = base + (2 * p if p < FIRST_PAIRS else FFN_IN2 + 2 * (p - FIRST_PAIRS))
                bank = (2 * which + 2 * p) % 4
                act.wait_ge(slot_used.sem, slot_used.at(l, n + 1) + it * 4)
                act.wait_ge(mul_ready.sem, mul_ready.at(l, pair - 1) + it * 2)
                A(act2[:, pair % 2, :], ps[:, bank, :], ACT.Silu).then_inc(act_ready.sem, 1)

            def feed_forward(l, which, base):
                with act.Fori(0, FIRST_PAIRS // 2) as it:
                    for j in range(4):
                        head(l, base + j + 2, it=it)
                        if j % 2 == 0:
                            silu(l, which, base, j // 2, it)
                for n in range(base + 2 * FIRST_PAIRS, base + FFN_SLOTS):
                    at = n - base
                    head(l, n + 2, 1024 if FFN_SLOTS - 2 <= at + 2 < FFN_SLOTS else 2048)
                    if FFN_IN2 <= at < FFN_OUT2 and (at - FFN_IN2) % 2 == 0:
                        silu(l, which, base, FIRST_PAIRS + (at - FFN_IN2) // 2)

            def from_slot(l, n):
                act.wait_ge(slot_used.sem, slot_used.at(l, n + 1))

            def mixer(l):
                for name, count in STAGES:
                    for j in range(count):
                        n = AT[name] + j
                        m = n - MIX0
                        bank = (2 + j) % 4
                        pair = slice(2 * j, 2 * j + 2)
                        pv = ps[:, bank, :].rearrange("p (a n) -> p a n", a=2)
                        c = m - 5
                        if 0 <= c < KD:
                            act.wait_ge(lru_gates.sem, lru_gates.at(l, c + 1))
                            act.wait_ge(gated_x.sem, gated_x.at(l, c - 1))
                            own.done(A(t_half[:, c, :], ps[:, 4 + c % 4, 0:S], ACT.Sigmoid,
                                       bias=lv[:, c, V_BA:V_BA + 1]))
                            A(act2[:, 0, S * (c % 2):S * (c % 2) + S], ps[:, 4 + c % 4, S:2 * S], ACT.Sigmoid,
                              bias=lv[:, c, V_BX:V_BX + 1])
                            A(t_half[:, c, :], t_half[:, c, :], ACT.Tanh, scale=lv[:, c, V_LAM:V_LAM + 1])\
                              .then_inc(lru_acts.sem, 1)
                            if c == KD - 1:
                                act.wait_ge(lru_acts.sem, lru_acts.at(l, KD))
                                A(a0[:, 0:2048], a5[:, :], ACT.Sqrt).then_inc(roots_ready.sem, 1)
                        if name == "g" and j % 2 == 1:
                            h = j // 2
                            act.wait_ge(ret_out.sem, ret_out.at(l, h + 1))
                            if h >= 1:
                                act.wait_ge(ret_scale.sem, ret_scale.at(l, h))
                            for tt in range(TT):
                                own.done(A(act2[:, 1, :], ps[:, 5 + tt, :], ACT.Square, accum_out=ret_ss[:, tt:tt + 1]))
                            act.sem_inc(ret_sum.sem, 1)
                            own.restart()
                        head(l, n + 2)
                        if name in ("xa", "ya", "ga", "g", "sc", "gb", "gc"):
                            from_slot(l, n)
                        if name == "xa":
                            A(xa_pad[:, pair, 3:3 + S], pv, ACT.Copy).then_inc(xa_ready.sem, 1)
                        elif name == "ya":
                            A(tiles(a2)[:, pair, :], pv, ACT.Gelu_apprx_tanh).then_inc(gelu_ready.sem, 1)
                        elif name == "ga":
                            act.wait_ge(oa_ready.sem, oa_ready.at(l, j + 1))
                            A(tiles(a5)[:, pair, :], pv, ACT.Sigmoid).then_inc(ga_ready.sem, 1)
                        elif name == "v" and j % 4 == 3:
                            from_slot(l, n)
                            A(v_rows[0][:, D * (j // 4):D * (j // 4) + D], ps[:, 4:6, :].rearrange("p a n -> p (a n)"),
                              ACT.Copy).then_inc(v_ready0.sem, 1)
                        elif name == "g":
                            if j >= 4:
                                act.wait_ge(ret_ready.sem, ret_ready.at(l, j // 2 - 1))
                            A(a2[:, 512 * (j % 4):512 * (j % 4) + 512], ps[:, bank, :], ACT.Silu).then_inc(g_ready.sem, 1)
                        elif name == "sc":
                            A(tiles(a1)[:, pair, :], pv, ACT.Copy).then_inc(sc_ready.sem, 1)
                        elif name == "gb":
                            A(tiles(a4)[:, pair, :], pv, ACT.Sigmoid).then_inc(gb_ready.sem, 1)
                        elif name == "gc":
                            act.wait_ge(ret_added.sem, ret_added.at(l, j + 1))
                            A(tiles(a4)[:, pair, :], pv, ACT.Sigmoid).then_inc(gc_ready.sem, 1)

            for v, name in ((V_G1, "ffn1_pre_g"), (V_GM, "mix_pre_g"), (V_CB, "lru_conv_b"), (V_BA, "lru_b_a"),
                            (V_BX, "lru_b_x"), (V_LAM, "lru_lambda"), (V_G2, "ffn2_pre_g")):
                act.dma_start(rows[v:v + NV * (DEPTH - 1) + 1:NV, :], t[name]).then_inc(vec_loaded, 16)
            for l in range(DEPTH):
                act.dma_start(rows[l * NV + V_CW:l * NV + V_CW + 4, :], t["lru_conv_w"][l]).then_inc(vec_loaded, 16)
                act.dma_start(rows[l * NV + V_SW:l * NV + V_SW + 3, :], t["sc_conv_w"][l]).then_inc(vec_loaded, 16)
            act.dma_start(rows[V2_GMIX:V2_GMIX + 1, :], t["g_pre_mix_2"]).then_inc(vec_loaded, 16)
            act.dma_start(rows[V2_GMLP:V2_GMLP + 1, :], t["g_pre_mlp_2"]).then_inc(vec_loaded, 16)
            act.dma_start(rows[V2_GOUT:V2_GOUT + 1, 0:512], t["g_out_a_2"]).then_inc(vec_loaded, 16)
            act.dma_start(rows[V2_GOUT:V2_GOUT + 1, 512:D], t["g_out_b_2"]).then_inc(vec_loaded, 16)
            act.dma_start(a0[:, 0:S].bitcast(I32), bcast(t["positions"].rearrange("(a n) -> a n", a=1), S))\
               .then_inc(pos_loaded, 16)
            act.dma_start(inv_freq[:, :], t["inv_freq"]).then_inc(pos_loaded, 16)
            act.dma_start(a2[0:32, 1536:1536 + NHEAD], t["rel_bias_table_2"]).then_inc(consts_loaded, 16)
            act.dma_start(a3[0:32, 0:REL], t["onehot"]).then_inc(consts_loaded, 16)
            act.dma_start(a2[0:NHEAD, 512:512 + REL], t["allowed"]).then_inc(consts_loaded, 16)
            act.dma_start(decay[:, :, :].rearrange("p h n -> p (h n)"), t["decay"]).then_inc(consts_loaded, 16)
            act.dma_start(sink[:, :], bcast(t["sink_a_2"], 8)).then_inc(b["sink_loaded"], 16)
            act.wait_ge(lam_ready, 1)
            A(soft[:, 1, :], soft[:, 1, :], ACT.Exp, scale=-1.0).then_inc(lam_exp, 1)
            act.wait_ge(angles, 1)
            A(sin2[:, :], sin2[:, :], ACT.Sin).then_inc(sines, 1)
            A(cos2[:, :], cos2[:, :], ACT.Sin).then_inc(sines, 1)
            act.wait_ge(rel_ready, 1)
            act.dma_start(scratch[:, 0:REL], a2[0:NHEAD, 0:REL]).then_inc(rel_stored, 16)
            head(0, 0, first=True)
            head(0, 1, first=True)
            act.wait_ge(vec_ready, 1)
            with act.Fori(0, DEPTH) as l:
                act.wait_ge(lv_ready.sem, lv_ready.at(l, 1))
                pre(l, 0, lv, V_G1)
                feed_forward(l, 0, 0)
                post(l, 0, FFN_SLOTS - 1)
                pre(l, 1, lv, V_GM)
                mixer(l)
                post(l, 1, FFN2 - 1)
                pre(l, 2, lv, V_G2)
                feed_forward(l, 1, FFN2)
                post(l, 2, SLOTS - 1)

            l = DEPTH
            pre(l, 0, vec, V2_GMIX)
            dst = {0: (a3, 0), 1: (a3, 512), 2: (a4, 0), 3: (a3, 1024), 4: (a3, 1536), 5: (a4, 512), 6: (a4, 1024),
                   7: (a5, 0), 8: (a5, 512)}
            for j in range(9):
                head(l, j + 2)
                a, o = dst[j]
                A(a[:, o:o + 512], ps[:, j % 4, :], ACT.Copy).then_inc(b["proj_ready"], 1)
            act.wait_ge(b["proj_ready"], 3)
            act.dma_start(a4[64:128, 1536:1536 + S], a4[0:64, 0:S]).then_inc(b["ka_swapped"], 16)
            act.dma_start(a4[0:64, 1536:1536 + S], a4[64:128, 0:S]).then_inc(b["ka_swapped"], 16)
            act.wait_ge(b["v_turned"], 1)
            A(v_rows[0][:, 0:512], ps[:, 4, :], ACT.Copy).then_inc(b["v_rows_a"], 1)
            A(v_rows[0][:, 640:640 + 512], ps[:, 5, :], ACT.Copy).then_inc(b["v_rows_a"], 1)
            def exps_columns(h):
                act.wait_ge(b["turned"], h + 1)
                if h >= 2:
                    act.wait_ge(b["attended"], h - 1)
                A(mul2[:, h % 2, :], ps[:, 2 + h % 2, :], ACT.Copy).then_inc(b["exps_t"], 1)
            for h in range(NHEAD):
                act.wait_ge(b["row_max"], h + 1)
                for tt in range(TT):
                    c = 4 * (h % 2) + tt
                    A(act2[:, h % 2, S * tt:S * tt + S], act2[:, h % 2, S * tt:S * tt + S], ACT.Exp,
                      bias=small[:, 24 + c:25 + c], accum_out=probs[:, 0, 2 * h + tt:2 * h + tt + 1])\
                      .then_inc(b["exps"], 1)
                if h < 8:
                    for tt in range(TT):
                        c = 4 * (h % 2) + tt
                        A(probs[:, 1, 2 * h + tt:2 * h + tt + 1], sink[:, h:h + 1], ACT.Exp,
                          bias=small[:, 24 + c:25 + c]).then_inc(b["exps"], 1)
                if h >= 1:
                    exps_columns(h - 1)
            exps_columns(NHEAD - 1)
            for tt in range(TT):
                for kind in range(2):
                    i = 2 * tt + kind
                    act.wait_ge(b["attn_rows"], i + 1)
                    own.done(A(a5[:, 0:512], a1[:, D * tt + 512 * kind:D * tt + 512 * kind + 512], ACT.Square,
                               accum_out=pre_ss[:, i:i + 1]))
                    act.sem_inc(b["attn_sum"], 1)
            u_heads(l, 1, vec, V2_GOUT)
            for j in range(B_O, B_UP):
                head(l, j + 2)
            post(l, 0, B_UP - 1)
            for tt in range(TT):
                act.wait_ge(x_ready.sem, x_ready.at(l, tt + 1))
                A(a5[:, 0:D], x[:, tt, :], ACT.Square, accum_out=pre_ss[:, tt:tt + 1]).then_inc(pre_sum.sem, 1)
                act.wait_ge(pre_sum.sem, pre_sum.at(l, TT + tt + 1))
            u_heads(l, 2, vec, V2_GMLP)
            for part in range(2):
                for j in range(16):
                    n = (B_UP if part == 0 else B_UP2) + j
                    if n + 2 < B_SLOTS:
                        head(l, n + 2)
                    if j < 8:
                        p = 8 * part + j
                        act.wait_ge(slot_used.sem, slot_used.at(l, n + 1))
                        if p >= 2:
                            act.wait_ge(b["sq_ready"], p - 1)
                        A(act2[:, p % 2, :], ps[:, (9 + p) % 4, :], ACT.Relu).then_inc(b["relu_ready"], 1)
            post(l, 1, B_GATE - 1)
            for k in range(KD):
                act.wait_ge(u_turned.sem, u_turned.at(l, KD * 3 + (k | 1) + 1))
                A(u_hi[:, k, :], turned(l, 3, k), ACT.Copy).then_inc(u_head.sem, 1)
            act.wait_ge(b["p_turned"], 1)
            A(h_hi[:, 0:2, :], ps[:, 4, :].rearrange("p (a n) -> p a n", a=2), ACT.Copy).then_inc(b["p_head"], 1)
            for n in range(B_GATE, B_SLOTS - 2):
                head(l, n + 2)
            for tt in range(TT):
                act.wait_ge(b["gate_in"], tt + 1)
                A(a3[:, D * tt:D * tt + D], a3[:, D * tt:D * tt + D], ACT.Sigmoid).then_inc(b["gate_ready"], 1)
                act.wait_ge(b["gated"], tt + 1)
                own.done(A(a5[:, 0:D], a3[:, D * tt:D * tt + D], ACT.Square, accum_out=post_ss[:, tt:tt + 1]))
                act.sem_inc(b["ple_sum"], 1)

        @block.vector
        def _(dve):
            V = nc.vector
            own = Chain(dve, dve_own)

            def rest(l, n, size=2048, it=0):
                for i in range(2):
                    part = slice(i * size // 2, (i + 1) * size // 2)
                    dve.wait_ge(heads_done.sem, heads_done.at(l, 2 * n + i + 1) + it * 8)
                    ins = V.tensor_tensor(w_lo[n % SPLIT][:, part], raw[n % RAW][:, part], w_hi[n % SPLIT][:, part],
                                          ALU.subtract)
                ins.then_inc(split_done.sem, 1)

            def pre(l, i, gains, col):
                for tt in range(TT):
                    dve.wait_ge(pre_scale.sem, pre_scale.at(l, TT * i + tt + 1))
                    V.tensor_scalar(scaled[:, tt, :], x[:, tt, :], pre_rs[:, tt:tt + 1], None, ALU.mult)\
                     .then_inc(pre_scaled.sem, 1)
                u_rests(l, i, gains, col)

            def u_rests(l, i, gains, col):
                for k in range(KD):
                    dve.wait_ge(u_head.sem, u_head.at(l, KD * i + (k | 1) + 1))
                    V.scalar_tensor_tensor(u_lo[:, k, :], turned(l, i, k), gains[:, k, col:col + 1], u_hi[:, k, :], ALU.mult, ALU.subtract)\
                     .then_inc(u_ready.sem, 1)

            def post(l, i):
                dve.wait_ge(gain_loaded.sem, gain_loaded.at(l, 16 * (i + 1)))
                for tt in range(TT):
                    dve.wait_ge(post_scale.sem, post_scale.at(l, TT * i + tt + 1))
                    own.done(V.scalar_tensor_tensor(
                        rescaled[:, tt, :], ps[:, 4 + 2 * tt:6 + 2 * tt, :].rearrange("p a n -> p (a n)"),
                        post_rs[:, tt:tt + 1], gain_row[:, :], ALU.mult, ALU.mult))
                    V.tensor_tensor(x[:, tt, :], x[:, tt, :], rescaled[:, tt, :], ALU.add).then_inc(x_ready.sem, 1)

            def split(src, hi, lo, sig):
                own.done(V.tensor_copy(hi, src))
                V.tensor_tensor(lo, src, hi, ALU.subtract).then_inc(sig, 1)

            def hidden(l, which, base, p, it=0):
                pair = FFN_PAIRS * which + p
                n = base + (2 * p if p < FIRST_PAIRS else FFN_IN2 + 2 * (p - FIRST_PAIRS)) + 1
                bank = (2 * which + 2 * p) % 4 + 1
                dve.wait_ge(slot_used.sem, slot_used.at(l, n + 1) + it * 4)
                dve.wait_ge(act_ready.sem, act_ready.at(l, pair + 1) + it * 2)
                V.tensor_tensor(mul2[:, pair % 2, :], ps[:, bank, :], act2[:, pair % 2, :], ALU.mult)\
                 .then_inc(mul_ready.sem, 1)
                dve.wait_ge(mul_ready.sem, mul_ready.at(l, pair + 1) + it * 2)
                k = ds(2 * p + it * 4, 2) if p < FIRST_PAIRS else slice(2 * (p - FIRST_PAIRS), 2 * (p - FIRST_PAIRS) + 2)
                split(mul2[:, pair % 2, :].rearrange("p (a n) -> p a n", a=2), h_hi[:, k, :], h_lo[:, k, :], h_ready.sem)

            def feed_forward(l, which, base):
                own.restart()
                with dve.Fori(0, FIRST_PAIRS // 2) as it:
                    for j in range(4):
                        rest(l, base + j + 2, it=it)
                        if j % 2 == 1:
                            hidden(l, which, base, j // 2, it)
                    own.restart()
                for n in range(base + 2 * FIRST_PAIRS, base + FFN_SLOTS):
                    at = n - base
                    rest(l, n + 2, 1024 if FFN_SLOTS - 2 <= at + 2 < FFN_SLOTS else 2048)
                    if FFN_IN2 <= at < FFN_OUT2 and (at - FFN_IN2) % 2 == 1:
                        hidden(l, which, base, FIRST_PAIRS + (at - FFN_IN2) // 2)

            def rope(l, j, bank, dst, sig):
                pv = ps[:, bank, :].rearrange("p (a n) -> p a n", a=2)
                c3 = cos2[:, :].unsqueeze(1).broadcast_to([P, 2, S])
                s3 = sin2[:, :].unsqueeze(1).broadcast_to([P, 2, S])
                V.tensor_tensor(mul2[:, 0, :].rearrange("p (a n) -> p a n", a=2), pv, c3, ALU.mult)
                own.done(V.tensor_tensor(mul2[:, 1, :].rearrange("p (a n) -> p a n", a=2), pv, s3, ALU.mult))
                V.tensor_tensor(dst[:, 2 * j, :], mul2[:, 0, 0:S], mul2[:, 1, S:2 * S], ALU.subtract)
                own.done(V.tensor_tensor(dst[:, 2 * j + 1, :], mul2[:, 0, S:2 * S], mul2[:, 1, 0:S], ALU.add))
                dve.sem_inc(sig.sem, 1)

            def recurrence(l, j):
                f = slice(512 * j, 512 * j + 512)
                own.done(V.tensor_scalar(a5[:, f], a5[:, f], 1.0, None, ALU.add))
                own.done(V.reciprocal(a5[:, f], a5[:, f]))
                own.done(V.tensor_tensor(a0[:, f], a0[:, f], a5[:, f], ALU.mult))
                own.done(V.tensor_scalar(a5[:, f], a5[:, f], 2.0, -1.0, ALU.mult, ALU.add))
                own.done(V.scalar_tensor_tensor(a1[:, f], a0[:, f], 2.0, a1[:, f], ALU.mult, ALU.mult))
                for c in (2 * j, 2 * j + 1):
                    g = slice(S * c, S * c + S)
                    own.done(V.tensor_tensor_scan(a0[:, g], a5[:, g], a1[:, g], 0.0, ALU.mult, ALU.add))
                dve.wait_ge(gelu_ready.sem, gelu_ready.at(l, j + 1))
                own.done(V.tensor_tensor(a0[:, f], a0[:, f], a2[:, f], ALU.mult))
                split(tiles(a0)[:, 2 * j:2 * j + 2, :], h_hi[:, 2 * j:2 * j + 2, :], h_lo[:, 2 * j:2 * j + 2, :], oa_ready.sem)

            def mixer(l):
                own.done(V.memset(xa_pad[:, :, 0:3], 0.0))
                for name, count in STAGES:
                    for j in range(count):
                        n = AT[name] + j
                        m = n - MIX0
                        bank = (2 + j) % 4
                        pair = slice(2 * j, 2 * j + 2)
                        pv = ps[:, bank, :].rearrange("p (a n) -> p a n", a=2)
                        c = m - 5
                        if 0 <= c < KD:
                            dve.wait_ge(lru_acts.sem, lru_acts.at(l, c + 1))
                            V.tensor_tensor(tiles(a1)[:, c, :], tiles(a1)[:, c, :], act2[:, 0, S * (c % 2):S * (c % 2) + S],
                                            ALU.mult).then_inc(gated_x.sem, 1)
                            dve.wait_ge(gated_x.sem, gated_x.at(l, c + 1))
                        if name == "g" and j % 2 == 0:
                            h = j // 2
                            dve.wait_ge(ret_scores.sem, ret_scores.at(l, h + 1))
                            if h >= 2:
                                dve.wait_ge(ret_out.sem, ret_out.at(l, h - 1))
                            V.tensor_tensor(probs[:, h % 2, :], ps[:, 4, 0:384], decay[:, h, :], ALU.mult)\
                             .then_inc(ret_probs.sem, 1)
                        if name in ("g", "sc") and (m - 34) % 2 == 0 and 0 <= (m - 34) // 2 < HEADS:
                            h = (m - 34) // 2
                            dve.wait_ge(ret_turned.sem, ret_turned.at(l, h + 1))
                            dve.wait_ge(g_ready.sem, g_ready.at(l, 2 * h + 2))
                            sg = a2[:, D * (h % 2):D * (h % 2) + D]
                            own.done(V.tensor_tensor(sg, ps[:, 6:8, :].rearrange("p a n -> p (a n)"), sg, ALU.mult))
                            split(sg.rearrange("p (k n) -> p k n", n=S), h_hi[:, 4 * h:4 * h + 4, :],
                                  h_lo[:, 4 * h:4 * h + 4, :], ret_ready.sem)
                        if name == "g" and j % 2 == 1:
                            h = j // 2
                            dve.wait_ge(ret_scale.sem, ret_scale.at(l, h + 1))
                            V.tensor_scalar(mul2[:, 0, :], ps[:, 5, :], ret_rs[:, 0:1], None, ALU.mult)
                            V.tensor_scalar(mul2[:, 1, :], ps[:, 6, :], ret_rs[:, 1:2], None, ALU.mult)\
                             .then_inc(ret_scaled.sem, 1)
                        rest(l, n + 2)
                        if name == "xa":
                            dve.wait_ge(xa_ready.sem, xa_ready.at(l, j + 1))
                            for c in (2 * j, 2 * j + 1):
                                own.done(V.tensor_scalar(tiles(a1)[:, c, :], xa_pad[:, c, 3:3 + S],
                                                         lv[:, c, V_CW + 3:V_CW + 4], lv[:, c, V_CB:V_CB + 1],
                                                         ALU.mult, ALU.add))
                                for tap in (2, 1, 0):
                                    ins = V.scalar_tensor_tensor(tiles(a1)[:, c, :], xa_pad[:, c, tap:tap + S],
                                                                 lv[:, c, V_CW + tap:V_CW + tap + 1], tiles(a1)[:, c, :],
                                                                 ALU.mult, ALU.add)
                                    if tap:
                                        own.done(ins)
                                ins.then_inc(xc_ready.sem, 1)
                        elif name == "q":
                            dve.wait_ge(slot_used.sem, slot_used.at(l, n + 1))
                            rope(l, j, bank, q_t, q_ready)
                        elif name == "k":
                            dve.wait_ge(slot_used.sem, slot_used.at(l, n + 1))
                            rope(l, j, bank, k_t, k_ready)
                        if 13 <= m < 17:
                            if m == 13:
                                dve.wait_ge(roots_ready.sem, roots_ready.at(l, 1))
                            recurrence(l, m - 13)
                        if name == "lru_out":
                            dve.wait_ge(slot_used.sem, slot_used.at(l, n + 1))
                            dve.wait_ge(ga_ready.sem, ga_ready.at(l, j + 1))
                            V.tensor_tensor(tiles(a5)[:, pair, :], pv, tiles(a5)[:, pair, :], ALU.mult)\
                             .then_inc(acc_ready.sem, 1)
                        elif name == "v" and j % 4 == 3:
                            dve.wait_ge(slot_used.sem, slot_used.at(l, n + 1))
                            V.tensor_copy(v_rows[1][:, D * (j // 4):D * (j // 4) + D],
                                          ps[:, 6:8, :].rearrange("p a n -> p (a n)")).then_inc(v_ready1.sem, 1)
                        elif name == "sh":
                            dve.wait_ge(slot_used.sem, slot_used.at(l, n + 1))
                            if j == 0:
                                own.done(V.memset(prod_pad[:, :, 0:2], 0.0))
                            dve.wait_ge(sc_ready.sem, sc_ready.at(l, j + 1))
                            V.tensor_tensor(prod_pad[:, pair, 2:2 + S], pv, tiles(a1)[:, pair, :], ALU.mult)\
                             .then_inc(sh_ready.sem, 1)
                            dve.wait_ge(sh_ready.sem, sh_ready.at(l, j + 1))
                            for c in (2 * j, 2 * j + 1):
                                own.done(V.tensor_scalar(tiles(a1)[:, c, :], prod_pad[:, c, 2:2 + S],
                                                         lv[:, c, V_SW + 2:V_SW + 3], None, ALU.mult))
                                for tap in (1, 0):
                                    own.done(V.scalar_tensor_tensor(
                                        tiles(a1)[:, c, :], prod_pad[:, c, tap:tap + S],
                                        lv[:, c, V_SW + tap:V_SW + tap + 1], tiles(a1)[:, c, :], ALU.mult, ALU.add))
                        elif name == "ret_out" and j % 2 == 1:
                            g = j // 2
                            bb = (2 + 2 * g) % 4
                            dve.wait_ge(slot_used.sem, slot_used.at(l, n + 1))
                            dve.wait_ge(gb_ready.sem, gb_ready.at(l, g + 1))
                            tmp = mul2[:, g % 2, :].rearrange("p (a n) -> p a n", a=2)
                            own.done(V.tensor_tensor(tmp, ps[:, bb:bb + 2, 0:S], tiles(a4)[:, 2 * g:2 * g + 2, :], ALU.mult))
                            V.tensor_tensor(tiles(a5)[:, 2 * g:2 * g + 2, :], tiles(a5)[:, 2 * g:2 * g + 2, :], tmp,
                                            ALU.add).then_inc(ret_added.sem, 1)
                        elif name == "sb":
                            dve.wait_ge(slot_used.sem, slot_used.at(l, n + 1))
                            own.done(V.tensor_tensor(tiles(a1)[:, pair, :], pv, tiles(a1)[:, pair, :], ALU.mult))
                            split(tiles(a1)[:, pair, :], h_hi[:, pair, :], h_lo[:, pair, :], oc_ready.sem)
                        elif name == "sc_out":
                            dve.wait_ge(slot_used.sem, slot_used.at(l, n + 1))
                            dve.wait_ge(gc_ready.sem, gc_ready.at(l, j + 1))
                            tmp = mul2[:, j % 2, :].rearrange("p (a n) -> p a n", a=2)
                            own.done(V.tensor_tensor(tmp, pv, tiles(a4)[:, pair, :], ALU.mult))
                            own.done(V.tensor_tensor(tmp, tmp, tiles(a5)[:, pair, :], ALU.add))
                            split(tmp, u_hi[:, pair, :], u_lo[:, pair, :], mix_ready.sem)

            TWO_PI = 2 * np.pi
            C1 = 6.28125
            C2 = float(np.float32(np.round((TWO_PI - C1) * 2 ** 21) / 2 ** 21))
            C3 = float(np.float32(TWO_PI - C1 - C2))
            MAGIC = 1.5 * 2 ** 23
            PI_IN = float(np.nextafter(np.float32(np.pi), np.float32(0)))
            dve.wait_ge(pos_loaded, 32)
            ang, turns = a1[:, 0:S], a1[:, S:2 * S]
            own.done(V.tensor_copy(ang, a0[:, 0:S].bitcast(I32)))
            own.done(V.tensor_scalar(ang, ang, inv_freq[:, 0:1], None, ALU.mult))
            for dst, shift in ((sin2, 0.0), (cos2, 0.25)):
                own.done(V.tensor_scalar(turns, ang, 1.0 / TWO_PI, shift, ALU.mult, ALU.add))
                own.done(V.tensor_scalar(turns, turns, MAGIC, None, ALU.add))
                own.done(V.tensor_scalar(turns, turns, MAGIC, None, ALU.subtract))
                own.done(V.scalar_tensor_tensor(dst[:, :], turns, -C1, ang, ALU.mult, ALU.add))
                own.done(V.scalar_tensor_tensor(dst[:, :], turns, -C2, dst[:, :], ALU.mult, ALU.add))
                own.done(V.scalar_tensor_tensor(dst[:, :], turns, -C3, dst[:, :], ALU.mult, ALU.add))
                if shift:
                    own.done(V.tensor_scalar(dst[:, :], dst[:, :], float(np.pi / 2), None, ALU.add))
                own.done(V.tensor_scalar(dst[:, :], dst[:, :], PI_IN, -PI_IN, ALU.min, ALU.max))
            dve.sem_inc(angles, 1)
            dve.wait_ge(vec_turned, 1)
            own.done(V.tensor_copy(vec[:, :, :].rearrange("p k v -> p (k v)"), ps[:, 0, 0:KD * NVEC]))
            lam = vec[:, :, V_LAM:V_LAM + NV + 1:NV]
            lam3, z, w, w2, s = (soft[:, i, :].rearrange("p (k l) -> p k l", l=DEPTH) for i in range(5))
            own.done(V.tensor_scalar(lam3, lam, -1.0, None, ALU.mult))
            own.done(V.tensor_tensor(z, lam, lam3, ALU.max))
            dve.sem_inc(lam_ready, 1)
            dve.wait_ge(lam_exp, 1)
            own.done(V.tensor_scalar(w, z, 2.0, None, ALU.add))
            own.done(V.reciprocal(w, w))
            own.done(V.tensor_tensor(w, w, z, ALU.mult))
            own.done(V.tensor_tensor(w2, w, w, ALU.mult))
            own.done(V.tensor_scalar(s, w2, 1.0 / 17, None, ALU.mult))
            for odd in (15, 13, 11, 9, 7, 5, 3):
                own.done(V.scalar_tensor_tensor(s, s, 1.0 / odd, w2, ALU.add, ALU.mult))
            own.done(V.scalar_tensor_tensor(s, s, 1.0, w, ALU.add, ALU.mult))
            own.done(V.tensor_scalar(lam3, lam3, 0.0, 4.0, ALU.max, ALU.mult))
            own.done(V.scalar_tensor_tensor(lam, s, 8.0, lam3, ALU.mult, ALU.add))
            dve.sem_inc(vec_ready, 1)
            dve.wait_ge(rel_done, 1)
            own.done(V.tensor_tensor(a2[0:NHEAD, 0:REL], ps[0:NHEAD, 1, 0:REL], a2[0:NHEAD, 512:512 + REL], ALU.add))
            dve.sem_inc(rel_ready, 1)
            dve.wait_ge(rel_stored, 16)
            dve.sem_inc(ret_ready.sem, ret_ready.primed)
            dve.sem_inc(mul_ready.sem, mul_ready.primed)
            dve.sem_inc(act_ready.sem, act_ready.primed)
            dve.sem_inc(gated_x.sem, gated_x.primed)
            rest(0, 0)
            rest(0, 1)
            dve.wait_ge(x_loaded, 16)
            dve.sem_inc(x_ready.sem, x_ready.primed)
            dve.wait_ge(sines, 2)
            own.restart()
            with dve.Fori(0, DEPTH) as l:
                V.tensor_copy(lv[:, :, :], vec[:, :, ds(l * NV, NV)]).then_inc(lv_ready.sem, 1)
                dve.wait_ge(lv_ready.sem, lv_ready.at(l, 1))
                pre(l, 0, lv, V_G1)
                feed_forward(l, 0, 0)
                post(l, 0)
                pre(l, 1, lv, V_GM)
                mixer(l)
                post(l, 1)
                pre(l, 2, lv, V_G2)
                feed_forward(l, 1, FFN2)
                post(l, 2)
                own.restart()

            l = DEPTH
            pre(l, 0, vec, V2_GMIX)
            for j in range(9):
                rest(l, j + 2)
            dve.wait_ge(b["v_turned"], 1)
            V.tensor_copy(a0[:, 512:640], ps[:, 6, 0:128]).then_inc(b["v_rows_b"], 1)
            V.tensor_copy(a0[:, 1152:1280], ps[:, 6, 128:256]).then_inc(b["v_rows_b"], 1)
            dve.wait_ge(b["sink_loaded"], 16)
            for h in range(NHEAD):
                band = (a1 if h % 10 < 5 else a2)
                s0 = (h % 5) * BIASW
                dve.wait_ge(b["scored"], h + 1)
                dve.wait_ge(b["bias_loaded0" if h % 2 == 0 else "bias_loaded1"], 16 * (h // 2 + 1))
                if h >= 2:
                    dve.wait_ge(b["turned"], h - 1)
                for tt in range(TT):
                    o = s0 + P * tt + S - 1
                    bias = band[:, o:o - S if o >= S else None:-1]
                    ins = V.scalar_tensor_tensor(act2[:, h % 2, S * tt:S * tt + S], ps[:, h % 2, S * tt:S * tt + S], 0.125,
                                                 bias, ALU.mult, ALU.add)
                ins.then_inc(b["logits"], 1)
                dve.wait_ge(b["logits"], h + 1)
                c = 4 * (h % 2)
                own.done(V.tensor_reduce(small[:, 24 + c:26 + c], act2[:, h % 2, :].rearrange("p (t n) -> p t n", t=2),
                                         AX_X, ALU.max))
                if h < 8:
                    own.done(V.tensor_scalar(small[:, 24 + c:26 + c], small[:, 24 + c:26 + c], sink[:, h:h + 1], -1.0,
                                             ALU.max, ALU.mult))
                else:
                    own.done(V.tensor_scalar(small[:, 24 + c:26 + c], small[:, 24 + c:26 + c], -1.0, None, ALU.mult))
                dve.sem_inc(b["row_max"], 1)
            dve.wait_ge(b["exps"], 2 * NHEAD + 16)
            own.done(V.tensor_tensor(probs[:, 0, 0:16], probs[:, 0, 0:16], probs[:, 1, 0:16], ALU.add))
            own.done(V.reciprocal(probs[:, 0, 0:32], probs[:, 0, 0:32]))
            dve.wait_ge(b["attended"], NHEAD)
            for tt in range(TT):
                for kind in range(2):
                    r = probs[:, 0, 16 * kind + tt:16 * kind + tt + 15:2].unsqueeze(2).broadcast_to([P, 8, 64])
                    o = a1[:, D * tt + 512 * kind:D * tt + 512 * kind + 512]
                    V.tensor_tensor(o.rearrange("p (h e) -> p h e", e=64),
                                    ps[:, 4 + 2 * tt + kind, :].rearrange("p (h e) -> p h e", e=64), r, ALU.mult)\
                     .then_inc(b["attn_rows"], 1)
            dve.wait_ge(b["attn_scale"], 1)
            for tt in range(TT):
                for kind in range(2):
                    ins = V.tensor_scalar(scaled[:, tt, 512 * kind:512 * kind + 512],
                                          a1[:, D * tt + 512 * kind:D * tt + 512 * kind + 512],
                                          pre_rs[:, 2 * tt + kind:2 * tt + kind + 1], None, ALU.mult)
                ins.then_inc(b["den_ready"], 1)
            u_rests(l, 1, vec, V2_GOUT)
            for j in range(B_O, B_UP):
                rest(l, j + 2)
            post(l, 0)
            for tt in range(TT):
                dve.wait_ge(pre_scale.sem, pre_scale.at(l, TT + tt + 1))
                V.tensor_scalar(scaled[:, tt, :], x[:, tt, :], pre_rs[:, tt:tt + 1], None, ALU.mult)\
                 .then_inc(pre_scaled.sem, 1)
            u_rests(l, 2, vec, V2_GMLP)
            for part in range(2):
                for j in range(16):
                    n = (B_UP if part == 0 else B_UP2) + j
                    if n + 2 < B_SLOTS:
                        rest(l, n + 2)
                    if j < 8:
                        p = 8 * part + j
                        dve.wait_ge(b["relu_ready"], p + 1)
                        V.tensor_tensor(mul2[:, p % 2, :], act2[:, p % 2, :], act2[:, p % 2, :], ALU.mult)\
                         .then_inc(b["sq_ready"], 1)
                        dve.wait_ge(b["sq_ready"], p + 1)
                        split(mul2[:, p % 2, :].rearrange("p (a n) -> p a n", a=2), h_hi[:, 2 * j:2 * j + 2, :],
                              h_lo[:, 2 * j:2 * j + 2, :], b["hid_ready"])
            post(l, 1)
            for k in range(KD):
                dve.wait_ge(u_head.sem, u_head.at(l, KD * 3 + (k | 1) + 1))
                V.tensor_tensor(u_lo[:, k, :], turned(l, 3, k), u_hi[:, k, :], ALU.subtract)\
                 .then_inc(u_ready.sem, 1)
            dve.wait_ge(b["p_head"], 1)
            V.tensor_tensor(h_lo[:, 0:2, :], ps[:, 4, :].rearrange("p (a n) -> p a n", a=2), h_hi[:, 0:2, :],
                            ALU.subtract).then_inc(b["p_ready"], 1)
            for n in range(B_GATE, B_SLOTS - 2):
                rest(l, n + 2)
            dve.wait_ge(slot_used.sem, slot_used.at(l, B_GATE + 4))
            dve.wait_ge(b["brow_loaded"], 16)
            for tt in range(TT):
                V.tensor_tensor(a3[:, D * tt:D * tt + D], ps[:, 4 + 2 * tt:6 + 2 * tt, :].rearrange("p a n -> p (a n)"),
                                a2[:, 0:D], ALU.add).then_inc(b["gate_in"], 1)
            dve.wait_ge(slot_used.sem, slot_used.at(l, B_SLOTS))
            for tt in range(TT):
                dve.wait_ge(b["gate_ready"], tt + 1)
                V.tensor_tensor(a3[:, D * tt:D * tt + D], ps[:, 2 * tt:2 * tt + 2, :].rearrange("p a n -> p (a n)"),
                                a3[:, D * tt:D * tt + D], ALU.mult).then_inc(b["gated"], 1)
            dve.wait_ge(gain_loaded.sem, gain_loaded.at(l, 48))
            for tt in range(TT):
                dve.wait_ge(b["ple_scale"], tt + 1)
                own.done(V.scalar_tensor_tensor(a4[:, D * tt:D * tt + D], a3[:, D * tt:D * tt + D], post_rs[:, tt:tt + 1],
                                                gain_row[:, :], ALU.mult, ALU.mult))
                V.tensor_tensor(x[:, tt, :], x[:, tt, :], a4[:, D * tt:D * tt + D], ALU.add).then_inc(b["out_ready"], 1)

        @block.tensor
        def _(pe):
            M = nc.tensor.matmul

            def column_slot(l, n, dst, act_hi, act_lo, k0=0, first=True, last=True, it=0, u_from=None):
                pe.wait_ge(split_done.sem, split_done.at(l, n + 1) + it * 4)
                hi, lo = col_view(w_hi, n % SPLIT), col_view(w_lo, n % SPLIT)
                for a in range(2):
                    for k in range(KD):
                        if a == 0 and u_from is not None:
                            pe.wait_ge(u_ready.sem, u_ready.at(l, u_from + max(k, 1) + 1))
                        c = slice(P * a, P * a + P)
                        M(dst[a], hi[:, k, c], act_hi[:, k0 + k, :], start=first and k == 0, stop=False)
                        M(dst[a], hi[:, k, c], act_lo[:, k0 + k, :], start=False, stop=False)
                        ins = M(dst[a], lo[:, k, c], act_hi[:, k0 + k, :], start=False, stop=last and k == KD - 1)
                ins.then_inc(slot_used.sem, 1)

            def row_slot(l, n, ks, act_hi, act_lo, first, last, bank0=4):
                pe.wait_ge(split_done.sem, split_done.at(l, n + 1))
                hi, lo = row_view(w_hi, n % SPLIT), row_view(w_lo, n % SPLIT)
                for i, k in enumerate(ks):
                    for tt in range(TT):
                        tok = slice(P * tt, P * tt + P)
                        f, e = first and i == 0, last and i == len(ks) - 1
                        for a, (stat, mov) in enumerate(((act_hi, hi), (act_hi, lo), (act_lo, hi))):
                            for half in range(2):
                                ins = M(ps[:, bank0 + 2 * tt + half, :], stat[:, k, tok],
                                        mov[:, i, 512 * half:512 * half + 512], start=f and a == 0, stop=e and a == 2)
                ins.then_inc(slot_used.sem, 1)

            def bank(i):
                return [ps[:, i, 0:S], ps[:, i, S:2 * S]]

            def turn(l, i, src, sig, count):
                for tt in range(TT):
                    if sig is not None:
                        pe.wait_ge(sig, count(tt))
                    for k in range(KD):
                        ins = nc.tensor.transpose(turned(l, i, k)[:, P * tt:P * tt + P], src[:, tt, P * k:P * k + P], ident[:, :])
                        if tt == TT - 1:
                            ins.then_inc(u_turned.sem, 1)

            def pre(l, i):
                turn(l, i, scaled, pre_scaled.sem, lambda tt: pre_scaled.at(l, TT * i + tt + 1))

            def pair_slots(l, which, base, p, it=0):
                pair = FFN_PAIRS * which + p
                n = base + (2 * p if p < FIRST_PAIRS else FFN_IN2 + 2 * (p - FIRST_PAIRS))
                bk = (2 * which + 2 * p) % 4
                norm = 2 * which
                pe.wait_ge(act_ready.sem, act_ready.at(l, pair - 1) + it * 2)
                column_slot(l, n, bank(bk), u_hi, u_lo, it=it, u_from=KD * norm if p == 0 else None)
                pe.wait_ge(mul_ready.sem, mul_ready.at(l, pair - 1) + it * 2)
                column_slot(l, n + 1, bank(bk + 1), u_hi, u_lo, it=it)

            def feed_forward(l, which, base):
                with pe.Fori(0, FIRST_PAIRS // 2) as it:
                    for p in range(2):
                        pair_slots(l, which, base, p, it)
                for p in range(FIRST_PAIRS):
                    pe.wait_ge(h_ready.sem, h_ready.at(l, FFN_PAIRS * which + p + 1))
                    row_slot(l, base + 2 * FIRST_PAIRS + p, (2 * p, 2 * p + 1), h_hi, h_lo, p == 0, False)
                for p in range(FIRST_PAIRS, FFN_PAIRS):
                    pair_slots(l, which, base, p)
                for p in range(FIRST_PAIRS, FFN_PAIRS):
                    k = 2 * (p - FIRST_PAIRS)
                    pe.wait_ge(h_ready.sem, h_ready.at(l, FFN_PAIRS * which + p + 1))
                    n = base + FFN_OUT2 + p - FIRST_PAIRS
                    if p < FFN_PAIRS - 1:
                        row_slot(l, n, (k, k + 1), h_hi, h_lo, False, False)
                    else:
                        row_slot(l, n, (k,), h_hi, h_lo, False, False)
                        row_slot(l, n + 1, (k + 1,), h_hi, h_lo, False, True)

            def lru_gate(l, c):
                pe.wait_ge(xc_ready.sem, xc_ready.at(l, c + 1))
                pe.wait_ge(lru_w_loaded.sem, lru_w_loaded.at(l, 64))
                if c >= 4:
                    pe.wait_ge(lru_acts.sem, lru_acts.at(l, c - 3))
                for m in range(2):
                    ins = M(ps[:, 4 + c % 4, S * m:S * m + S], lru_w[:, m, c, :], tiles(a1)[:, c, :], start=True, stop=True)
                ins.then_inc(lru_gates.sem, 1)

            def scores(l, h):
                if h == 0:
                    pe.wait_ge(v_ready0.sem, v_ready0.at(l, 2))
                    pe.wait_ge(v_ready1.sem, v_ready1.at(l, 2))
                    pe.wait_ge(q_ready.sem, q_ready.at(l, 4))
                    pe.wait_ge(k_ready.sem, k_ready.at(l, 4))
                else:
                    pe.wait_ge(ret_probs.sem, ret_probs.at(l, h))
                for c in range(2):
                    M(ps[:, 4, 0:S], k_t[:, 2 * h + c, 0:P], q_t[:, 2 * h + c, :], start=c == 0, stop=c == 1)
                for c in range(2):
                    ins = M(ps[:, 4, S:S + P], k_t[:, 2 * h + c, P:S], q_t[:, 2 * h + c, P:S], start=c == 0, stop=c == 1)
                ins.then_inc(ret_scores.sem, 1)

            def attend(l, h):
                pe.wait_ge(ret_probs.sem, ret_probs.at(l, h + 1))
                if h >= 1:
                    pe.wait_ge(ret_ready.sem, ret_ready.at(l, h))
                pr, vs = probs[:, h % 2, :], slice(HV * h, HV * h + HV)
                M(ps[:, 5, :], pr[:, 0:P], v_rows[0][:, vs], start=True, stop=True)
                M(ps[:, 6, :], pr[:, P:S], v_rows[0][:, vs], start=True, stop=False)
                M(ps[:, 6, :], pr[:, S:S + P], v_rows[1][:, vs], start=False, stop=True).then_inc(ret_out.sem, 1)

            def turn_head(l, h):
                pe.wait_ge(ret_scaled.sem, ret_scaled.at(l, h + 1))
                for e in range(4):
                    for tt in range(TT):
                        o = S * (e % 2) + P * tt
                        ins = nc.tensor.transpose(ps[:, 6 + e // 2, o:o + P], mul2[:, tt, P * e:P * e + P], ident[:, :])
                ins.then_inc(ret_turned.sem, 1)

            EMPTIED = {"xa": xa_ready, "q": q_ready, "k": k_ready, "ya": gelu_ready, "ga": ga_ready, "lru_out": acc_ready,
                       "g": g_ready, "sc": sc_ready, "sh": sh_ready, "gb": gb_ready, "ret_out": ret_added,
                       "sb": oc_ready, "gc": gc_ready}
            BEFORE = {"q": "xa", "k": "q", "ya": "k", "ga": "ya", "lru_out": "ga", "g": "lru_out", "sc": "g",
                      "sh": "sc", "gb": "sh", "ret_out": "gb", "sb": "ret_out", "gc": "sb", "sc_out": "gc"}

            def mixer(l):
                for name, count in STAGES:
                    for j in range(count):
                        n = AT[name] + j
                        m = n - MIX0
                        if 0 <= m - 5 < KD:
                            lru_gate(l, m - 5)
                        if name == "g":
                            (scores if j % 2 == 0 else attend)(l, j // 2)
                        if name == "v":
                            if j == 0:
                                pe.wait_ge(lru_acts.sem, lru_acts.at(l, KD))
                            if j == 4:
                                pe.wait_ge(v_ready0.sem, v_ready0.at(l, 1))
                                pe.wait_ge(v_ready1.sem, v_ready1.at(l, 1))
                            row_slot(l, n, (2 * (j % 4), 2 * (j % 4) + 1), u_hi, u_lo, j % 4 == 0, j % 4 == 3)
                            continue
                        if name == "mix_out":
                            pe.wait_ge(mix_ready.sem, mix_ready.at(l, j + 1))
                            if j == 0:
                                pe.wait_ge(ret_ready.sem, ret_ready.at(l, HEADS))
                            row_slot(l, n, (2 * j, 2 * j + 1), u_hi, u_lo, j == 0, j == 3)
                            continue
                        if name == "ret_out":
                            g = j // 2
                            if j % 2 == 0:
                                if g < 2:
                                    pe.wait_ge(gb_ready.sem, gb_ready.at(l, 2 * g + 2))
                                else:
                                    pe.wait_ge(ret_added.sem, ret_added.at(l, g - 1))
                            if j == 0:
                                pe.wait_ge(ret_ready.sem, ret_ready.at(l, HEADS))
                            bb = (2 + 2 * g) % 4
                            column_slot(l, n, [ps[:, bb, 0:S], ps[:, bb + 1, 0:S]], h_hi, h_lo, KD * (j % 2),
                                        j % 2 == 0, j % 2 == 1)
                            continue
                        if name == "sb":
                            pe.wait_ge(ret_added.sem, ret_added.at(l, 3 + j // 2))
                        elif name == "g" and j >= 4:
                            pe.wait_ge(g_ready.sem, g_ready.at(l, j - 3))
                        elif name == "sc":
                            pe.wait_ge(g_ready.sem, g_ready.at(l, j + 5))
                        elif name != "xa":
                            before = EMPTIED[BEFORE[name]]
                            pe.wait_ge(before.sem, before.at(l, j + 1))
                        ah, al = u_hi, u_lo
                        if name == "lru_out":
                            ah, al = h_hi, h_lo
                            pe.wait_ge(oa_ready.sem, oa_ready.at(l, 4))
                        if name == "sc_out":
                            ah, al = h_hi, h_lo
                            pe.wait_ge(oc_ready.sem, oc_ready.at(l, 4))
                        column_slot(l, n, bank((2 + j) % 4), ah, al, u_from=KD if name == "xa" and j == 0 else None)
                        if name == "g" and j % 2 == 1:
                            turn_head(l, j // 2)

            pe.wait_ge(ident_ready, 1)
            pe.wait_ge(vec_loaded, 16 * (7 + 2 * DEPTH + 4))
            for k in range(KD):
                ins = nc.tensor.transpose(ps[:, 0, NVEC * k:NVEC * k + NVEC], rows[:, P * k:P * k + P],
                                          ident[0:NVEC, 0:NVEC])
            ins.then_inc(vec_turned, 1)
            pe.wait_ge(consts_loaded, 64)
            M(ps[0:NHEAD, 1, 0:REL], a2[0:32, 1536:1536 + NHEAD], a3[0:32, 0:REL], start=True, stop=True).then_inc(rel_done, 1)
            pe.wait_ge(vec_ready, 1)
            pe.wait_ge(rel_ready, 1)
            with pe.Fori(0, DEPTH) as l:
                pre(l, 0)
                feed_forward(l, 0, 0)
                pre(l, 1)
                mixer(l)
                pre(l, 2)
                feed_forward(l, 1, FFN2)

            l = DEPTH
            pre(l, 0)
            for j in range(9):
                if j >= 4:
                    pe.wait_ge(b["proj_ready"], j - 3)
                column_slot(l, j, bank(j % 4), u_hi, u_lo, u_from=0 if j == 0 else None)
            pe.wait_ge(b["proj_ready"], 9)
            for tt in range(TT):
                for c in range(4):
                    nc.tensor.transpose(ps[:, 4 + tt, P * c:P * c + P], a5[:, S * c + P * tt:S * c + P * tt + P], ident[:, :])
            for tt in range(TT):
                ins = nc.tensor.transpose(ps[:, 6, P * tt:P * tt + P], a4[:, S + P * tt:S + P * tt + P], ident[:, :])
            ins.then_inc(b["v_turned"], 1)
            pe.wait_ge(b["ka_swapped"], 32)
            pe.wait_ge(b["v_rows_a"], 2)
            pe.wait_ge(b["v_rows_b"], 2)

            def logits(h):
                part = slice(64 * (h % 2), 64 * (h % 2) + 64)
                if h < 8:
                    q_off = S * (h // 2)
                    k_off = 0 if h // 4 == h % 2 else 1536
                else:
                    q_off = 1024 + S * ((h - 8) // 2)
                    k_off = 512 + S * ((h - 8) // 2)
                if h >= 2:
                    pe.wait_ge(b["logits"], h - 1)
                for tt in range(TT):
                    ins = M(ps[:, h % 2, S * tt:S * tt + S], a3[part, q_off + P * tt:q_off + P * tt + P],
                            a4[part, k_off:k_off + S], start=True, stop=True)
                ins.then_inc(b["scored"], 1)

            def turn_exps(h):
                pe.wait_ge(b["exps"], 4 * (h + 1) if h < 8 else 32 + 2 * (h - 7))
                if h >= 2:
                    pe.wait_ge(b["exps_t"], h - 1)
                for kt in range(2):
                    for tt in range(TT):
                        ins = nc.tensor.transpose(ps[:, 2 + h % 2, S * kt + P * tt:S * kt + P * tt + P],
                                                  act2[:, h % 2, S * tt + P * kt:S * tt + P * kt + P], ident[:, :])
                ins.then_inc(b["turned"], 1)

            def weigh(h):
                pe.wait_ge(b["exps_t"], h + 1)
                kind = h // 8
                v_off = 512 + 64 * (h // 4) if kind == 0 else 64 * (h - 8)
                for tt in range(TT):
                    for kt in range(2):
                        ins = M(ps[:, 4 + 2 * tt + kind, 64 * (h % 8):64 * (h % 8) + 64],
                                mul2[:, h % 2, S * kt + P * tt:S * kt + P * tt + P],
                                a0[:, 640 * kt + v_off:640 * kt + v_off + 64], start=kt == 0, stop=kt == 1)
                ins.then_inc(b["attended"], 1)

            for h in range(NHEAD + 2):
                if h < NHEAD:
                    logits(h)
                if 1 <= h <= NHEAD:
                    turn_exps(h - 1)
                if h >= 2:
                    weigh(h - 2)
            turn(l, 1, scaled, b["den_ready"], lambda tt: tt + 1)
            for j in range(4):
                for k in (2 * j, 2 * j + 1):
                    pe.wait_ge(u_ready.sem, u_ready.at(l, KD + k + 1))
                row_slot(l, B_O + j, (2 * j, 2 * j + 1), u_hi, u_lo, j == 0, j == 3)
            turn(l, 2, scaled, pre_scaled.sem, lambda tt: pre_scaled.at(l, TT + tt + 1))
            for part in range(2):
                for j in range(8):
                    p = 8 * part + j
                    if p >= 4:
                        pe.wait_ge(b["relu_ready"], p - 3)
                    column_slot(l, (B_UP if part == 0 else B_UP2) + j, bank((9 + p) % 4), u_hi, u_lo,
                                u_from=2 * KD if p == 0 else None)
                for j in range(8):
                    pe.wait_ge(b["hid_ready"], 8 * part + j + 1)
                    row_slot(l, (B_DN if part == 0 else B_DN2) + j, (2 * j, 2 * j + 1), h_hi, h_lo,
                             part == 0 and j == 0, part == 1 and j == 7)
            turn(l, 3, x, x_ready.sem, lambda tt: x_ready.at(l, TT + tt + 1))
            pe.wait_ge(b["p_loaded"], 16)
            for c in range(2):
                for tt in range(TT):
                    ins = nc.tensor.transpose(ps[:, 4, S * c + P * tt:S * c + P * tt + P],
                                              a1[:, S * tt + P * c:S * tt + P * c + P], ident[:, :])
            ins.then_inc(b["p_turned"], 1)
            pe.wait_ge(b["p_ready"], 1)
            for j in range(4):
                for k in (2 * j, 2 * j + 1):
                    pe.wait_ge(u_ready.sem, u_ready.at(l, 3 * KD + k + 1))
                row_slot(l, B_GATE + j, (2 * j, 2 * j + 1), u_hi, u_lo, j == 0, j == 3)
            row_slot(l, B_PLE, (0, 1), h_hi, h_lo, True, True, bank0=0)


_INS = ["x", "positions", "ffn1_pre_g", "ffn1_w_in", "ffn1_w_out", "ffn1_post_g", "mix_pre_g", "w_mix_in",
        "lru_conv_w", "lru_conv_b", "lru_w_a", "lru_b_a", "lru_w_x", "lru_b_x", "lru_lambda", "w_lru_out",
        "w_ret_out", "sc_conv_w", "w_sc_out", "w_mix_out", "mix_post_g", "ffn2_pre_g", "ffn2_w_in", "ffn2_w_out",
        "ffn2_post_g", "p_2", "rel_bias_table_2", "g_pre_mix_2", "w_in_2", "sink_a_2", "g_out_a_2", "g_out_b_2",
        "w_o_2", "g_post_mix_2", "g_pre_mlp_2", "w_up_2", "w_down_2", "g_post_mlp_2", "w_ple_proj_2",
        "w_ple_gate_2", "b_ple_gate_2", "g_post_ple_2"]


def kernel(**inputs):
    import concourse.bacc as _bacc
    from concourse.bass_utils import run_bass_kernel_spmd as _run

    nc = _bacc.Bacc("TRN2", target_bir_lowering=False, num_devices=1)
    arrays, args = {}, {}

    def declare(name, a):
        arrays[f"in_{name}_dram"] = a
        args[name] = nc.dram_tensor(f"in_{name}_dram", a.shape, mybir.dt.from_np(a.dtype), kind="ExternalInput").ap()

    for name in _INS:
        declare(name, np.ascontiguousarray(inputs[name]))
    for name, a in constants().items():
        declare(name, a)
    out = nc.dram_tensor("out_0_dram", (1, S, D), F32, kind="ExternalOutput").ap()
    scratch = nc.dram_tensor("rel_scratch_dram", (NHEAD, 512), F32).ap()
    build(nc, args, out, scratch)
    r = _run(nc, [arrays], core_ids=[0])
    return r.results[0]["out_0_dram"]
```

```python
from contextlib import ExitStack

import numpy as np
import concourse.bass as bass
from concourse import mybir

F32 = mybir.dt.float32
F32R = mybir.dt.float32r
I32 = mybir.dt.int32
ALU = mybir.AluOpType
ACT = mybir.ActivationFunctionType
AX_X = mybir.AxisListType.X
ds = bass.ds

P = 128
S = 256
D = 1024
DEPTH = 2
EPS = 1e-6
CHUNK = 64
HEADS = 4
HV = 512
D_FF = 2816
TT = S // P
KD = D // P
SLOTC = 256

FFN_PAIRS = D_FF // SLOTC
FIRST_PAIRS = 8
LAST_PAIRS = FFN_PAIRS - FIRST_PAIRS
FFN_IN2 = 3 * FIRST_PAIRS
FFN_OUT2 = FFN_IN2 + 2 * LAST_PAIRS
FFN_SLOTS = FFN_OUT2 + LAST_PAIRS + 1
MIX0 = FFN_SLOTS
STAGES = [("xa", 4), ("q", 4), ("k", 4), ("ya", 4), ("v0", 4), ("ga", 4), ("v1", 4), ("lru_out", 4), ("g", 8),
          ("sc", 4), ("sh", 4), ("gb", 4), ("ret_out", 8), ("sb", 4), ("gc", 4), ("sc_out", 4),
          ("mix_out", 4)]
V_HALF = {"v0": 0, "v1": 1}
AT = {}
for _name, _n in STAGES:
    AT[_name] = MIX0 + sum(n for m, n in STAGES[:len(AT)])
FFN2 = MIX0 + sum(n for _, n in STAGES)
SLOTS = FFN2 + FFN_SLOTS
RAW, SPLIT = 4, 2
assert SLOTS % RAW == 0 and SLOTS % SPLIT == 0 and SPLIT == 2

MC = {"xa": 0, "ya": 1024, "q": 2048, "k": 3072, "v": 4096, "g": 6144, "sb": 8192, "sc": 9216,
      "sh": 10240, "ga": 11264, "gb": 12288, "gc": 13312}

V_G1, V_GM, V_CW, V_CB, V_BA, V_BX, V_LAM, V_SW, V_G2, NV = 0, 1, 2, 6, 7, 8, 9, 10, 13, 14
V2_GMIX, V2_GOUT, V2_GMLP = DEPTH * NV, DEPTH * NV + 1, DEPTH * NV + 2
NVEC = DEPTH * NV + 3

B_IN, B_O, B_UP, B_DN, B_UP2, B_DN2, B_GATE, B_PLE, B_SLOTS = 0, 9, 13, 21, 29, 37, 45, 49, 50
NHEAD = 16
BIASW = 384
REL = 2 * S - 1


class Signal:

    def __init__(self, sem, per, primed=0):
        self.sem, self.per, self.primed = sem, per, primed

    def at(self, l, k):
        return l * self.per + (self.primed + k)


class Chain:

    def __init__(self, eng, sem):
        self.eng, self.sem, self.n = eng, sem, 0

    def done(self, ins):
        ins.then_inc(self.sem, 1)
        self.n += 1
        self.eng.wait_ge(self.sem, self.n)

    def restart(self):
        if self.n:
            self.eng.sem_clear(self.sem)
            self.n = 0


def constants():
    half = 128
    inv_freq = (10000.0 ** (-np.arange(half, dtype=np.float64) / half)).astype(np.float32)[:, None]
    log_g = np.log1p(-(2.0 ** (-5.0 - np.arange(HEADS))))
    i, j = np.arange(S)[None, :], np.arange(S)[:, None]
    seen = (j // CHUNK) <= (i // CHUNK)
    full = np.exp(log_g[:, None, None] * np.abs(i - j)) * seen / 16.0
    decay = np.concatenate([full[:, :P, :], full[:, P:, P:]], axis=2).transpose(1, 0, 2)
    d = np.arange(S - 1, -S, -1)
    n = np.abs(d)
    large = 8 + (np.log(np.maximum(n, 1).astype(np.float32) / np.float32(8)) / np.float32(np.log(1024 / 8))
                 * np.float32(8)).astype(np.int32)
    bucket = np.where(d > 0, 16, 0) + np.where(n < 8, n, np.minimum(large, 15))
    onehot = (np.arange(32)[:, None] == bucket[None, :]).astype(np.float32)
    times = (n <= 64).astype(int) + (d % 4 == 0) * (n <= 256) + (d % 16 == 0)
    seen_b = np.where(times > 0, np.log(np.maximum(times, 1)), -1e30)
    seen_a = np.where(n <= 128, 0.0, -1e30)
    allowed = np.concatenate([np.tile(seen_a, (8, 1)), np.tile(seen_b, (8, 1))]).astype(np.float32)
    return {"inv_freq": inv_freq, "decay": np.ascontiguousarray(decay.reshape(P, -1)).astype(np.float32),
            "onehot": onehot, "allowed": allowed}


def build(nc, t, out, scratch):
    ctx = ExitStack()
    with ctx:
        def sb(name, shape, dt=F32):
            return ctx.enter_context(nc.sbuf_tensor(name, shape, dt))

        def sem(name):
            return ctx.enter_context(nc.semaphore(name))

        def signal(name, per, primed=0):
            return Signal(sem(name), per, primed)

        x = sb("x", [P, TT, D])
        raw = [sb(f"raw{i}", [P, 2048]) for i in range(RAW)]
        w_hi = [sb(f"w_hi{i}", [P, 2048], F32R) for i in range(SPLIT)]
        w_lo = [sb(f"w_lo{i}", [P, 2048], F32R) for i in range(SPLIT)]
        u_hi = sb("u_hi", [P, KD, S], F32R)
        u_lo = sb("u_lo", [P, KD, S], F32R)
        h_hi = sb("h_hi", [P, 16, S], F32R)
        h_lo = sb("h_lo", [P, 16, S], F32R)
        a0 = sb("a0", [P, 8 * (S + 3)])
        a1, a2, a3, a4, a5 = (sb(f"a{i}", [P, 2048]) for i in range(1, 6))
        act2 = sb("act2", [P, 2, 512])
        mul2 = sb("mul2", [P, 2, 512])
        probs = sb("probs", [P, 2, 384])
        gain_row = sb("gain_row", [P, D])
        decay = sb("decay", [P, HEADS, 384])
        cos2 = sb("cos2", [P, S])
        sin2 = sb("sin2", [P, S])
        ident = sb("ident", [P, P])
        rows = sb("rows", [32, D])
        vec = sb("vec", [P, KD, NVEC])
        lv = sb("lv", [P, KD, NV])
        small = sb("small", [P, 64])
        inv_freq = sb("inv_freq", [P, 1])
        minus_half = sb("minus_half", [P, 4])
        sink = sb("sink", [P, 8])
        soft = sb("soft", [P, 5, 2 * KD])
        rates = sb("rates", [P, KD, 2 * DEPTH])
        lrates = sb("lrates", [P, KD, 2])
        ps = ctx.enter_context(nc.psum_tensor("ps", [P, 8, 512], F32))

        def tiles(a):
            return a[:, 0:2048].rearrange("p (k n) -> p k n", n=S)

        xa_pad = a0[:, :].rearrange("p (k n) -> p k n", n=S + 3)
        prod_pad = a0[:, 0:8 * (S + 2)].rearrange("p (k n) -> p k n", n=S + 2)
        scaled = a3[:, :].rearrange("p (t n) -> p t n", t=TT)
        rescaled = a4[:, :].rearrange("p (t n) -> p t n", t=TT)
        lru_w = a2[:, :].rearrange("p (m c n) -> p m c n", m=2, c=KD)
        q_t, k_t = tiles(a3), tiles(a4)
        v_rows = [a0, a1]
        pre_ss, pre_ms, pre_rs = small[:, 0:4], small[:, 4:8], small[:, 8:12]
        onehot, allowed = rows[0:32, 0:REL], rows[0:NHEAD, 512:512 + REL]
        rel = rows[0:NHEAD, 0:REL]
        table = small[0:32, 32:32 + NHEAD]
        post_ss, post_ms, post_rs = small[:, 48:52], small[:, 12:14], small[:, 14:16]
        ret_ss, ret_ms, ret_rs = small[:, 16:18], small[:, 18:20], small[:, 20:22]

        raw_loaded = [signal(f"raw_loaded{i}", 16 * SLOTS // RAW) for i in range(RAW)]
        heads_done = signal("heads_done", 2 * SLOTS)
        split_done = signal("split_done", SLOTS, RAW)
        slot_used = signal("slot_used", SLOTS)
        x_loaded = sem("x_loaded")
        x_ready = signal("x_ready", 12, 4)
        pre_sum = signal("pre_sum", 12)
        pre_scale = signal("pre_scale", 6)
        pre_scaled = signal("pre_scaled", 12)
        u_turned = signal("u_turned", 3 * KD)
        u_head = signal("u_head", 3 * KD)
        u_ready = signal("u_ready", 3 * KD)
        rows_done = signal("rows_done", 3)
        post_sum = signal("post_sum", 12)
        gained = signal("gained", 12)
        post_scale = signal("post_scale", 6)
        gain_loaded = signal("gain_loaded", 3 * 16)
        act_ready = signal("act_ready", 2 * FFN_PAIRS, 2)
        mul_ready = signal("mul_ready", 2 * FFN_PAIRS, 2)
        h_ready = signal("h_ready", 2 * FFN_PAIRS)
        lv_ready = signal("lv_ready", 1)
        lru_w_loaded = signal("lru_w_loaded", 4 * 16)
        xa_ready = signal("xa_ready", 4)
        xc_ready = signal("xc_ready", KD)
        lru_gates = signal("lru_gates", KD)
        lru_acts = signal("lru_acts", KD)
        gated_x = signal("gated_x", KD, 2)
        roots_ready = signal("roots_ready", 1)
        q_ready = signal("q_ready", 4)
        k_ready = signal("k_ready", 4)
        gelu_ready = signal("gelu_ready", 4)
        oa_ready = signal("oa_ready", 4)
        ga_ready = signal("ga_ready", 4)
        acc_ready = signal("acc_ready", 4)
        v_ready0 = signal("v_ready0", 2)
        v_ready1 = signal("v_ready1", 2)
        g_ready = signal("g_ready", 8)
        ret_scores = signal("ret_scores", HEADS)
        ret_probs = signal("ret_probs", HEADS)
        ret_out = signal("ret_out", HEADS)
        ret_sum = signal("ret_sum", HEADS)
        ret_scale = signal("ret_scale", HEADS)
        ret_scaled = signal("ret_scaled", HEADS)
        ret_turned = signal("ret_turned", HEADS)
        ret_ready = signal("ret_ready", HEADS, 1)
        sc_ready = signal("sc_ready", 4)
        sh_ready = signal("sh_ready", 4)
        gb_ready = signal("gb_ready", 4)
        ret_added = signal("ret_added", 4)
        oc_ready = signal("oc_ready", 4)
        gc_ready = signal("gc_ready", 4)
        mix_ready = signal("mix_ready", 4)
        vec_loaded, consts_loaded = sem("vec_loaded"), sem("consts_loaded")
        pos_loaded = sem("pos_loaded")
        ident_ready, halves_ready = sem("ident_ready"), sem("halves_ready")
        vec_turned = sem("vec_turned")
        lam_ready, lam_exp, angles, sines = sem("lam_ready"), sem("lam_exp"), sem("angles"), sem("sines")
        rel_done, rel_ready, rel_stored = sem("rel_done"), sem("rel_ready"), sem("rel_stored")
        act_own, dve_own, pool_own, pool_steps = sem("act_own"), sem("dve_own"), sem("pool_own"), sem("pool_steps")
        b = {n: sem(n) for n in (
            "proj_ready", "ka_swapped", "v_turned", "v_rows_a", "v_rows_b", "bias_loaded0", "bias_loaded1",
            "scored", "logits", "row_max", "exps", "turned", "exps_t", "attended", "den_ready",
            "attn_rows", "attn_sum", "attn_scale", "relu_ready", "sq_ready", "hid_ready", "p_loaded",
            "p_turned", "p_head", "p_ready", "brow_loaded", "gate_in", "gate_ready", "gated", "ple_sum",
            "ple_scale", "out_ready", "out_stored", "sink_loaded")}

        k_major = "l (k p) n -> p (l k) n"
        w_ffn_in = [t["ffn1_w_in"].rearrange(k_major, p=P), t["ffn2_w_in"].rearrange(k_major, p=P)]
        w_ffn_out = [t["ffn1_w_out"].rearrange(k_major, p=P), t["ffn2_w_out"].rearrange(k_major, p=P)]
        w_mix_in = t["w_mix_in"].rearrange(k_major, p=P)
        w_out = {n: t[w].rearrange(k_major, p=P) for n, w in (
            ("lru_out", "w_lru_out"), ("ret_out", "w_ret_out"), ("sc_out", "w_sc_out"), ("mix_out", "w_mix_out"))}
        b_w = {n: t[n + "_2"].rearrange(k_major, p=P)
               for n in ("w_in", "w_o", "w_up", "w_down", "w_ple_gate", "w_ple_proj")}

        def turned(l, i, k):
            first = (0, 2, 1, 0)[i] if l is DEPTH else (0, 2, 2)[i]
            bank = (first + k // 2) % 4
            return ps[:, bank, S * (k % 2):S * (k % 2) + S]

        def bcast(row, n):
            return row.broadcast_to([P, n])

        def col_view(buf, n):
            return buf[n][:, :].rearrange("p (k n) -> p k n", n=SLOTC)

        def row_view(buf, n):
            return buf[n][:, :].rearrange("p (k n) -> p k n", n=D)

        block = ctx.enter_context(nc.Block())

        @block.sync
        def _(sp):
            def load(l, n, src, half=False):
                sp.wait_ge(split_done.sem, split_done.at(l, n - RAW + 1))
                size = src.shape[1] * src.shape[2]
                dst = raw[n % RAW][:, 0:size].rearrange("p (k n) -> p k n", n=src.shape[2])
                sp.dma_start(dst, src).then_inc(raw_loaded[n % RAW].sem, 16)

            def feed_forward(l, which, base):
                w_in, w_o = w_ffn_in[which], w_ffn_out[which]

                def gate_up(n, col):
                    load(l, n, w_in[:, ds(l * KD, KD), ds(col, SLOTC)])
                    load(l, n + 1, w_in[:, ds(l * KD, KD), ds(col + D_FF, SLOTC)])

                with sp.Fori(0, FIRST_PAIRS // 2) as it:
                    for j in range(4):
                        n = base + j
                        sp.wait_ge(split_done.sem, l * SLOTS + it * 4 + (RAW + n - RAW + 1))
                        col = it * (2 * SLOTC) + ((j // 2) * SLOTC + (j % 2) * D_FF)
                        sp.dma_start(col_view(raw, n % RAW), w_in[:, ds(l * KD, KD), ds(col, SLOTC)])\
                          .then_inc(raw_loaded[n % RAW].sem, 16)
                for p in range(FIRST_PAIRS):
                    load(l, base + 2 * FIRST_PAIRS + p, w_o[:, ds(l * 2 * FFN_PAIRS + 2 * p, 2), :])
                for p in range(FIRST_PAIRS, FFN_PAIRS):
                    gate_up(base + FFN_IN2 + 2 * (p - FIRST_PAIRS), p * SLOTC)
                for i in range(2):
                    load(l, base + FFN_OUT2 + i, w_o[:, ds(l * 2 * FFN_PAIRS + 2 * FIRST_PAIRS + i, 1), :])
                for p in range(FIRST_PAIRS + 1, FFN_PAIRS):
                    load(l, base + FFN_OUT2 + 1 + p - FIRST_PAIRS, w_o[:, ds(l * 2 * FFN_PAIRS + 2 * p, 2), :])

            def mixer(l):
                for name, count in STAGES:
                    for j in range(count):
                        n = AT[name] + j
                        if name in V_HALF:
                            c = MC["v"] + D * V_HALF[name]
                            src = w_mix_in[:, ds(l * KD + 2 * j, 2), c:c + D]
                        elif name in MC:
                            src = w_mix_in[:, ds(l * KD, KD), MC[name] + SLOTC * j:MC[name] + SLOTC * (j + 1)]
                        elif name == "ret_out":
                            c = SLOTC * (j // 2)
                            src = w_out[name][:, ds(l * 2 * KD + KD * (j % 2), KD), c:c + SLOTC]
                        elif name == "mix_out":
                            src = w_out[name][:, ds(l * KD + 2 * j, 2), :]
                        else:
                            src = w_out[name][:, ds(l * KD, KD), SLOTC * j:SLOTC * (j + 1)]
                        load(l, n, src)

            sp.sem_inc(split_done.sem, RAW)
            sp.dma_start(x[:, :, :], t["x"].rearrange("b (t p) d -> p (b t) d", p=P)).then_inc(x_loaded, 16)
            with sp.Fori(0, DEPTH) as l:
                feed_forward(l, 0, 0)
                mixer(l)
                feed_forward(l, 1, FFN2)
            l = DEPTH
            for j in range(9):
                load(l, B_IN + j, b_w["w_in"][:, :, SLOTC * j:SLOTC * (j + 1)])
            for j in range(4):
                load(l, B_O + j, b_w["w_o"][:, 2 * j:2 * j + 2, :])
            for part in range(2):
                up, down = (B_UP, B_DN) if part == 0 else (B_UP2, B_DN2)
                for j in range(8):
                    c = SLOTC * (8 * part + j)
                    load(l, up + j, b_w["w_up"][:, :, c:c + SLOTC])
                for j in range(8):
                    k = 2 * (8 * part + j)
                    load(l, down + j, b_w["w_down"][:, k:k + 2, :])
            for j in range(4):
                load(l, B_GATE + j, b_w["w_ple_gate"][:, 2 * j:2 * j + 2, :])
            load(l, B_PLE, b_w["w_ple_proj"][:, 0:2, :])
            for tt in range(TT):
                sp.wait_ge(b["out_ready"], tt + 1)
                sp.dma_start(out.rearrange("b (t p) d -> p (b t) d", p=P)[:, tt, :], x[:, tt, :])\
                  .then_inc(b["out_stored"], 16)
            sp.wait_ge(b["out_stored"], 16 * TT)

        @block.gpsimd
        def _(pool):
            own = Chain(pool, pool_own)

            def until(sig, count):
                pool.wait_ge(sig.sem, count)
                pool.sem_inc(pool_steps, 1)

            def norm(l, i, ss, ms, rs, sums, scale, by=1.0):
                for tt in range(TT):
                    until(sums, sums.at(l, 4 * i + 2 * tt + 2))
                    own.done(nc.gpsimd.tensor_scalar(ms[:, tt:tt + 1], ss[:, 2 * tt:2 * tt + 1],
                                                     ss[:, 2 * tt + 1:2 * tt + 2], EPS / (by * by), ALU.add, ALU.add))
                    nc.gpsimd.tensor_tensor(rs[:, tt:tt + 1], ms[:, tt:tt + 1], minus_half[:, 0:1], ALU.pow)\
                      .then_inc(scale.sem, 1)

            def pre(l, i):
                norm(l, i, pre_ss, pre_ms, pre_rs, pre_sum, pre_scale)

            def post(l, i, by):
                norm(l, i, post_ss, post_ms, post_rs, post_sum, post_scale, by)

            def gain(l, i, src):
                until(x_ready, x_ready.at(l, 4 * i))
                pool.dma_start(gain_row[:, :], src).then_inc(gain_loaded.sem, 16)

            def gain_of(name, l):
                return bcast(t[name][ds(l, 1), :], D)

            nc.gpsimd.memset(minus_half[:, :], -0.5).then_inc(halves_ready, 1)
            pool.wait_ge(halves_ready, 1)
            own.done(nc.gpsimd.memset(ident[:, :], 0.0))
            nc.gpsimd.affine_select(out=ident[:, :], in_=ident[:, :], compare_op=ALU.not_equal, fill=1.0,
                                    base=0, pattern=[[-1, P]], channel_multiplier=1).then_inc(ident_ready, 1)
            pool.dma_start(a0[:, 0:S].bitcast(I32), bcast(t["positions"].rearrange("(a n) -> a n", a=1), S))\
                .then_inc(pos_loaded, 16)
            pool.dma_start(inv_freq[:, :], t["inv_freq"]).then_inc(pos_loaded, 16)
            pool.dma_start(sink[:, :], bcast(t["sink_a_2"], 8)).then_inc(b["sink_loaded"], 16)
            pool.dma_start(decay[:, :, :].rearrange("p h n -> p (h n)"), t["decay"]).then_inc(consts_loaded, 16)
            pool.wait_ge(vec_turned, 1)
            pool.dma_start(table, t["rel_bias_table_2"]).then_inc(consts_loaded, 16)
            pool.dma_start(onehot, t["onehot"]).then_inc(consts_loaded, 16)
            pool.dma_start(allowed, t["allowed"]).then_inc(consts_loaded, 16)
            own.restart()
            with pool.Fori(0, DEPTH) as l:
                pre(l, 0)
                until(ret_ready, ret_ready.at(l, 0))
                own.done(nc.gpsimd.memset(a2[:, :], 0.0))
                for m, name in enumerate(("lru_w_a", "lru_w_x")):
                    w = t[name].rearrange("l (c e) i j -> e i (l c) j", e=2)
                    for e in range(2):
                        pool.dma_start(lru_w[64 * e:64 * e + 64, m, :, 64 * e:64 * e + 64],
                                       w[e, :, ds(l * KD, KD), :]).then_inc(lru_w_loaded.sem, 16)
                gain(l, 0, gain_of("ffn1_post_g", l))
                post(l, 0, 0.5)
                pre(l, 1)
                gain(l, 1, gain_of("mix_post_g", l))
                for h in range(HEADS):
                    until(ret_sum, ret_sum.at(l, h + 1))
                    own.done(nc.gpsimd.tensor_scalar(ret_ms, ret_ss, 1.0 / HV, EPS, ALU.mult, ALU.add))
                    nc.gpsimd.tensor_tensor(ret_rs, ret_ms, minus_half[:, 0:2], ALU.pow).then_inc(ret_scale.sem, 1)
                post(l, 1, 1.0)
                pre(l, 2)
                gain(l, 2, gain_of("ffn2_post_g", l))
                post(l, 2, 0.5)
                own.restart()
            l = DEPTH
            pre(l, 0)
            gain(l, 0, gain_of("g_post_mix_2", 0))
            pool.wait_ge(rel_stored, 16)
            def band(h):
                ring = a1 if h % 10 < 5 else a2
                s = (h % 5) * BIASW
                return ring[:, s:s + BIASW]
            for h in range(NHEAD):
                if h >= 10:
                    pool.wait_ge(b["logits"], h - 9)
                elif h == 0:
                    pool.wait_ge(x_ready.sem, x_ready.at(l, 0))
                src = bass.AP(tensor=scratch.tensor, offset=scratch.offset + h * 512, ap=[[1, P], [1, BIASW]])
                pool.dma_start(band(h), src).then_inc(b["bias_loaded0" if h % 2 == 0 else "bias_loaded1"], 16)
                pool.wait_ge(b["bias_loaded0" if h % 2 == 0 else "bias_loaded1"], 16 * (h // 2 + 1))
            pool.wait_ge(b["attn_sum"], 4)
            own.done(nc.gpsimd.tensor_scalar(pre_ms, pre_ss, 1.0 / 512, EPS, ALU.mult, ALU.add))
            nc.gpsimd.tensor_tensor(pre_rs, pre_ms, minus_half[:, :], ALU.pow).then_inc(b["attn_scale"], 1)
            post(l, 0, 1.0)
            pre(l, 1)
            gain(l, 1, gain_of("g_post_mlp_2", 0))
            pool.wait_ge(b["den_ready"], 2)
            pool.dma_start(a1[:, 0:2 * S].rearrange("p (t n) -> p t n", t=TT),
                           t["p_2"].rearrange("l b (t p) n -> p (l b t) n", p=P)).then_inc(b["p_loaded"], 16)
            post(l, 1, 1.0)
            gain(l, 2, gain_of("g_post_ple_2", 0))
            pool.dma_start(a2[:, 0:D], gain_of("b_ple_gate_2", 0)).then_inc(b["brow_loaded"], 16)
            for tt in range(TT):
                pool.wait_ge(b["ple_sum"], tt + 1)
                own.done(nc.gpsimd.tensor_scalar(post_ms[:, tt:tt + 1], post_ss[:, tt:tt + 1], 1.0 / D, EPS,
                                                 ALU.mult, ALU.add))
                nc.gpsimd.tensor_tensor(post_rs[:, tt:tt + 1], post_ms[:, tt:tt + 1], minus_half[:, 0:1], ALU.pow)\
                  .then_inc(b["ple_scale"], 1)

        @block.scalar
        def _(act):
            A = nc.scalar.activation
            own = Chain(act, act_own)

            def head(l, n, size=2048, it=0, first=False):
                r = n % RAW
                act.wait_ge(raw_loaded[r].sem, raw_loaded[r].at(l, 16 * (n // RAW + 1)) + it * 16)
                if not first:
                    act.wait_ge(slot_used.sem, slot_used.at(l, n - 1) + it * 4)
                for i in range(2):
                    part = slice(i * size // 2, (i + 1) * size // 2)
                    A(w_hi[n % SPLIT][:, part], raw[r][:, part], ACT.Copy).then_inc(heads_done.sem, 1)

            def pre(l, i, gains, col, base, t=None):
                for q in range(2 * TT):
                    tt, half = q // 2, slice(512 * (q % 2), 512 * (q % 2) + 512)
                    act.wait_ge(x_ready.sem, x_ready.at(l, 4 * i + q - 3))
                    A(a5[:, 512 * q:512 * q + 512], x[:, tt, half], ACT.Square, scale=D ** -0.5,
                      accum_out=pre_ss[:, q:q + 1]).then_inc(pre_sum.sem, 1)
                head(l, base + 1)
                if i == 0 and gains is lv:
                    act.wait_ge(lv_ready.sem, lv_ready.at(l, 1))
                u_heads(l, i if t is None else t, gains, col)

            def u_heads(l, i, gains, col):
                for k in range(KD):
                    act.wait_ge(u_turned.sem, u_turned.at(l, KD * i + (k | 1) + 1))
                    A(u_hi[:, k, :], turned(l, i, k), ACT.Copy, scale=gains[:, k, col:col + 1]).then_inc(u_head.sem, 1)

            def post(l, i, end, by=1.0):
                for q in range(2 * TT):
                    tt = q // 2
                    if q == 0:
                        act.wait_ge(rows_done.sem, rows_done.at(l, i + 1))
                    elif q == 2:
                        act.wait_ge(slot_used.sem, slot_used.at(l, end))
                    else:
                        act.wait_ge(gained.sem, gained.at(l, 4 * i + 2 * tt + 1))
                    A(a5[:, 512 * q:512 * q + 512], ps[:, 4 + q, :], ACT.Square, scale=D ** -0.5 / by,
                      accum_out=post_ss[:, q:q + 1]).then_inc(post_sum.sem, 1)

            def silu(l, which, base, p, it=0):
                pair = FFN_PAIRS * which + p
                n = base + (2 * p if p < FIRST_PAIRS else FFN_IN2 + 2 * (p - FIRST_PAIRS))
                bank = (2 * which + 2 * p) % 4
                act.wait_ge(slot_used.sem, slot_used.at(l, n + 1) + it * 4)
                act.wait_ge(mul_ready.sem, mul_ready.at(l, pair - 1) + it * 2)
                A(act2[:, pair % 2, :], ps[:, bank, :], ACT.Silu).then_inc(act_ready.sem, 1)

            def feed_forward(l, which, base):
                with act.Fori(0, FIRST_PAIRS // 2) as it:
                    for j in range(4):
                        head(l, base + j + 2, it=it)
                        if j % 2 == 0:
                            silu(l, which, base, j // 2, it)
                for n in range(base + 2 * FIRST_PAIRS, base + FFN_SLOTS - 1):
                    at = n - base
                    head(l, n + 2, 1024 if FFN_OUT2 <= at + 2 < FFN_OUT2 + 2 else 2048)
                    if FFN_IN2 <= at < FFN_OUT2 and (at - FFN_IN2) % 2 == 0:
                        silu(l, which, base, FIRST_PAIRS + (at - FFN_IN2) // 2)
                post(l, 2 * which, base + FFN_SLOTS, 0.5)

            def from_slot(l, n):
                act.wait_ge(slot_used.sem, slot_used.at(l, n + 1))

            def mixer(l):
                for name, count in STAGES:
                    for j in range(count):
                        n = AT[name] + j
                        m = n - MIX0
                        bank = (2 + j) % 4
                        pair = slice(2 * j, 2 * j + 2)
                        pv = ps[:, bank, :].rearrange("p (a n) -> p a n", a=2)
                        c = m - 5
                        if 0 <= c < KD:
                            act.wait_ge(lru_gates.sem, lru_gates.at(l, c + 1))
                            act.wait_ge(gated_x.sem, gated_x.at(l, c - 1))
                            if c == 0:
                                act.wait_ge(xc_ready.sem, xc_ready.at(l, KD))
                            own.done(A(tiles(a5)[:, c, :], ps[:, 4 + c % 4, 0:S], ACT.Sigmoid,
                                       bias=lv[:, c, V_BA:V_BA + 1]))
                            A(act2[:, 0, S * (c % 2):S * (c % 2) + S], ps[:, 4 + c % 4, S:2 * S], ACT.Sigmoid,
                              bias=lv[:, c, V_BX:V_BX + 1])
                            A(tiles(a0)[:, c, :], tiles(a5)[:, c, :], ACT.Tanh, scale=lrates[:, c, 0:1])\
                              .then_inc(lru_acts.sem, 1)
                            if c == KD - 1:
                                act.wait_ge(lru_acts.sem, lru_acts.at(l, KD))
                                for k in range(KD):
                                    A(tiles(a5)[:, k, :], tiles(a5)[:, k, :], ACT.Exp, scale=lrates[:, k, 1:2])
                                A(a0[:, 0:2048], a0[:, 0:2048], ACT.Sqrt).then_inc(roots_ready.sem, 1)
                        if name == "g" and j % 2 == 1:
                            h = j // 2
                            act.wait_ge(ret_out.sem, ret_out.at(l, h + 1))
                            if h >= 1:
                                act.wait_ge(ret_scale.sem, ret_scale.at(l, h))
                            for tt in range(TT):
                                own.done(A(act2[:, 1, :], ps[:, 5 + tt, :], ACT.Square, accum_out=ret_ss[:, tt:tt + 1]))
                            act.sem_inc(ret_sum.sem, 1)
                            own.restart()
                        if n < FFN2 - 1:
                            head(l, n + 2)
                        if name in ("xa", "ya", "ga", "g", "sc", "gb", "gc"):
                            from_slot(l, n)
                        if name == "xa":
                            A(xa_pad[:, pair, 3:3 + S], pv, ACT.Copy).then_inc(xa_ready.sem, 1)
                        elif name == "ya":
                            A(tiles(a2)[:, pair, :], pv, ACT.Gelu_apprx_tanh).then_inc(gelu_ready.sem, 1)
                        elif name == "ga":
                            act.wait_ge(oa_ready.sem, oa_ready.at(l, j + 1))
                            A(tiles(a5)[:, pair, :], pv, ACT.Sigmoid).then_inc(ga_ready.sem, 1)
                        elif name in V_HALF and j == 3:
                            from_slot(l, n)
                            act.wait_ge(oa_ready.sem, oa_ready.at(l, 4))
                            A(v_rows[0][:, D * V_HALF[name]:D * V_HALF[name] + D], ps[:, 4:6, :].rearrange("p a n -> p (a n)"),
                              ACT.Copy).then_inc(v_ready0.sem, 1)
                        elif name == "g":
                            if j >= 4:
                                act.wait_ge(ret_ready.sem, ret_ready.at(l, j // 2 - 1))
                            A(a2[:, 512 * (j % 4):512 * (j % 4) + 512], ps[:, bank, :], ACT.Silu).then_inc(g_ready.sem, 1)
                        elif name == "sc":
                            A(tiles(a1)[:, pair, :], pv, ACT.Copy).then_inc(sc_ready.sem, 1)
                        elif name == "gb":
                            A(tiles(a4)[:, pair, :], pv, ACT.Sigmoid).then_inc(gb_ready.sem, 1)
                        elif name == "gc":
                            act.wait_ge(ret_added.sem, ret_added.at(l, j + 1))
                            A(tiles(a4)[:, pair, :], pv, ACT.Sigmoid).then_inc(gc_ready.sem, 1)
                post(l, 1, FFN2)

            for v, name in ((V_G1, "ffn1_pre_g"), (V_GM, "mix_pre_g"), (V_CB, "lru_conv_b"), (V_BA, "lru_b_a"),
                            (V_BX, "lru_b_x"), (V_LAM, "lru_lambda"), (V_G2, "ffn2_pre_g")):
                act.dma_start(rows[v:v + NV * (DEPTH - 1) + 1:NV, :], t[name]).then_inc(vec_loaded, 16)
            for l in range(DEPTH):
                act.dma_start(rows[l * NV + V_CW:l * NV + V_CW + 4, :], t["lru_conv_w"][l]).then_inc(vec_loaded, 16)
                act.dma_start(rows[l * NV + V_SW:l * NV + V_SW + 3, :], t["sc_conv_w"][l]).then_inc(vec_loaded, 16)
            act.dma_start(rows[V2_GMIX:V2_GMIX + 1, :], t["g_pre_mix_2"]).then_inc(vec_loaded, 16)
            act.dma_start(rows[V2_GMLP:V2_GMLP + 1, :], t["g_pre_mlp_2"]).then_inc(vec_loaded, 16)
            act.dma_start(rows[V2_GOUT:V2_GOUT + 1, 0:512], t["g_out_a_2"]).then_inc(vec_loaded, 16)
            act.dma_start(rows[V2_GOUT:V2_GOUT + 1, 512:D], t["g_out_b_2"]).then_inc(vec_loaded, 16)
            act.wait_ge(angles, 1)
            A(sin2[:, :], sin2[:, :], ACT.Sin).then_inc(sines, 1)
            A(cos2[:, :], cos2[:, :], ACT.Sin).then_inc(sines, 1)
            head(0, 0, first=True)
            act.wait_ge(lam_ready, 1)
            A(soft[:, 1, :], soft[:, 1, :], ACT.Exp, scale=-1.0).then_inc(lam_exp, 1)
            with act.Fori(0, DEPTH) as l:
                pre(l, 0, lv, V_G1, 0)
                feed_forward(l, 0, 0)
                pre(l, 1, lv, V_GM, MIX0)
                mixer(l)
                pre(l, 2, lv, V_G2, FFN2)
                feed_forward(l, 1, FFN2)

            l = DEPTH
            pre(l, 0, vec, V2_GMIX, B_IN)
            act.wait_ge(rel_ready, 1)
            act.dma_start(scratch[:, 0:REL], rel).then_inc(rel_stored, 16)
            dst = {0: (a3, 0), 1: (a3, 512), 2: (a4, 0), 3: (a3, 1024), 4: (a3, 1536), 5: (a4, 512), 6: (a4, 1024),
                   7: (a5, 0), 8: (a5, 512)}
            for j in range(9):
                head(l, j + 2)
                a, o = dst[j]
                A(a[:, o:o + 512], ps[:, j % 4, :], ACT.Copy).then_inc(b["proj_ready"], 1)
            act.wait_ge(b["proj_ready"], 3)
            act.dma_start(a4[64:128, 1536:1536 + S], a4[0:64, 0:S]).then_inc(b["ka_swapped"], 16)
            act.dma_start(a4[0:64, 1536:1536 + S], a4[64:128, 0:S]).then_inc(b["ka_swapped"], 16)
            act.wait_ge(b["v_turned"], 1)
            A(v_rows[0][:, 0:512], ps[:, 4, :], ACT.Copy).then_inc(b["v_rows_a"], 1)
            A(v_rows[0][:, 640:640 + 512], ps[:, 5, :], ACT.Copy).then_inc(b["v_rows_a"], 1)
            def exps_columns(h):
                act.wait_ge(b["turned"], h + 1)
                if h >= 2:
                    act.wait_ge(b["attended"], h - 1)
                A(mul2[:, h % 2, :], ps[:, 2 + h % 2, :], ACT.Copy).then_inc(b["exps_t"], 1)
            for h in range(NHEAD):
                act.wait_ge(b["row_max"], h + 1)
                for tt in range(TT):
                    c = 4 * (h % 2) + tt
                    A(act2[:, h % 2, S * tt:S * tt + S], act2[:, h % 2, S * tt:S * tt + S], ACT.Exp,
                      bias=small[:, 24 + c:25 + c], accum_out=probs[:, 0, 2 * h + tt:2 * h + tt + 1])\
                      .then_inc(b["exps"], 1)
                if h < 8:
                    for tt in range(TT):
                        c = 4 * (h % 2) + tt
                        A(probs[:, 1, 2 * h + tt:2 * h + tt + 1], sink[:, h:h + 1], ACT.Exp,
                          bias=small[:, 24 + c:25 + c]).then_inc(b["exps"], 1)
                if h >= 1:
                    exps_columns(h - 1)
            exps_columns(NHEAD - 1)
            for tt in range(TT):
                for kind in range(2):
                    i = 2 * tt + kind
                    act.wait_ge(b["attn_rows"], i + 1)
                    own.done(A(a5[:, 0:512], a1[:, D * tt + 512 * kind:D * tt + 512 * kind + 512], ACT.Square,
                               accum_out=pre_ss[:, i:i + 1]))
                    act.sem_inc(b["attn_sum"], 1)
            u_heads(l, 1, vec, V2_GOUT)
            for j in range(B_O, B_UP - 1):
                head(l, j + 2)
            post(l, 0, B_UP)
            pre(l, 1, vec, V2_GMLP, B_UP, t=2)
            for part in range(2):
                for j in range(16):
                    n = (B_UP if part == 0 else B_UP2) + j
                    if n < B_GATE - 1:
                        head(l, n + 2)
                    if j < 8:
                        p = 8 * part + j
                        act.wait_ge(slot_used.sem, slot_used.at(l, n + 1))
                        if p >= 2:
                            act.wait_ge(b["sq_ready"], p - 1)
                        A(act2[:, p % 2, :], ps[:, (9 + p) % 4, :], ACT.Relu).then_inc(b["relu_ready"], 1)
            post(l, 1, B_GATE)
            for k in range(KD):
                act.wait_ge(u_turned.sem, u_turned.at(l, KD * 3 + (k | 1) + 1))
                A(u_hi[:, k, :], turned(l, 3, k), ACT.Copy).then_inc(u_head.sem, 1)
            act.wait_ge(b["p_turned"], 1)
            A(h_hi[:, 0:2, :], ps[:, 4, :].rearrange("p (a n) -> p a n", a=2), ACT.Copy).then_inc(b["p_head"], 1)
            for n in range(B_GATE - 1, B_SLOTS - 2):
                head(l, n + 2)
            for tt in range(TT):
                act.wait_ge(b["gate_in"], tt + 1)
                A(a3[:, D * tt:D * tt + D], a3[:, D * tt:D * tt + D], ACT.Sigmoid).then_inc(b["gate_ready"], 1)
                act.wait_ge(b["gated"], tt + 1)
                own.done(A(a5[:, 0:D], a3[:, D * tt:D * tt + D], ACT.Square, accum_out=post_ss[:, tt:tt + 1]))
                act.sem_inc(b["ple_sum"], 1)

        @block.vector
        def _(dve):
            V = nc.vector
            own = Chain(dve, dve_own)

            def rest(l, n, size=2048, it=0):
                for i in range(2):
                    part = slice(i * size // 2, (i + 1) * size // 2)
                    dve.wait_ge(heads_done.sem, heads_done.at(l, 2 * n + i + 1) + it * 8)
                    ins = V.tensor_tensor(w_lo[n % SPLIT][:, part], raw[n % RAW][:, part], w_hi[n % SPLIT][:, part],
                                          ALU.subtract)
                ins.then_inc(split_done.sem, 1)

            def pre(l, i, gains, col, base, t=None):
                for q in range(2 * TT):
                    tt, half = q // 2, slice(512 * (q % 2), 512 * (q % 2) + 512)
                    dve.wait_ge(pre_scale.sem, pre_scale.at(l, TT * i + tt + 1))
                    V.tensor_scalar(scaled[:, tt, half], x[:, tt, half], pre_rs[:, tt:tt + 1], None, ALU.mult)\
                     .then_inc(pre_scaled.sem, 1)
                u_rests(l, i if t is None else t, gains, col)
                rest(l, base + 1)

            def u_rests(l, i, gains, col):
                for k in range(KD):
                    dve.wait_ge(u_head.sem, u_head.at(l, KD * i + (k | 1) + 1))
                    V.scalar_tensor_tensor(u_lo[:, k, :], turned(l, i, k), gains[:, k, col:col + 1], u_hi[:, k, :], ALU.mult, ALU.subtract)\
                     .then_inc(u_ready.sem, 1)

            def post(l, i, end):
                def gain_halves(tt):
                    if tt == 0:
                        dve.wait_ge(rows_done.sem, rows_done.at(l, i + 1))
                    else:
                        dve.wait_ge(slot_used.sem, slot_used.at(l, end))
                    for q in (2 * tt + 1, 2 * tt):
                        half = slice(512 * (q % 2), 512 * (q % 2) + 512)
                        if q == 2 * tt:
                            dve.wait_ge(post_sum.sem, post_sum.at(l, 4 * i + q + 1))
                        V.tensor_tensor(rescaled[:, tt, half], ps[:, 4 + q, :], gain_row[:, half], ALU.mult)\
                         .then_inc(gained.sem, 1)
                    dve.wait_ge(gained.sem, gained.at(l, 4 * i + 2 * tt + 2))

                def add(q):
                    tt, half = q // 2, slice(512 * (q % 2), 512 * (q % 2) + 512)
                    dve.wait_ge(post_scale.sem, post_scale.at(l, TT * i + tt + 1))
                    V.scalar_tensor_tensor(x[:, tt, half], rescaled[:, tt, half], post_rs[:, tt:tt + 1], x[:, tt, half],
                                           ALU.mult, ALU.add).then_inc(x_ready.sem, 1)

                dve.wait_ge(gain_loaded.sem, gain_loaded.at(l, 16 * (i + 1)))
                gain_halves(0)
                add(0)
                gain_halves(1)
                for q in (1, 2, 3):
                    add(q)

            def split(src, hi, lo, sig):
                own.done(V.tensor_copy(hi, src))
                V.tensor_tensor(lo, src, hi, ALU.subtract).then_inc(sig, 1)

            def hidden(l, which, base, p, it=0):
                pair = FFN_PAIRS * which + p
                n = base + (2 * p if p < FIRST_PAIRS else FFN_IN2 + 2 * (p - FIRST_PAIRS)) + 1
                bank = (2 * which + 2 * p) % 4 + 1
                dve.wait_ge(slot_used.sem, slot_used.at(l, n + 1) + it * 4)
                dve.wait_ge(act_ready.sem, act_ready.at(l, pair + 1) + it * 2)
                V.tensor_tensor(mul2[:, pair % 2, :], ps[:, bank, :], act2[:, pair % 2, :], ALU.mult)\
                 .then_inc(mul_ready.sem, 1)
                dve.wait_ge(mul_ready.sem, mul_ready.at(l, pair + 1) + it * 2)
                k = ds(2 * p + it * 4, 2) if p < FIRST_PAIRS else slice(2 * (p - FIRST_PAIRS), 2 * (p - FIRST_PAIRS) + 2)
                split(mul2[:, pair % 2, :].rearrange("p (a n) -> p a n", a=2), h_hi[:, k, :], h_lo[:, k, :], h_ready.sem)

            def feed_forward(l, which, base):
                own.restart()
                with dve.Fori(0, FIRST_PAIRS // 2) as it:
                    for j in range(4):
                        rest(l, base + j + 2, it=it)
                        if j % 2 == 1:
                            hidden(l, which, base, j // 2, it)
                    own.restart()
                for n in range(base + 2 * FIRST_PAIRS, base + FFN_SLOTS - 1):
                    at = n - base
                    rest(l, n + 2, 1024 if FFN_OUT2 <= at + 2 < FFN_OUT2 + 2 else 2048)
                    if FFN_IN2 <= at < FFN_OUT2 and (at - FFN_IN2) % 2 == 1:
                        hidden(l, which, base, FIRST_PAIRS + (at - FFN_IN2) // 2)
                post(l, 2 * which, base + FFN_SLOTS)

            def rope(l, j, bank, dst, sig):
                pv = ps[:, bank, :].rearrange("p (a n) -> p a n", a=2)
                c3 = cos2[:, :].unsqueeze(1).broadcast_to([P, 2, S])
                s3 = sin2[:, :].unsqueeze(1).broadcast_to([P, 2, S])
                V.tensor_tensor(mul2[:, 0, :].rearrange("p (a n) -> p a n", a=2), pv, c3, ALU.mult)
                own.done(V.tensor_tensor(mul2[:, 1, :].rearrange("p (a n) -> p a n", a=2), pv, s3, ALU.mult))
                V.tensor_tensor(dst[:, 2 * j, :], mul2[:, 0, 0:S], mul2[:, 1, S:2 * S], ALU.subtract)
                own.done(V.tensor_tensor(dst[:, 2 * j + 1, :], mul2[:, 0, S:2 * S], mul2[:, 1, 0:S], ALU.add))
                dve.sem_inc(sig.sem, 1)

            def recurrence(l, j):
                f = slice(512 * j, 512 * j + 512)
                own.done(V.scalar_tensor_tensor(a0[:, f], a5[:, f], 1.0, a0[:, f], ALU.add, ALU.mult))
                own.done(V.tensor_tensor(a1[:, f], a0[:, f], a1[:, f], ALU.mult))
                for c in (2 * j, 2 * j + 1):
                    g = slice(S * c, S * c + S)
                    own.done(V.tensor_tensor_scan(a0[:, g], a5[:, g], a1[:, g], 0.0, ALU.mult, ALU.add))
                dve.wait_ge(gelu_ready.sem, gelu_ready.at(l, j + 1))
                own.done(V.tensor_tensor(a0[:, f], a0[:, f], a2[:, f], ALU.mult))
                split(tiles(a0)[:, 2 * j:2 * j + 2, :], h_hi[:, 2 * j:2 * j + 2, :], h_lo[:, 2 * j:2 * j + 2, :], oa_ready.sem)

            def mixer(l):
                own.done(V.memset(xa_pad[:, :, 0:3], 0.0))
                for name, count in STAGES:
                    for j in range(count):
                        n = AT[name] + j
                        m = n - MIX0
                        bank = (2 + j) % 4
                        pair = slice(2 * j, 2 * j + 2)
                        pv = ps[:, bank, :].rearrange("p (a n) -> p a n", a=2)
                        c = m - 5
                        if 0 <= c < KD:
                            dve.wait_ge(lru_acts.sem, lru_acts.at(l, c + 1))
                            V.tensor_tensor(tiles(a1)[:, c, :], tiles(a1)[:, c, :], act2[:, 0, S * (c % 2):S * (c % 2) + S],
                                            ALU.mult).then_inc(gated_x.sem, 1)
                            dve.wait_ge(gated_x.sem, gated_x.at(l, c + 1))
                        if name == "g" and j % 2 == 0:
                            h = j // 2
                            dve.wait_ge(ret_scores.sem, ret_scores.at(l, h + 1))
                            if h >= 2:
                                dve.wait_ge(ret_out.sem, ret_out.at(l, h - 1))
                            V.tensor_tensor(probs[:, h % 2, :], ps[:, 4, 0:384], decay[:, h, :], ALU.mult)\
                             .then_inc(ret_probs.sem, 1)
                        if name in ("g", "sc") and (m - 34) % 2 == 0 and 0 <= (m - 34) // 2 < HEADS:
                            h = (m - 34) // 2
                            dve.wait_ge(ret_turned.sem, ret_turned.at(l, h + 1))
                            dve.wait_ge(g_ready.sem, g_ready.at(l, 2 * h + 2))
                            sg = a2[:, D * (h % 2):D * (h % 2) + D]
                            own.done(V.tensor_tensor(sg, ps[:, 6:8, :].rearrange("p a n -> p (a n)"), sg, ALU.mult))
                            split(sg.rearrange("p (k n) -> p k n", n=S), h_hi[:, 4 * h:4 * h + 4, :],
                                  h_lo[:, 4 * h:4 * h + 4, :], ret_ready.sem)
                        if name == "g" and j % 2 == 1:
                            h = j // 2
                            dve.wait_ge(ret_scale.sem, ret_scale.at(l, h + 1))
                            V.tensor_scalar(mul2[:, 0, :], ps[:, 5, :], ret_rs[:, 0:1], None, ALU.mult)
                            V.tensor_scalar(mul2[:, 1, :], ps[:, 6, :], ret_rs[:, 1:2], None, ALU.mult)\
                             .then_inc(ret_scaled.sem, 1)
                        if n < FFN2 - 1:
                            rest(l, n + 2)
                        if name == "xa":
                            dve.wait_ge(xa_ready.sem, xa_ready.at(l, j + 1))
                            for c in (2 * j, 2 * j + 1):
                                own.done(V.tensor_scalar(tiles(a1)[:, c, :], xa_pad[:, c, 3:3 + S],
                                                         lv[:, c, V_CW + 3:V_CW + 4], lv[:, c, V_CB:V_CB + 1],
                                                         ALU.mult, ALU.add))
                                for tap in (2, 1, 0):
                                    ins = V.scalar_tensor_tensor(tiles(a1)[:, c, :], xa_pad[:, c, tap:tap + S],
                                                                 lv[:, c, V_CW + tap:V_CW + tap + 1], tiles(a1)[:, c, :],
                                                                 ALU.mult, ALU.add)
                                    if tap:
                                        own.done(ins)
                                ins.then_inc(xc_ready.sem, 1)
                        elif name == "q":
                            dve.wait_ge(slot_used.sem, slot_used.at(l, n + 1))
                            rope(l, j, bank, q_t, q_ready)
                        elif name == "k":
                            dve.wait_ge(slot_used.sem, slot_used.at(l, n + 1))
                            rope(l, j, bank, k_t, k_ready)
                        if 13 <= m < 17:
                            if m == 13:
                                dve.wait_ge(roots_ready.sem, roots_ready.at(l, 1))
                            recurrence(l, m - 13)
                        if name == "lru_out":
                            dve.wait_ge(slot_used.sem, slot_used.at(l, n + 1))
                            dve.wait_ge(ga_ready.sem, ga_ready.at(l, j + 1))
                            V.tensor_tensor(tiles(a5)[:, pair, :], pv, tiles(a5)[:, pair, :], ALU.mult)\
                             .then_inc(acc_ready.sem, 1)
                        elif name in V_HALF and j == 3:
                            dve.wait_ge(slot_used.sem, slot_used.at(l, n + 1))
                            V.tensor_copy(v_rows[1][:, D * V_HALF[name]:D * V_HALF[name] + D],
                                          ps[:, 6:8, :].rearrange("p a n -> p (a n)")).then_inc(v_ready1.sem, 1)
                        elif name == "sh":
                            dve.wait_ge(slot_used.sem, slot_used.at(l, n + 1))
                            if j == 0:
                                own.done(V.memset(prod_pad[:, :, 0:2], 0.0))
                            dve.wait_ge(sc_ready.sem, sc_ready.at(l, j + 1))
                            V.tensor_tensor(prod_pad[:, pair, 2:2 + S], pv, tiles(a1)[:, pair, :], ALU.mult)\
                             .then_inc(sh_ready.sem, 1)
                            dve.wait_ge(sh_ready.sem, sh_ready.at(l, j + 1))
                            for c in (2 * j, 2 * j + 1):
                                own.done(V.tensor_scalar(tiles(a1)[:, c, :], prod_pad[:, c, 2:2 + S],
                                                         lv[:, c, V_SW + 2:V_SW + 3], None, ALU.mult))
                                for tap in (1, 0):
                                    own.done(V.scalar_tensor_tensor(
                                        tiles(a1)[:, c, :], prod_pad[:, c, tap:tap + S],
                                        lv[:, c, V_SW + tap:V_SW + tap + 1], tiles(a1)[:, c, :], ALU.mult, ALU.add))
                        elif name == "ret_out" and j % 2 == 1:
                            g = j // 2
                            bb = (2 + 2 * g) % 4
                            dve.wait_ge(slot_used.sem, slot_used.at(l, n + 1))
                            dve.wait_ge(gb_ready.sem, gb_ready.at(l, g + 1))
                            tmp = mul2[:, g % 2, :].rearrange("p (a n) -> p a n", a=2)
                            own.done(V.tensor_tensor(tmp, ps[:, bb:bb + 2, 0:S], tiles(a4)[:, 2 * g:2 * g + 2, :], ALU.mult))
                            V.tensor_tensor(tiles(a5)[:, 2 * g:2 * g + 2, :], tiles(a5)[:, 2 * g:2 * g + 2, :], tmp,
                                            ALU.add).then_inc(ret_added.sem, 1)
                        elif name == "sb":
                            dve.wait_ge(slot_used.sem, slot_used.at(l, n + 1))
                            own.done(V.tensor_tensor(tiles(a1)[:, pair, :], pv, tiles(a1)[:, pair, :], ALU.mult))
                            split(tiles(a1)[:, pair, :], h_hi[:, pair, :], h_lo[:, pair, :], oc_ready.sem)
                        elif name == "sc_out":
                            dve.wait_ge(slot_used.sem, slot_used.at(l, n + 1))
                            dve.wait_ge(gc_ready.sem, gc_ready.at(l, j + 1))
                            tmp = mul2[:, j % 2, :].rearrange("p (a n) -> p a n", a=2)
                            own.done(V.tensor_tensor(tmp, pv, tiles(a4)[:, pair, :], ALU.mult))
                            own.done(V.tensor_tensor(tmp, tmp, tiles(a5)[:, pair, :], ALU.add))
                            split(tmp, u_hi[:, pair, :], u_lo[:, pair, :], mix_ready.sem)
                post(l, 1, FFN2)

            TWO_PI = 2 * np.pi
            C1 = 6.28125
            C2 = float(np.float32(np.round((TWO_PI - C1) * 2 ** 21) / 2 ** 21))
            C3 = float(np.float32(TWO_PI - C1 - C2))
            MAGIC = 1.5 * 2 ** 23
            PI_IN = float(np.nextafter(np.float32(np.pi), np.float32(0)))
            dve.wait_ge(pos_loaded, 32)
            ang, turns = a1[:, 0:S], a1[:, S:2 * S]
            own.done(V.tensor_copy(ang, a0[:, 0:S].bitcast(I32)))
            own.done(V.tensor_scalar(ang, ang, inv_freq[:, 0:1], None, ALU.mult))
            for dst, shift in ((sin2, 0.0), (cos2, 0.25)):
                own.done(V.tensor_scalar(turns, ang, 1.0 / TWO_PI, shift, ALU.mult, ALU.add))
                own.done(V.tensor_scalar(turns, turns, MAGIC, None, ALU.add))
                own.done(V.tensor_scalar(turns, turns, MAGIC, None, ALU.subtract))
                own.done(V.scalar_tensor_tensor(dst[:, :], turns, -C1, ang, ALU.mult, ALU.add))
                own.done(V.scalar_tensor_tensor(dst[:, :], turns, -C2, dst[:, :], ALU.mult, ALU.add))
                own.done(V.scalar_tensor_tensor(dst[:, :], turns, -C3, dst[:, :], ALU.mult, ALU.add))
                if shift:
                    own.done(V.tensor_scalar(dst[:, :], dst[:, :], float(np.pi / 2), None, ALU.add))
                own.done(V.tensor_scalar(dst[:, :], dst[:, :], PI_IN, -PI_IN, ALU.min, ALU.max))
            dve.sem_inc(angles, 1)
            rest(0, 0)
            dve.wait_ge(vec_turned, 1)
            own.done(V.tensor_copy(vec[:, :, :].rearrange("p k v -> p (k v)"), ps[:, 4, 0:KD * NVEC]))
            lam = vec[:, :, V_LAM:V_LAM + NV + 1:NV]
            lam3, z, w, w2, s = (soft[:, i, :].rearrange("p (k l) -> p k l", l=DEPTH) for i in range(5))
            own.done(V.tensor_scalar(lam3, lam, -1.0, None, ALU.mult))
            own.done(V.tensor_tensor(z, lam, lam3, ALU.max))
            dve.sem_inc(lam_ready, 1)
            dve.wait_ge(lam_exp, 1)
            own.done(V.tensor_scalar(w, z, 2.0, None, ALU.add))
            own.done(V.reciprocal(w, w))
            own.done(V.tensor_tensor(w, w, z, ALU.mult))
            own.done(V.tensor_tensor(w2, w, w, ALU.mult))
            own.done(V.tensor_scalar(s, w2, 1.0 / 17, None, ALU.mult))
            for odd in (15, 13, 11, 9, 7, 5, 3):
                own.done(V.scalar_tensor_tensor(s, s, 1.0 / odd, w2, ALU.add, ALU.mult))
            own.done(V.scalar_tensor_tensor(s, s, 1.0, w, ALU.add, ALU.mult))
            own.done(V.tensor_scalar(lam3, lam3, 0.0, 4.0, ALU.max, ALU.mult))
            own.done(V.scalar_tensor_tensor(rates[:, :, 0:2 * DEPTH:2], s, 8.0, lam3, ALU.mult, ALU.add))
            own.done(V.tensor_scalar(rates[:, :, 1:2 * DEPTH:2], rates[:, :, 0:2 * DEPTH:2], -2.0, None, ALU.mult))
            dve.sem_inc(ret_ready.sem, ret_ready.primed)
            dve.sem_inc(mul_ready.sem, mul_ready.primed)
            dve.sem_inc(act_ready.sem, act_ready.primed)
            dve.sem_inc(gated_x.sem, gated_x.primed)
            dve.wait_ge(x_loaded, 16)
            dve.sem_inc(x_ready.sem, x_ready.primed)
            dve.wait_ge(sines, 2)
            own.restart()
            with dve.Fori(0, DEPTH) as l:
                V.tensor_copy(lrates[:, :, :], rates[:, :, ds(l * 2, 2)])
                V.tensor_copy(lv[:, :, :], vec[:, :, ds(l * NV, NV)]).then_inc(lv_ready.sem, 1)
                dve.wait_ge(lv_ready.sem, lv_ready.at(l, 1))
                pre(l, 0, lv, V_G1, 0)
                feed_forward(l, 0, 0)
                pre(l, 1, lv, V_GM, MIX0)
                mixer(l)
                pre(l, 2, lv, V_G2, FFN2)
                feed_forward(l, 1, FFN2)
                own.restart()

            l = DEPTH
            dve.wait_ge(rel_done, 1)
            V.tensor_tensor(rel, ps[0:NHEAD, 1, 0:REL], allowed, ALU.add).then_inc(rel_ready, 1)
            pre(l, 0, vec, V2_GMIX, B_IN)
            for j in range(9):
                rest(l, j + 2)
            dve.wait_ge(b["v_turned"], 1)
            V.tensor_copy(a0[:, 512:640], ps[:, 6, 0:128]).then_inc(b["v_rows_b"], 1)
            V.tensor_copy(a0[:, 1152:1280], ps[:, 6, 128:256]).then_inc(b["v_rows_b"], 1)
            dve.wait_ge(b["sink_loaded"], 16)
            for h in range(NHEAD):
                band = (a1 if h % 10 < 5 else a2)
                s0 = (h % 5) * BIASW
                dve.wait_ge(b["scored"], h + 1)
                dve.wait_ge(b["bias_loaded0" if h % 2 == 0 else "bias_loaded1"], 16 * (h // 2 + 1))
                if h >= 2:
                    dve.wait_ge(b["turned"], h - 1)
                for tt in range(TT):
                    o = s0 + P * tt + S - 1
                    bias = band[:, o:o - S if o >= S else None:-1]
                    ins = V.scalar_tensor_tensor(act2[:, h % 2, S * tt:S * tt + S], ps[:, h % 2, S * tt:S * tt + S], 0.125,
                                                 bias, ALU.mult, ALU.add)
                ins.then_inc(b["logits"], 1)
                dve.wait_ge(b["logits"], h + 1)
                c = 4 * (h % 2)
                own.done(V.tensor_reduce(small[:, 24 + c:26 + c], act2[:, h % 2, :].rearrange("p (t n) -> p t n", t=2),
                                         AX_X, ALU.max))
                if h < 8:
                    own.done(V.tensor_scalar(small[:, 24 + c:26 + c], small[:, 24 + c:26 + c], sink[:, h:h + 1], -1.0,
                                             ALU.max, ALU.mult))
                else:
                    own.done(V.tensor_scalar(small[:, 24 + c:26 + c], small[:, 24 + c:26 + c], -1.0, None, ALU.mult))
                dve.sem_inc(b["row_max"], 1)
            dve.wait_ge(b["exps"], 2 * NHEAD + 16)
            own.done(V.tensor_tensor(probs[:, 0, 0:16], probs[:, 0, 0:16], probs[:, 1, 0:16], ALU.add))
            own.done(V.reciprocal(probs[:, 0, 0:32], probs[:, 0, 0:32]))
            dve.wait_ge(b["attended"], NHEAD)
            for tt in range(TT):
                for kind in range(2):
                    r = probs[:, 0, 16 * kind + tt:16 * kind + tt + 15:2].unsqueeze(2).broadcast_to([P, 8, 64])
                    o = a1[:, D * tt + 512 * kind:D * tt + 512 * kind + 512]
                    V.tensor_tensor(o.rearrange("p (h e) -> p h e", e=64),
                                    ps[:, 4 + 2 * tt + kind, :].rearrange("p (h e) -> p h e", e=64), r, ALU.mult)\
                     .then_inc(b["attn_rows"], 1)
            dve.wait_ge(b["attn_scale"], 1)
            for tt in range(TT):
                for kind in range(2):
                    ins = V.tensor_scalar(scaled[:, tt, 512 * kind:512 * kind + 512],
                                          a1[:, D * tt + 512 * kind:D * tt + 512 * kind + 512],
                                          pre_rs[:, 2 * tt + kind:2 * tt + kind + 1], None, ALU.mult)
                ins.then_inc(b["den_ready"], 1)
            u_rests(l, 1, vec, V2_GOUT)
            for j in range(B_O, B_UP - 1):
                rest(l, j + 2)
            post(l, 0, B_UP)
            pre(l, 1, vec, V2_GMLP, B_UP, t=2)
            for part in range(2):
                for j in range(16):
                    n = (B_UP if part == 0 else B_UP2) + j
                    if n < B_GATE - 1:
                        rest(l, n + 2)
                    if j < 8:
                        p = 8 * part + j
                        dve.wait_ge(b["relu_ready"], p + 1)
                        V.tensor_tensor(mul2[:, p % 2, :], act2[:, p % 2, :], act2[:, p % 2, :], ALU.mult)\
                         .then_inc(b["sq_ready"], 1)
                        dve.wait_ge(b["sq_ready"], p + 1)
                        split(mul2[:, p % 2, :].rearrange("p (a n) -> p a n", a=2), h_hi[:, 2 * j:2 * j + 2, :],
                              h_lo[:, 2 * j:2 * j + 2, :], b["hid_ready"])
            post(l, 1, B_GATE)
            for k in range(KD):
                dve.wait_ge(u_head.sem, u_head.at(l, KD * 3 + (k | 1) + 1))
                V.tensor_tensor(u_lo[:, k, :], turned(l, 3, k), u_hi[:, k, :], ALU.subtract)\
                 .then_inc(u_ready.sem, 1)
            dve.wait_ge(b["p_head"], 1)
            V.tensor_tensor(h_lo[:, 0:2, :], ps[:, 4, :].rearrange("p (a n) -> p a n", a=2), h_hi[:, 0:2, :],
                            ALU.subtract).then_inc(b["p_ready"], 1)
            for n in range(B_GATE - 1, B_SLOTS - 2):
                rest(l, n + 2)
            dve.wait_ge(slot_used.sem, slot_used.at(l, B_GATE + 4))
            dve.wait_ge(b["brow_loaded"], 16)
            for tt in range(TT):
                V.tensor_tensor(a3[:, D * tt:D * tt + D], ps[:, 4 + 2 * tt:6 + 2 * tt, :].rearrange("p a n -> p (a n)"),
                                a2[:, 0:D], ALU.add).then_inc(b["gate_in"], 1)
            dve.wait_ge(slot_used.sem, slot_used.at(l, B_SLOTS))
            for tt in range(TT):
                dve.wait_ge(b["gate_ready"], tt + 1)
                V.tensor_tensor(a3[:, D * tt:D * tt + D], ps[:, 2 * tt:2 * tt + 2, :].rearrange("p a n -> p (a n)"),
                                a3[:, D * tt:D * tt + D], ALU.mult).then_inc(b["gated"], 1)
            dve.wait_ge(gain_loaded.sem, gain_loaded.at(l, 48))
            for tt in range(TT):
                dve.wait_ge(b["ple_scale"], tt + 1)
                own.done(V.scalar_tensor_tensor(a4[:, D * tt:D * tt + D], a3[:, D * tt:D * tt + D], post_rs[:, tt:tt + 1],
                                                gain_row[:, :], ALU.mult, ALU.mult))
                V.tensor_tensor(x[:, tt, :], x[:, tt, :], a4[:, D * tt:D * tt + D], ALU.add).then_inc(b["out_ready"], 1)

        @block.tensor
        def _(pe):
            M = nc.tensor.matmul

            def column_slot(l, n, dst, act_hi, act_lo, k0=0, first=True, last=True, it=0, u_from=None):
                pe.wait_ge(split_done.sem, split_done.at(l, n + 1) + it * 4)
                hi, lo = col_view(w_hi, n % SPLIT), col_view(w_lo, n % SPLIT)
                for a in range(2):
                    for k in range(KD):
                        if a == 0 and u_from is not None:
                            pe.wait_ge(u_ready.sem, u_ready.at(l, u_from + max(k, 1) + 1))
                        c = slice(P * a, P * a + P)
                        M(dst[a], hi[:, k, c], act_hi[:, k0 + k, :], start=first and k == 0, stop=False)
                        M(dst[a], hi[:, k, c], act_lo[:, k0 + k, :], start=False, stop=False)
                        ins = M(dst[a], lo[:, k, c], act_hi[:, k0 + k, :], start=False, stop=last and k == KD - 1)
                ins.then_inc(slot_used.sem, 1)

            def row_slot(l, n, ks, act_hi, act_lo, first, last, bank0=4):
                pe.wait_ge(split_done.sem, split_done.at(l, n + 1))
                hi, lo = row_view(w_hi, n % SPLIT), row_view(w_lo, n % SPLIT)
                for i, k in enumerate(ks):
                    for tt in range(TT):
                        tok = slice(P * tt, P * tt + P)
                        f, e = first and i == 0, last and i == len(ks) - 1
                        for a, (stat, mov) in enumerate(((act_hi, hi), (act_hi, lo), (act_lo, hi))):
                            for half in range(2):
                                ins = M(ps[:, bank0 + 2 * tt + half, :], stat[:, k, tok],
                                        mov[:, i, 512 * half:512 * half + 512], start=f and a == 0, stop=e and a == 2)
                ins.then_inc(slot_used.sem, 1)

            def last_rows(l, i, n, ks, act_hi, act_lo):
                pe.wait_ge(split_done.sem, split_done.at(l, n + 1))
                hi, lo = row_view(w_hi, n % SPLIT), row_view(w_lo, n % SPLIT)
                for tt in range(TT):
                    tok = slice(P * tt, P * tt + P)
                    for r, k in enumerate(ks):
                        for a, (stat, mov) in enumerate(((act_hi, hi), (act_hi, lo), (act_lo, hi))):
                            for half in range(2):
                                ins = M(ps[:, 4 + 2 * tt + half, :], stat[:, k, tok],
                                        mov[:, r, 512 * half:512 * half + 512], start=False,
                                        stop=k == ks[-1] and a == 2)
                    ins.then_inc(rows_done.sem if tt == 0 else slot_used.sem, 1)

            def bank(i):
                return [ps[:, i, 0:S], ps[:, i, S:2 * S]]

            def turn(l, i, src, sig, count):
                for tt in range(TT):
                    for k in range(KD):
                        if k % 4 == 0:
                            pe.wait_ge(sig, count(2 * tt + k // 4))
                        ins = nc.tensor.transpose(turned(l, i, k)[:, P * tt:P * tt + P], src[:, tt, P * k:P * k + P], ident[:, :])
                        if tt == TT - 1:
                            ins.then_inc(u_turned.sem, 1)

            def pre(l, i):
                turn(l, i, scaled, pre_scaled.sem, lambda q: pre_scaled.at(l, 4 * i + q + 1))

            def pair_slots(l, which, base, p, it=0):
                pair = FFN_PAIRS * which + p
                n = base + (2 * p if p < FIRST_PAIRS else FFN_IN2 + 2 * (p - FIRST_PAIRS))
                bk = (2 * which + 2 * p) % 4
                norm = 2 * which
                pe.wait_ge(act_ready.sem, act_ready.at(l, pair - 1) + it * 2)
                column_slot(l, n, bank(bk), u_hi, u_lo, it=it, u_from=KD * norm if p == 0 else None)
                pe.wait_ge(mul_ready.sem, mul_ready.at(l, pair - 1) + it * 2)
                column_slot(l, n + 1, bank(bk + 1), u_hi, u_lo, it=it)

            def feed_forward(l, which, base):
                with pe.Fori(0, FIRST_PAIRS // 2) as it:
                    for p in range(2):
                        pair_slots(l, which, base, p, it)
                for p in range(FIRST_PAIRS):
                    pe.wait_ge(h_ready.sem, h_ready.at(l, FFN_PAIRS * which + p + 1))
                    row_slot(l, base + 2 * FIRST_PAIRS + p, (2 * p, 2 * p + 1), h_hi, h_lo, p == 0, False)
                for p in range(FIRST_PAIRS, FFN_PAIRS):
                    pair_slots(l, which, base, p)
                for p in range(FIRST_PAIRS, FFN_PAIRS):
                    k = 2 * (p - FIRST_PAIRS)
                    pe.wait_ge(h_ready.sem, h_ready.at(l, FFN_PAIRS * which + p + 1))
                    n = base + FFN_OUT2 + 1 + p - FIRST_PAIRS
                    if p == FIRST_PAIRS:
                        row_slot(l, n - 1, (k,), h_hi, h_lo, False, False)
                        row_slot(l, n, (k + 1,), h_hi, h_lo, False, False)
                    elif p < FFN_PAIRS - 1:
                        row_slot(l, n, (k, k + 1), h_hi, h_lo, False, False)
                    else:
                        last_rows(l, 2 * which, n, (k, k + 1), h_hi, h_lo)

            def lru_gate(l, c):
                pe.wait_ge(xc_ready.sem, xc_ready.at(l, c + 1))
                pe.wait_ge(lru_w_loaded.sem, lru_w_loaded.at(l, 64))
                if c >= 4:
                    pe.wait_ge(lru_acts.sem, lru_acts.at(l, c - 3))
                for m in range(2):
                    ins = M(ps[:, 4 + c % 4, S * m:S * m + S], lru_w[:, m, c, :], tiles(a1)[:, c, :], start=True, stop=True)
                ins.then_inc(lru_gates.sem, 1)

            def scores(l, h):
                if h == 0:
                    pe.wait_ge(v_ready0.sem, v_ready0.at(l, 2))
                    pe.wait_ge(v_ready1.sem, v_ready1.at(l, 2))
                    pe.wait_ge(q_ready.sem, q_ready.at(l, 4))
                    pe.wait_ge(k_ready.sem, k_ready.at(l, 4))
                else:
                    pe.wait_ge(ret_probs.sem, ret_probs.at(l, h))
                for c in range(2):
                    M(ps[:, 4, 0:S], k_t[:, 2 * h + c, 0:P], q_t[:, 2 * h + c, :], start=c == 0, stop=c == 1)
                for c in range(2):
                    ins = M(ps[:, 4, S:S + P], k_t[:, 2 * h + c, P:S], q_t[:, 2 * h + c, P:S], start=c == 0, stop=c == 1)
                ins.then_inc(ret_scores.sem, 1)

            def attend(l, h):
                pe.wait_ge(ret_probs.sem, ret_probs.at(l, h + 1))
                if h >= 1:
                    pe.wait_ge(ret_ready.sem, ret_ready.at(l, h))
                pr, vs = probs[:, h % 2, :], slice(HV * h, HV * h + HV)
                M(ps[:, 5, :], pr[:, 0:P], v_rows[0][:, vs], start=True, stop=True)
                M(ps[:, 6, :], pr[:, P:S], v_rows[0][:, vs], start=True, stop=False)
                M(ps[:, 6, :], pr[:, S:S + P], v_rows[1][:, vs], start=False, stop=True).then_inc(ret_out.sem, 1)

            def turn_head(l, h):
                pe.wait_ge(ret_scaled.sem, ret_scaled.at(l, h + 1))
                for e in range(4):
                    for tt in range(TT):
                        o = S * (e % 2) + P * tt
                        ins = nc.tensor.transpose(ps[:, 6 + e // 2, o:o + P], mul2[:, tt, P * e:P * e + P], ident[:, :])
                ins.then_inc(ret_turned.sem, 1)

            EMPTIED = {"xa": xa_ready, "q": q_ready, "k": k_ready, "ya": gelu_ready, "ga": ga_ready, "lru_out": acc_ready,
                       "g": g_ready, "sc": sc_ready, "sh": sh_ready, "gb": gb_ready, "ret_out": ret_added,
                       "sb": oc_ready, "gc": gc_ready}
            BEFORE = {"q": "xa", "k": "q", "ya": "k", "ga": "ya", "lru_out": "ga", "g": "lru_out", "sc": "g",
                      "sh": "sc", "gb": "sh", "ret_out": "gb", "sb": "ret_out", "gc": "sb", "sc_out": "gc"}

            def mixer(l):
                for name, count in STAGES:
                    for j in range(count):
                        n = AT[name] + j
                        m = n - MIX0
                        if 0 <= m - 5 < KD:
                            lru_gate(l, m - 5)
                        if name == "g":
                            (scores if j % 2 == 0 else attend)(l, j // 2)
                        if name in V_HALF:
                            if name == "v0" and j == 0:
                                pe.wait_ge(lru_acts.sem, lru_acts.at(l, KD))
                            if name == "v1" and j == 0:
                                pe.wait_ge(v_ready0.sem, v_ready0.at(l, 1))
                                pe.wait_ge(v_ready1.sem, v_ready1.at(l, 1))
                            row_slot(l, n, (2 * j, 2 * j + 1), u_hi, u_lo, j == 0, j == 3)
                            continue
                        if name == "mix_out":
                            pe.wait_ge(mix_ready.sem, mix_ready.at(l, j + 1))
                            if j == 0:
                                pe.wait_ge(ret_ready.sem, ret_ready.at(l, HEADS))
                            if j < 3:
                                row_slot(l, n, (2 * j, 2 * j + 1), u_hi, u_lo, j == 0, False)
                            else:
                                last_rows(l, 1, n, (6, 7), u_hi, u_lo)
                            continue
                        if name == "ret_out":
                            g = j // 2
                            if j % 2 == 0:
                                if g < 2:
                                    pe.wait_ge(gb_ready.sem, gb_ready.at(l, 2 * g + 2))
                                else:
                                    pe.wait_ge(ret_added.sem, ret_added.at(l, g - 1))
                            if j == 0:
                                pe.wait_ge(ret_ready.sem, ret_ready.at(l, HEADS))
                            bb = (2 + 2 * g) % 4
                            column_slot(l, n, [ps[:, bb, 0:S], ps[:, bb + 1, 0:S]], h_hi, h_lo, KD * (j % 2),
                                        j % 2 == 0, j % 2 == 1)
                            continue
                        if name == "sb":
                            pe.wait_ge(ret_added.sem, ret_added.at(l, 3 + j // 2))
                        elif name == "g" and j >= 4:
                            pe.wait_ge(g_ready.sem, g_ready.at(l, j - 3))
                        elif name == "sc":
                            pe.wait_ge(g_ready.sem, g_ready.at(l, j + 5))
                        elif name != "xa":
                            before = EMPTIED[BEFORE[name]]
                            pe.wait_ge(before.sem, before.at(l, j + 1))
                        ah, al = u_hi, u_lo
                        if name == "lru_out":
                            ah, al = h_hi, h_lo
                            pe.wait_ge(oa_ready.sem, oa_ready.at(l, 4))
                        if name == "sc_out":
                            ah, al = h_hi, h_lo
                            pe.wait_ge(oc_ready.sem, oc_ready.at(l, 4))
                        column_slot(l, n, bank((2 + j) % 4), ah, al, u_from=KD if name == "xa" and j == 0 else None)
                        if name == "g" and j % 2 == 1:
                            turn_head(l, j // 2)

            pe.wait_ge(ident_ready, 1)
            pe.wait_ge(vec_loaded, 16 * (7 + 2 * DEPTH + 4))
            for k in range(KD):
                ins = nc.tensor.transpose(ps[:, 4, NVEC * k:NVEC * k + NVEC], rows[0:NVEC, P * k:P * k + P],
                                          ident[0:NVEC, 0:NVEC])
            ins.then_inc(vec_turned, 1)
            with pe.Fori(0, DEPTH) as l:
                pre(l, 0)
                feed_forward(l, 0, 0)
                pre(l, 1)
                mixer(l)
                pre(l, 2)
                feed_forward(l, 1, FFN2)

            l = DEPTH
            pe.wait_ge(consts_loaded, 64)
            M(ps[0:NHEAD, 1, 0:REL], table, onehot, start=True, stop=True).then_inc(rel_done, 1)
            pe.wait_ge(rel_ready, 1)
            pre(l, 0)
            for j in range(9):
                if j >= 4:
                    pe.wait_ge(b["proj_ready"], j - 3)
                column_slot(l, j, bank(j % 4), u_hi, u_lo, u_from=0 if j == 0 else None)
            pe.wait_ge(b["proj_ready"], 9)
            for tt in range(TT):
                for c in range(4):
                    nc.tensor.transpose(ps[:, 4 + tt, P * c:P * c + P], a5[:, S * c + P * tt:S * c + P * tt + P], ident[:, :])
            for tt in range(TT):
                ins = nc.tensor.transpose(ps[:, 6, P * tt:P * tt + P], a4[:, S + P * tt:S + P * tt + P], ident[:, :])
            ins.then_inc(b["v_turned"], 1)
            pe.wait_ge(b["ka_swapped"], 32)
            pe.wait_ge(b["v_rows_a"], 2)
            pe.wait_ge(b["v_rows_b"], 2)

            def logits(h):
                part = slice(64 * (h % 2), 64 * (h % 2) + 64)
                if h < 8:
                    q_off = S * (h // 2)
                    k_off = 0 if h // 4 == h % 2 else 1536
                else:
                    q_off = 1024 + S * ((h - 8) // 2)
                    k_off = 512 + S * ((h - 8) // 2)
                if h >= 2:
                    pe.wait_ge(b["logits"], h - 1)
                for tt in range(TT):
                    ins = M(ps[:, h % 2, S * tt:S * tt + S], a3[part, q_off + P * tt:q_off + P * tt + P],
                            a4[part, k_off:k_off + S], start=True, stop=True)
                ins.then_inc(b["scored"], 1)

            def turn_exps(h):
                pe.wait_ge(b["exps"], 4 * (h + 1) if h < 8 else 32 + 2 * (h - 7))
                if h >= 2:
                    pe.wait_ge(b["exps_t"], h - 1)
                for kt in range(2):
                    for tt in range(TT):
                        ins = nc.tensor.transpose(ps[:, 2 + h % 2, S * kt + P * tt:S * kt + P * tt + P],
                                                  act2[:, h % 2, S * tt + P * kt:S * tt + P * kt + P], ident[:, :])
                ins.then_inc(b["turned"], 1)

            def weigh(h):
                pe.wait_ge(b["exps_t"], h + 1)
                kind = h // 8
                v_off = 512 + 64 * (h // 4) if kind == 0 else 64 * (h - 8)
                for tt in range(TT):
                    for kt in range(2):
                        ins = M(ps[:, 4 + 2 * tt + kind, 64 * (h % 8):64 * (h % 8) + 64],
                                mul2[:, h % 2, S * kt + P * tt:S * kt + P * tt + P],
                                a0[:, 640 * kt + v_off:640 * kt + v_off + 64], start=kt == 0, stop=kt == 1)
                ins.then_inc(b["attended"], 1)

            for h in range(NHEAD + 2):
                if h < NHEAD:
                    logits(h)
                if 1 <= h <= NHEAD:
                    turn_exps(h - 1)
                if h >= 2:
                    weigh(h - 2)
            turn(l, 1, scaled, b["den_ready"], lambda q: q // 2 + 1)
            for j in range(4):
                for k in (2 * j, 2 * j + 1):
                    pe.wait_ge(u_ready.sem, u_ready.at(l, KD + k + 1))
                if j < 3:
                    row_slot(l, B_O + j, (2 * j, 2 * j + 1), u_hi, u_lo, j == 0, False)
                else:
                    last_rows(l, 0, B_O + 3, (6, 7), u_hi, u_lo)
            turn(l, 2, scaled, pre_scaled.sem, lambda q: pre_scaled.at(l, 4 + q + 1))
            for part in range(2):
                for j in range(8):
                    p = 8 * part + j
                    if p >= 4:
                        pe.wait_ge(b["relu_ready"], p - 3)
                    column_slot(l, (B_UP if part == 0 else B_UP2) + j, bank((9 + p) % 4), u_hi, u_lo,
                                u_from=2 * KD if p == 0 else None)
                for j in range(8):
                    pe.wait_ge(b["hid_ready"], 8 * part + j + 1)
                    if part == 0 or j < 7:
                        row_slot(l, (B_DN if part == 0 else B_DN2) + j, (2 * j, 2 * j + 1), h_hi, h_lo,
                                 part == 0 and j == 0, False)
                    else:
                        last_rows(l, 1, B_DN2 + 7, (14, 15), h_hi, h_lo)
            turn(l, 3, x, x_ready.sem, lambda q: x_ready.at(l, 4 + q + 1))
            pe.wait_ge(b["p_loaded"], 16)
            for c in range(2):
                for tt in range(TT):
                    ins = nc.tensor.transpose(ps[:, 4, S * c + P * tt:S * c + P * tt + P],
                                              a1[:, S * tt + P * c:S * tt + P * c + P], ident[:, :])
            ins.then_inc(b["p_turned"], 1)
            pe.wait_ge(b["p_ready"], 1)
            for j in range(4):
                for k in (2 * j, 2 * j + 1):
                    pe.wait_ge(u_ready.sem, u_ready.at(l, 3 * KD + k + 1))
                row_slot(l, B_GATE + j, (2 * j, 2 * j + 1), u_hi, u_lo, j == 0, j == 3)
            row_slot(l, B_PLE, (0, 1), h_hi, h_lo, True, True, bank0=0)


_INS = ["x", "positions", "ffn1_pre_g", "ffn1_w_in", "ffn1_w_out", "ffn1_post_g", "mix_pre_g", "w_mix_in",
        "lru_conv_w", "lru_conv_b", "lru_w_a", "lru_b_a", "lru_w_x", "lru_b_x", "lru_lambda", "w_lru_out",
        "w_ret_out", "sc_conv_w", "w_sc_out", "w_mix_out", "mix_post_g", "ffn2_pre_g", "ffn2_w_in", "ffn2_w_out",
        "ffn2_post_g", "p_2", "rel_bias_table_2", "g_pre_mix_2", "w_in_2", "sink_a_2", "g_out_a_2", "g_out_b_2",
        "w_o_2", "g_post_mix_2", "g_pre_mlp_2", "w_up_2", "w_down_2", "g_post_mlp_2", "w_ple_proj_2",
        "w_ple_gate_2", "b_ple_gate_2", "g_post_ple_2"]


def kernel(**inputs):
    import concourse.bacc as _bacc
    from concourse.bass_utils import run_bass_kernel_spmd as _run

    nc = _bacc.Bacc("TRN2", target_bir_lowering=False, num_devices=1)
    arrays, args = {}, {}

    def declare(name, a):
        arrays[f"in_{name}_dram"] = a
        args[name] = nc.dram_tensor(f"in_{name}_dram", a.shape, mybir.dt.from_np(a.dtype), kind="ExternalInput").ap()

    for name in _INS:
        declare(name, np.ascontiguousarray(inputs[name]))
    for name, a in constants().items():
        declare(name, a)
    out = nc.dram_tensor("out_0_dram", (1, S, D), F32, kind="ExternalOutput").ap()
    scratch = nc.dram_tensor("rel_scratch_dram", (NHEAD, 512), F32).ap()
    build(nc, args, out, scratch)
    r = _run(nc, [arrays], core_ids=[0])
    return r.results[0]["out_0_dram"]
```

```python
from contextlib import ExitStack

import numpy as np
import concourse.bass as bass
from concourse import mybir

F32 = mybir.dt.float32
F32R = mybir.dt.float32r
I32 = mybir.dt.int32
ALU = mybir.AluOpType
ACT = mybir.ActivationFunctionType
AX_X = mybir.AxisListType.X
ds = bass.ds

P = 128
S = 256
D = 1024
DEPTH = 2
EPS = 1e-6
CHUNK = 64
HEADS = 4
HV = 512
D_FF = 2816
TT = S // P
KD = D // P
SLOTC = 256

FFN_PAIRS = D_FF // SLOTC
FIRST_PAIRS = 8
LAST_PAIRS = FFN_PAIRS - FIRST_PAIRS
FFN_IN2 = 3 * FIRST_PAIRS
FFN_OUT2 = FFN_IN2 + 2 * LAST_PAIRS
FFN_SLOTS = FFN_OUT2 + LAST_PAIRS + 1
MIX0 = FFN_SLOTS
STAGES = [("xa", 4), ("q", 4), ("k", 4), ("ya", 4), ("v0", 4), ("ga", 4), ("v1", 4), ("lru_out", 4), ("g", 8),
          ("sc", 4), ("sh", 4), ("gb", 4), ("ret_out", 8), ("sb", 4), ("gc", 4), ("sc_out", 4),
          ("mix_out", 4)]
GATE0, REC0 = 5, 15
V_HALF = {"v0": 0, "v1": 1}
AT = {}
for _name, _n in STAGES:
    AT[_name] = MIX0 + sum(n for m, n in STAGES[:len(AT)])
FFN2 = MIX0 + sum(n for _, n in STAGES)
SLOTS = FFN2 + FFN_SLOTS
RAW, SPLIT = 4, 2
WARM = 24
WARM_HEAD = 3
assert SLOTS % RAW == 0 and SLOTS % SPLIT == 0 and SPLIT == 2

MC = {"xa": 0, "ya": 1024, "q": 2048, "k": 3072, "v": 4096, "g": 6144, "sb": 8192, "sc": 9216,
      "sh": 10240, "ga": 11264, "gb": 12288, "gc": 13312}

V_G1, V_GM, V_CW, V_CB, V_BA, V_BX, V_LAM, V_SW, V_G2, NV = 0, 1, 2, 6, 7, 8, 9, 10, 13, 14
V2_GMIX, V2_GOUT, V2_GMLP = DEPTH * NV, DEPTH * NV + 1, DEPTH * NV + 2
NVEC = DEPTH * NV + 3

B_IN, B_O, B_UP, B_DN, B_UP2, B_DN2, B_GATE, B_SLOTS = 0, 9, 13, 21, 29, 37, 46, 50
B_PLE = B_DN2 + 6
NHEAD = 16
BIASW = 384
REL = 2 * S - 1


class Signal:

    def __init__(self, sem, per, primed=0):
        self.sem, self.per, self.primed = sem, per, primed

    def at(self, l, k):
        return l * self.per + (self.primed + k)


class Chain:

    def __init__(self, eng, sem):
        self.eng, self.sem, self.n = eng, sem, 0

    def done(self, ins):
        ins.then_inc(self.sem, 1)
        self.n += 1
        self.eng.wait_ge(self.sem, self.n)

    def restart(self):
        if self.n:
            self.eng.sem_clear(self.sem)
            self.n = 0


def constants():
    half = 128
    inv_freq = (10000.0 ** (-np.arange(half, dtype=np.float64) / half)).astype(np.float32)[:, None]
    log_g = np.log1p(-(2.0 ** (-5.0 - np.arange(HEADS))))
    i, j = np.arange(S)[None, :], np.arange(S)[:, None]
    seen = (j // CHUNK) <= (i // CHUNK)
    full = np.exp(log_g[:, None, None] * np.abs(i - j)) * seen / 16.0
    decay = np.concatenate([full[:, :P, :], full[:, P:, P:]], axis=2).transpose(1, 0, 2)
    d = np.arange(S - 1, -S, -1)
    n = np.abs(d)
    large = 8 + (np.log(np.maximum(n, 1).astype(np.float32) / np.float32(8)) / np.float32(np.log(1024 / 8))
                 * np.float32(8)).astype(np.int32)
    bucket = np.where(d > 0, 16, 0) + np.where(n < 8, n, np.minimum(large, 15))
    onehot = (np.arange(32)[:, None] == bucket[None, :]).astype(np.float32)
    times = (n <= 64).astype(int) + (d % 4 == 0) * (n <= 256) + (d % 16 == 0)
    seen_b = np.where(times > 0, np.log(np.maximum(times, 1)), -1e30)
    seen_a = np.where(n <= 128, 0.0, -1e30)
    allowed = np.concatenate([np.tile(seen_a, (8, 1)), np.tile(seen_b, (8, 1))]).astype(np.float32)
    return {"inv_freq": inv_freq, "decay": np.ascontiguousarray(decay.reshape(P, -1)).astype(np.float32),
            "onehot": onehot, "allowed": allowed}


def build(nc, t, out, scratch):
    ctx = ExitStack()
    with ctx:
        def sb(name, shape, dt=F32):
            return ctx.enter_context(nc.sbuf_tensor(name, shape, dt))

        def sem(name):
            return ctx.enter_context(nc.semaphore(name))

        def signal(name, per, primed=0):
            return Signal(sem(name), per, primed)

        x = sb("x", [P, TT, D])
        raw = [sb(f"raw{i}", [P, 2048]) for i in range(RAW)]
        w_hi = [sb(f"w_hi{i}", [P, 2048], F32R) for i in range(SPLIT)]
        w_lo = [sb(f"w_lo{i}", [P, 2048], F32R) for i in range(SPLIT)]
        u_hi = sb("u_hi", [P, KD, S], F32R)
        u_lo = sb("u_lo", [P, KD, S], F32R)
        h_hi = sb("h_hi", [P, 16, S], F32R)
        h_lo = sb("h_lo", [P, 16, S], F32R)
        a0 = sb("a0", [P, 8 * (S + 3)])
        a1, a2, a3, a4, a5 = (sb(f"a{i}", [P, 2048]) for i in range(1, 6))
        act2 = sb("act2", [P, 2, 512])
        mul2 = sb("mul2", [P, 2, 512])
        probs = sb("probs", [P, 2, 384])
        gain_row = sb("gain_row", [P, D])
        decay = sb("decay", [P, HEADS, 384])
        cos2 = sb("cos2", [P, S])
        sin2 = sb("sin2", [P, S])
        ident = sb("ident", [P, P])
        rows = sb("rows", [32, D])
        bias_rows = sb("bias_rows", [32, D])
        first_gain = sb("first_gain", [P, KD])
        vec = sb("vec", [P, KD, NVEC])
        lv = sb("lv", [P, KD, NV])
        small = sb("small", [P, 64])
        inv_freq = sb("inv_freq", [P, 1])
        minus_half = sb("minus_half", [P, KD])
        sink = sb("sink", [P, 8])
        soft = sb("soft", [P, 5, KD])
        rates = sb("rates", [P, 2, KD])
        angle = sb("angle", [P, 2, S])
        ps = ctx.enter_context(nc.psum_tensor("ps", [P, 8, 512], F32))

        first = first_gain[:, :].unsqueeze(2)

        def tiles(a):
            return a[:, 0:2048].rearrange("p (k n) -> p k n", n=S)

        xa_pad = a0[:, :].rearrange("p (k n) -> p k n", n=S + 3)
        prod_pad = a0[:, 0:8 * (S + 2)].rearrange("p (k n) -> p k n", n=S + 2)
        ple = a0[:, 0:TT * D].rearrange("p (t n) -> p t n", t=TT)
        scaled = a3[:, :].rearrange("p (t n) -> p t n", t=TT)
        rescaled = a4[:, :].rearrange("p (t n) -> p t n", t=TT)
        lru_w = a2[:, :].rearrange("p (m c n) -> p m c n", m=2, c=KD)
        q_t, k_t = tiles(a3), tiles(a4)
        v_rows = [a0, a1]
        pre_ss, pre_ms, pre_rs = small[:, 0:4], small[:, 4:8], small[:, 8:12]
        onehot, allowed = bias_rows[0:32, 0:REL], bias_rows[0:NHEAD, 512:512 + REL]
        rel = bias_rows[0:NHEAD, 0:REL]
        table = small[0:32, 32:32 + NHEAD]
        post_ss, post_ms, post_rs = small[:, 48:52], small[:, 12:14], small[:, 14:16]
        ret_ss, ret_ms, ret_rs = small[:, 16:18], small[:, 18:20], small[:, 20:22]

        raw_loaded = [signal(f"raw_loaded{i}", 16 * SLOTS // RAW) for i in range(RAW)]
        heads_done = signal("heads_done", 2 * SLOTS)
        split_done = signal("split_done", SLOTS, RAW)
        slot_used = signal("slot_used", SLOTS)
        x_loaded = sem("x_loaded")
        x_ready = signal("x_ready", 12, 4)
        pre_sum = signal("pre_sum", 12)
        pre_scale = signal("pre_scale", 6)
        pre_scaled = signal("pre_scaled", 12)
        u_turned = signal("u_turned", 3 * KD)
        u_head = signal("u_head", 3 * KD)
        u_ready = signal("u_ready", 3 * KD)
        rows_done = signal("rows_done", 3)
        post_sum = signal("post_sum", 12)
        gained = signal("gained", 12)
        post_scale = signal("post_scale", 6)
        gain_loaded = signal("gain_loaded", 3 * 16)
        act_ready = signal("act_ready", 2 * FFN_PAIRS, 2)
        mul_ready = signal("mul_ready", 2 * FFN_PAIRS, 2)
        h_ready = signal("h_ready", 2 * FFN_PAIRS)
        vec_turned = signal("vec_turned", 1)
        lv_ready = signal("lv_ready", 1)
        first_ready = signal("first_ready", 1, 1)
        lru_w_loaded = signal("lru_w_loaded", 4 * 16)
        xa_ready = signal("xa_ready", 4)
        xc_ready = signal("xc_ready", KD)
        lru_gates = signal("lru_gates", KD)
        lru_acts = signal("lru_acts", KD)
        gated_x = signal("gated_x", KD, 2)
        decays_ready = signal("decays_ready", 1)
        roots_ready = signal("roots_ready", 1)
        q_ready = signal("q_ready", 4)
        k_ready = signal("k_ready", 4)
        gelu_ready = signal("gelu_ready", 4)
        oa_ready = signal("oa_ready", 4)
        ga_ready = signal("ga_ready", 4)
        acc_ready = signal("acc_ready", 4)
        v_ready0 = signal("v_ready0", 2)
        v_ready1 = signal("v_ready1", 2)
        g_ready = signal("g_ready", 8)
        ret_scores = signal("ret_scores", HEADS)
        ret_probs = signal("ret_probs", HEADS)
        ret_out = signal("ret_out", HEADS)
        ret_sum = signal("ret_sum", HEADS)
        ret_scale = signal("ret_scale", HEADS)
        ret_scaled = signal("ret_scaled", HEADS)
        ret_turned = signal("ret_turned", HEADS)
        ret_ready = signal("ret_ready", HEADS, 1)
        sc_ready = signal("sc_ready", 4)
        sh_ready = signal("sh_ready", 4)
        gb_ready = signal("gb_ready", 4)
        ret_added = signal("ret_added", 4)
        oc_ready = signal("oc_ready", 4)
        gc_ready = signal("gc_ready", 4)
        mix_ready = signal("mix_ready", 4)
        vec_loaded = [sem(f"vec_loaded{i}") for i in range(3)]
        consts_loaded = sem("consts_loaded")
        pos_loaded = sem("pos_loaded")
        ident_ready, halves_ready = sem("ident_ready"), sem("halves_ready")
        first_turned = sem("first_turned")
        lam_ready, lam_exp = signal("lam_ready", 1), signal("lam_exp", 1)
        rates_ready = signal("rates_ready", 1)
        angles, sines = sem("angles"), signal("sines", 2)
        rel_done, rel_ready, rel_stored = sem("rel_done"), sem("rel_ready"), sem("rel_stored")
        act_own, dve_own, pool_own, pool_steps = sem("act_own"), sem("dve_own"), sem("pool_own"), sem("pool_steps")
        b = {n: sem(n) for n in (
            "proj_ready", "ka_swapped", "v_turned", "v_rows_a", "v_rows_b", "bias_loaded0", "bias_loaded1",
            "scored", "logits", "row_max", "exps", "turned", "exps_t", "attended", "den_ready",
            "attn_rows", "attn_sum", "attn_scale", "relu_ready", "sq_ready", "hid_ready", "p_loaded",
            "p_turned", "p_head", "p_ready", "brow_loaded", "gate_in", "gate_ready", "gated", "ple_sum", "ple_rows", "ple_gained",
            "ple_scale", "out_ready", "out_stored", "sink_loaded")}

        k_major = "l (k p) n -> p (l k) n"
        w_ffn_in = [t["ffn1_w_in"].rearrange(k_major, p=P), t["ffn2_w_in"].rearrange(k_major, p=P)]
        w_ffn_out = [t["ffn1_w_out"].rearrange(k_major, p=P), t["ffn2_w_out"].rearrange(k_major, p=P)]
        w_mix_in = t["w_mix_in"].rearrange(k_major, p=P)
        w_out = {n: t[w].rearrange(k_major, p=P) for n, w in (
            ("lru_out", "w_lru_out"), ("ret_out", "w_ret_out"), ("sc_out", "w_sc_out"), ("mix_out", "w_mix_out"))}
        b_w = {n: t[n + "_2"].rearrange(k_major, p=P)
               for n in ("w_in", "w_o", "w_up", "w_down", "w_ple_gate", "w_ple_proj")}

        def turned(l, i, k):
            bank = k // 2 + (0 if l is DEPTH and i in (1, 3) else 4)
            return ps[:, bank, S * (k % 2):S * (k % 2) + S]

        def bcast(row, n):
            return row.broadcast_to([P, n])

        def col_view(buf, n):
            return buf[n][:, :].rearrange("p (k n) -> p k n", n=SLOTC)

        def row_view(buf, n):
            return buf[n][:, :].rearrange("p (k n) -> p k n", n=D)

        VECTORS = [(slice(v, v + NV * (DEPTH - 1) + 1, NV), slice(0, D), t[name]) for v, name in (
            (V_G1, "ffn1_pre_g"), (V_GM, "mix_pre_g"), (V_CB, "lru_conv_b"), (V_BA, "lru_b_a"), (V_BX, "lru_b_x"),
            (V_LAM, "lru_lambda"), (V_G2, "ffn2_pre_g"))]
        for l in range(DEPTH):
            VECTORS += [(slice(l * NV + V_CW, l * NV + V_CW + 4), slice(0, D), t["lru_conv_w"][l]),
                        (slice(l * NV + V_SW, l * NV + V_SW + 3), slice(0, D), t["sc_conv_w"][l])]
        VECTORS += [(slice(V2_GMIX, V2_GMIX + 1), slice(0, D), t["g_pre_mix_2"]),
                    (slice(V2_GMLP, V2_GMLP + 1), slice(0, D), t["g_pre_mlp_2"]),
                    (slice(V2_GOUT, V2_GOUT + 1), slice(0, 512), t["g_out_a_2"]),
                    (slice(V2_GOUT, V2_GOUT + 1), slice(512, D), t["g_out_b_2"])]

        def load_vectors(queue, vectors, loaded):
            for part, cols, src in vectors:
                queue.dma_start(rows[part, cols], src).then_inc(loaded, 16)

        block = ctx.enter_context(nc.Block())

        @block.sync
        def _(sp):
            def load(l, n, src, half=False):
                sp.wait_ge(split_done.sem, split_done.at(l, n - RAW + 1))
                size = src.shape[1] * src.shape[2]
                dst = raw[n % RAW][:, 0:size].rearrange("p (k n) -> p k n", n=src.shape[2])
                sp.dma_start(dst, src).then_inc(raw_loaded[n % RAW].sem, 16)

            def feed_forward(l, which, base):
                w_in, w_o = w_ffn_in[which], w_ffn_out[which]

                def gate_up(n, col):
                    load(l, n, w_in[:, ds(l * KD, KD), ds(col, SLOTC)])
                    load(l, n + 1, w_in[:, ds(l * KD, KD), ds(col + D_FF, SLOTC)])

                with sp.Fori(0, FIRST_PAIRS // 2) as it:
                    for j in range(4):
                        n = base + j
                        sp.wait_ge(split_done.sem, l * SLOTS + it * 4 + (RAW + n - RAW + 1))
                        col = it * (2 * SLOTC) + ((j // 2) * SLOTC + (j % 2) * D_FF)
                        sp.dma_start(col_view(raw, n % RAW), w_in[:, ds(l * KD, KD), ds(col, SLOTC)])\
                          .then_inc(raw_loaded[n % RAW].sem, 16)
                for p in range(FIRST_PAIRS):
                    load(l, base + 2 * FIRST_PAIRS + p, w_o[:, ds(l * 2 * FFN_PAIRS + 2 * p, 2), :])
                for p in range(FIRST_PAIRS, FFN_PAIRS):
                    gate_up(base + FFN_IN2 + 2 * (p - FIRST_PAIRS), p * SLOTC)
                for i in range(2):
                    load(l, base + FFN_OUT2 + i, w_o[:, ds(l * 2 * FFN_PAIRS + 2 * FIRST_PAIRS + i, 1), :])
                for p in range(FIRST_PAIRS + 1, FFN_PAIRS):
                    load(l, base + FFN_OUT2 + 1 + p - FIRST_PAIRS, w_o[:, ds(l * 2 * FFN_PAIRS + 2 * p, 2), :])

            def mixer(l):
                for name, count in STAGES:
                    for j in range(count):
                        n = AT[name] + j
                        if name in V_HALF:
                            c = MC["v"] + D * V_HALF[name]
                            src = w_mix_in[:, ds(l * KD + 2 * j, 2), c:c + D]
                        elif name in MC:
                            src = w_mix_in[:, ds(l * KD, KD), MC[name] + SLOTC * j:MC[name] + SLOTC * (j + 1)]
                        elif name == "ret_out":
                            c = SLOTC * (j // 2)
                            src = w_out[name][:, ds(l * 2 * KD + KD * (j % 2), KD), c:c + SLOTC]
                        elif name == "mix_out":
                            src = w_out[name][:, ds(l * KD + 2 * j, 2), :]
                        else:
                            src = w_out[name][:, ds(l * KD, KD), SLOTC * j:SLOTC * (j + 1)]
                        load(l, n, src)

            sp.sem_inc(split_done.sem, RAW)
            sp.dma_start(a0[:, 0:S].bitcast(I32), bcast(t["positions"].rearrange("(a n) -> a n", a=1), S))\
              .then_inc(pos_loaded, 16)
            for tt in range(TT):
                sp.dma_start(x[:, tt, :], t["x"].rearrange("b (t p) d -> p (b t) d", p=P)[:, tt, :]).then_inc(x_loaded, 16)
            with sp.Fori(0, DEPTH) as l:
                feed_forward(l, 0, 0)
                mixer(l)
                feed_forward(l, 1, FFN2)
            l = DEPTH
            for j in range(9):
                load(l, B_IN + j, b_w["w_in"][:, :, SLOTC * j:SLOTC * (j + 1)])
            for j in range(4):
                load(l, B_O + j, b_w["w_o"][:, 2 * j:2 * j + 2, :])
            for part in range(2):
                up, down = (B_UP, B_DN) if part == 0 else (B_UP2, B_DN2)
                for j in range(8):
                    c = SLOTC * (8 * part + j)
                    load(l, up + j, b_w["w_up"][:, :, c:c + SLOTC])
                for j in range(8):
                    k = 2 * (8 * part + j)
                    if down + j == B_PLE:
                        load(l, B_PLE, b_w["w_ple_proj"][:, 0:2, :])
                    load(l, down + j + (down + j >= B_PLE), b_w["w_down"][:, k:k + 2, :])
            for j in range(4):
                load(l, B_GATE + j, b_w["w_ple_gate"][:, 2 * j:2 * j + 2, :])
            for q in range(2 * TT):
                half = slice(512 * (q % 2), 512 * (q % 2) + 512)
                sp.wait_ge(b["out_ready"], q + 1)
                sp.dma_start(out.rearrange("b (t p) d -> p (b t) d", p=P)[:, q // 2, half], x[:, q // 2, half])\
                  .then_inc(b["out_stored"], 16)
            sp.wait_ge(b["out_stored"], 16 * 2 * TT)

        @block.gpsimd
        def _(pool):
            own = Chain(pool, pool_own)

            def until(sig, count):
                pool.wait_ge(sig.sem, count)
                pool.sem_inc(pool_steps, 1)

            def norm(l, i, ss, ms, rs, sums, scale, by=1.0):
                for tt in range(TT):
                    until(sums, sums.at(l, 4 * i + 2 * tt + 2))
                    own.done(nc.gpsimd.tensor_scalar(ms[:, tt:tt + 1], ss[:, 2 * tt:2 * tt + 1],
                                                     ss[:, 2 * tt + 1:2 * tt + 2], EPS / (by * by), ALU.add, ALU.add))
                    nc.gpsimd.tensor_tensor(rs[:, tt:tt + 1], ms[:, tt:tt + 1], minus_half[:, 0:1], ALU.pow)\
                      .then_inc(scale.sem, 1)

            def pre(l, i):
                norm(l, i, pre_ss, pre_ms, pre_rs, pre_sum, pre_scale)

            def post(l, i, by):
                norm(l, i, post_ss, post_ms, post_rs, post_sum, post_scale, by)

            def gain(l, i, src):
                until(x_ready, x_ready.at(l, 4 * i))
                pool.dma_start(gain_row[:, :], src).then_inc(gain_loaded.sem, 16)

            def gain_of(name, l):
                return bcast(t[name][ds(l, 1), :], D)

            nc.gpsimd.memset(minus_half[:, :], -0.5).then_inc(halves_ready, 1)
            pool.wait_ge(halves_ready, 1)
            own.done(nc.gpsimd.memset(ident[:, :], 0.0))
            nc.gpsimd.affine_select(out=ident[:, :], in_=ident[:, :], compare_op=ALU.not_equal, fill=1.0,
                                    base=0, pattern=[[-1, P]], channel_multiplier=1).then_inc(ident_ready, 1)
            load_vectors(pool, VECTORS[4:8], vec_loaded[2])
            pool.wait_ge(x_loaded, 16 * TT)
            pool.sem_inc(x_ready.sem, x_ready.primed)
            pre(0, 0)
            load_vectors(pool, VECTORS[8:], vec_loaded[2])
            pool.dma_start(sink[:, :], bcast(t["sink_a_2"], 8)).then_inc(b["sink_loaded"], 16)
            pool.dma_start(decay[:, :, :].rearrange("p h n -> p (h n)"), t["decay"]).then_inc(consts_loaded, 16)
            pool.dma_start(table, t["rel_bias_table_2"]).then_inc(consts_loaded, 16)
            pool.dma_start(onehot, t["onehot"]).then_inc(consts_loaded, 16)
            pool.dma_start(allowed, t["allowed"]).then_inc(consts_loaded, 16)
            own.restart()
            with pool.Fori(0, DEPTH) as l:
                until(ret_ready, ret_ready.at(l, 0))
                own.done(nc.gpsimd.memset(a2[:, :], 0.0))
                for m, name in enumerate(("lru_w_a", "lru_w_x")):
                    w = t[name].rearrange("l (c e) i j -> e i (l c) j", e=2)
                    for e in range(2):
                        pool.dma_start(lru_w[64 * e:64 * e + 64, m, :, 64 * e:64 * e + 64],
                                       w[e, :, ds(l * KD, KD), :]).then_inc(lru_w_loaded.sem, 16)
                gain(l, 0, gain_of("ffn1_post_g", l))
                G = nc.gpsimd
                lam = lv[:, :, V_LAM]
                lam3, z, w, w2, s = (soft[:, i, :] for i in range(5))
                until(lv_ready, lv_ready.at(l, 1))
                own.done(G.tensor_scalar(lam3, lam, -1.0, 0.0, ALU.mult, ALU.max))
                own.done(G.tensor_scalar(w, lam3, 2.0, None, ALU.mult))
                own.done(G.tensor_tensor(z, w, lam, ALU.add))
                pool.sem_inc(lam_ready.sem, 1)
                until(lam_exp, lam_exp.at(l, 1))
                own.done(G.tensor_scalar(w, z, 2.0, None, ALU.add))
                own.done(G.tensor_tensor(w, w, w, ALU.mult))
                own.done(G.tensor_tensor(w, w, minus_half[:, :], ALU.pow))
                own.done(G.tensor_tensor(w, w, z, ALU.mult))
                own.done(G.tensor_tensor(w2, w, w, ALU.mult))
                own.done(G.tensor_scalar(s, w2, 1.0 / 17, None, ALU.mult))
                for odd in (15, 13, 11, 9, 7, 5, 3):
                    own.done(G.tensor_scalar(s, s, 1.0 / odd, None, ALU.add))
                    own.done(G.tensor_tensor(s, s, w2, ALU.mult))
                own.done(G.tensor_scalar(s, s, 1.0, 8.0, ALU.add, ALU.mult))
                own.done(G.tensor_tensor(s, s, w, ALU.mult))
                own.done(G.tensor_scalar(lam3, lam3, 4.0, None, ALU.mult))
                own.done(G.tensor_tensor(rates[:, 0, :], s, lam3, ALU.add))
                own.done(G.tensor_scalar(rates[:, 1, :], rates[:, 0, :], -2.0, None, ALU.mult))
                pool.sem_inc(rates_ready.sem, 1)
                post(l, 0, 0.5)
                pre(l, 1)
                gain(l, 1, gain_of("mix_post_g", l))
                for h in range(HEADS):
                    until(ret_sum, ret_sum.at(l, h + 1))
                    own.done(nc.gpsimd.tensor_scalar(ret_ms, ret_ss, 1.0 / HV, EPS, ALU.mult, ALU.add))
                    nc.gpsimd.tensor_tensor(ret_rs, ret_ms, minus_half[:, 0:2], ALU.pow).then_inc(ret_scale.sem, 1)
                post(l, 1, 1.0)
                pre(l, 2)
                gain(l, 2, gain_of("ffn2_post_g", l))
                post(l, 2, 0.5)
                pre(l, 3)
                own.restart()
            l = DEPTH
            gain(l, 0, gain_of("g_post_mix_2", 0))
            pool.wait_ge(rel_stored, 16)
            def band(h):
                ring = a1 if h % 10 < 5 else a2
                s = (h % 5) * BIASW
                return ring[:, s:s + BIASW]
            for h in range(NHEAD):
                if h >= 10:
                    pool.wait_ge(b["logits"], h - 9)
                elif h == 0:
                    pool.wait_ge(x_ready.sem, x_ready.at(l, 0))
                src = bass.AP(tensor=scratch.tensor, offset=scratch.offset + h * 512, ap=[[1, P], [1, BIASW]])
                pool.dma_start(band(h), src).then_inc(b["bias_loaded0" if h % 2 == 0 else "bias_loaded1"], 16)
                pool.wait_ge(b["bias_loaded0" if h % 2 == 0 else "bias_loaded1"], 16 * (h // 2 + 1))
            pool.wait_ge(b["attn_sum"], 4)
            own.done(nc.gpsimd.tensor_scalar(pre_ms, pre_ss, 1.0 / 512, EPS, ALU.mult, ALU.add))
            nc.gpsimd.tensor_tensor(pre_rs, pre_ms, minus_half[:, 0:4], ALU.pow).then_inc(b["attn_scale"], 1)
            post(l, 0, 1.0)
            pre(l, 1)
            gain(l, 1, gain_of("g_post_mlp_2", 0))
            pool.wait_ge(b["den_ready"], 2)
            pool.dma_start(a1[:, 0:2 * S].rearrange("p (t n) -> p t n", t=TT),
                           t["p_2"].rearrange("l b (t p) n -> p (l b t) n", p=P)).then_inc(b["p_loaded"], 16)
            post(l, 1, 1.0)
            gain(l, 2, gain_of("g_post_ple_2", 0))
            pool.dma_start(a2[:, 0:D], gain_of("b_ple_gate_2", 0)).then_inc(b["brow_loaded"], 16)
            for tt in range(TT):
                pool.wait_ge(b["ple_sum"], 2 * tt + 2)
                own.done(nc.gpsimd.tensor_scalar(post_ms[:, tt:tt + 1], post_ss[:, 2 * tt:2 * tt + 1],
                                                 post_ss[:, 2 * tt + 1:2 * tt + 2], EPS, ALU.add, ALU.add))
                nc.gpsimd.tensor_tensor(post_rs[:, tt:tt + 1], post_ms[:, tt:tt + 1], minus_half[:, 0:1], ALU.pow)\
                  .then_inc(b["ple_scale"], 1)

        @block.scalar
        def _(act):
            A = nc.scalar.activation
            own = Chain(act, act_own)

            def head(l, n, size=2048, it=0, first=False):
                r = n % RAW
                act.wait_ge(raw_loaded[r].sem, raw_loaded[r].at(l, 16 * (n // RAW + 1)) + it * 16)
                if not first:
                    act.wait_ge(slot_used.sem, slot_used.at(l, n - 1) + it * 4)
                for i in range(2):
                    part = slice(i * size // 2, (i + 1) * size // 2)
                    A(w_hi[n % SPLIT][:, part], raw[r][:, part], ACT.Copy).then_inc(heads_done.sem, 1)

            def pre(l, i, gains, col, base, t=None):
                squares(l, i)
                head(l, base + 1)
                if i == 1 and gains is lv:
                    act.wait_ge(lv_ready.sem, lv_ready.at(l, 1))
                elif i == 3:
                    act.wait_ge(first_ready.sem, first_ready.at(l, 1))
                u_heads(l, i if t is None else t, gains, col)

            def squares(l, i):
                for q in range(2 * TT):
                    tt, half = q // 2, slice(512 * (q % 2), 512 * (q % 2) + 512)
                    act.wait_ge(x_ready.sem, x_ready.at(l, 4 * i + q - 3))
                    A(a5[:, 512 * q:512 * q + 512], x[:, tt, half], ACT.Square, scale=D ** -0.5,
                      accum_out=pre_ss[:, q:q + 1]).then_inc(pre_sum.sem, 1)

            def u_heads(l, i, gains, col):
                for k in range(KD):
                    act.wait_ge(u_turned.sem, u_turned.at(l, KD * i + (k | 1) + 1))
                    A(u_hi[:, k, :], turned(l, i, k), ACT.Copy, scale=gains[:, k, col:col + 1]).then_inc(u_head.sem, 1)

            def post(l, i, end, by=1.0):
                for q in range(2 * TT):
                    tt = q // 2
                    if q == 0:
                        act.wait_ge(rows_done.sem, rows_done.at(l, i + 1))
                    elif q == 2:
                        act.wait_ge(slot_used.sem, slot_used.at(l, end))
                    else:
                        act.wait_ge(gained.sem, gained.at(l, 4 * i + 2 * tt + 1))
                    A(a5[:, 512 * q:512 * q + 512], ps[:, 4 + q, :], ACT.Square, scale=D ** -0.5 / by,
                      accum_out=post_ss[:, q:q + 1]).then_inc(post_sum.sem, 1)

            def silu(l, which, base, p, it=0):
                pair = FFN_PAIRS * which + p
                n = base + (2 * p if p < FIRST_PAIRS else FFN_IN2 + 2 * (p - FIRST_PAIRS))
                bank = (2 * which + 2 * p) % 4
                act.wait_ge(slot_used.sem, slot_used.at(l, n + 1) + it * 4)
                act.wait_ge(mul_ready.sem, mul_ready.at(l, pair - 1) + it * 2)
                A(act2[:, pair % 2, :], ps[:, bank, :], ACT.Silu).then_inc(act_ready.sem, 1)

            def feed_forward(l, which, base):
                with act.Fori(0, FIRST_PAIRS // 2) as it:
                    for j in range(4):
                        head(l, base + j + 2, it=it)
                        if j % 2 == 0:
                            silu(l, which, base, j // 2, it)
                for n in range(base + 2 * FIRST_PAIRS, base + FFN_SLOTS - 1):
                    at = n - base
                    head(l, n + 2, 1024 if FFN_OUT2 <= at + 2 < FFN_OUT2 + 2 else 2048)
                    if which == 0 and at == 2 * FIRST_PAIRS + 1:
                        for r, wave in enumerate((sin2, cos2)):
                            A(wave[:, :], angle[:, r, :], ACT.Sin).then_inc(sines.sem, 1)
                    if which == 0 and at == FFN_IN2 - 1:
                        act.wait_ge(lam_ready.sem, lam_ready.at(l, 1))
                        A(soft[:, 1, :], soft[:, 1, :], ACT.Exp, scale=-1.0).then_inc(lam_exp.sem, 1)
                    if FFN_IN2 <= at < FFN_OUT2 and (at - FFN_IN2) % 2 == 0:
                        silu(l, which, base, FIRST_PAIRS + (at - FFN_IN2) // 2)
                post(l, 2 * which, base + FFN_SLOTS, 0.5)

            def from_slot(l, n):
                act.wait_ge(slot_used.sem, slot_used.at(l, n + 1))

            def mixer(l):
                for name, count in STAGES:
                    for j in range(count):
                        n = AT[name] + j
                        m = n - MIX0
                        bank = (2 + j) % 4
                        pair = slice(2 * j, 2 * j + 2)
                        pv = ps[:, bank, :].rearrange("p (a n) -> p a n", a=2)
                        c = m - GATE0
                        if 0 <= c < KD:
                            act.wait_ge(lru_gates.sem, lru_gates.at(l, c + 1))
                            act.wait_ge(gated_x.sem, gated_x.at(l, c - 1))
                            if c == 0:
                                act.wait_ge(rates_ready.sem, rates_ready.at(l, 1))
                                act.wait_ge(xc_ready.sem, xc_ready.at(l, KD))
                            own.done(A(tiles(a5)[:, c, :], ps[:, 4 + c % 4, 0:S], ACT.Sigmoid,
                                       bias=lv[:, c, V_BA:V_BA + 1]))
                            A(act2[:, 0, S * (c % 2):S * (c % 2) + S], ps[:, 4 + c % 4, S:2 * S], ACT.Sigmoid,
                              bias=lv[:, c, V_BX:V_BX + 1])
                            A(tiles(a0)[:, c, :], tiles(a5)[:, c, :], ACT.Tanh, scale=rates[:, 0, c:c + 1])\
                              .then_inc(lru_acts.sem, 1)
                        if name == "g" and j % 2 == 1:
                            h = j // 2
                            act.wait_ge(ret_out.sem, ret_out.at(l, h + 1))
                            if h >= 1:
                                act.wait_ge(ret_scale.sem, ret_scale.at(l, h))
                            for tt in range(TT):
                                own.done(A(act2[:, 1, :], ps[:, 5 + tt, :], ACT.Square, accum_out=ret_ss[:, tt:tt + 1]))
                            act.sem_inc(ret_sum.sem, 1)
                            own.restart()
                        if n < FFN2 - 1:
                            head(l, n + 2)
                        if name in ("xa", "ya", "ga", "g", "sc", "gb", "gc"):
                            from_slot(l, n)
                        if name == "xa":
                            A(xa_pad[:, pair, 3:3 + S], pv, ACT.Copy).then_inc(xa_ready.sem, 1)
                        elif name == "ya":
                            A(tiles(a2)[:, pair, :], pv, ACT.Gelu_apprx_tanh).then_inc(gelu_ready.sem, 1)
                        elif name == "ga":
                            act.wait_ge(oa_ready.sem, oa_ready.at(l, j + 1))
                            A(tiles(a5)[:, pair, :], pv, ACT.Sigmoid).then_inc(ga_ready.sem, 1)
                        elif name in V_HALF and j == 3:
                            from_slot(l, n)
                            act.wait_ge(oa_ready.sem, oa_ready.at(l, 4))
                            A(v_rows[0][:, D * V_HALF[name]:D * V_HALF[name] + D], ps[:, 4:6, :].rearrange("p a n -> p (a n)"),
                              ACT.Copy).then_inc(v_ready0.sem, 1)
                        elif name == "g":
                            if j >= 4:
                                act.wait_ge(ret_ready.sem, ret_ready.at(l, j // 2 - 1))
                            A(a2[:, 512 * (j % 4):512 * (j % 4) + 512], ps[:, bank, :], ACT.Silu).then_inc(g_ready.sem, 1)
                        elif name == "sc":
                            A(tiles(a1)[:, pair, :], pv, ACT.Copy).then_inc(sc_ready.sem, 1)
                        elif name == "gb":
                            A(tiles(a4)[:, pair, :], pv, ACT.Sigmoid).then_inc(gb_ready.sem, 1)
                        elif name == "gc":
                            act.wait_ge(ret_added.sem, ret_added.at(l, j + 1))
                            A(tiles(a4)[:, pair, :], pv, ACT.Sigmoid).then_inc(gc_ready.sem, 1)
                        if m == GATE0 + KD - 1:
                            act.wait_ge(lru_acts.sem, lru_acts.at(l, KD))
                            for k in range(KD):
                                ins = A(tiles(a5)[:, k, :], tiles(a5)[:, k, :], ACT.Exp, scale=rates[:, 1, k:k + 1])
                            ins.then_inc(decays_ready.sem, 1)
                        if m == GATE0 + KD + 1:
                            A(a0[:, 0:2048], a0[:, 0:2048], ACT.Sqrt).then_inc(roots_ready.sem, 1)
                post(l, 1, FFN2)

            load_vectors(act, VECTORS[0:1], vec_loaded[0])
            act.dma_start(inv_freq[:, :], t["inv_freq"]).then_inc(pos_loaded, 16)
            load_vectors(act, VECTORS[1:4], vec_loaded[1])
            squares(0, 0)
            head(0, 0, first=True)
            act.wait_ge(first_ready.sem, 1)
            u_heads(0, 0, first, 0)
            head(0, 1, first=True)
            act.wait_ge(angles, 1)
            with act.Fori(0, DEPTH) as l:
                feed_forward(l, 0, 0)
                pre(l, 1, lv, V_GM, MIX0)
                mixer(l)
                pre(l, 2, lv, V_G2, FFN2)
                feed_forward(l, 1, FFN2)
                pre(l, 3, first, 0, SLOTS)

            l = DEPTH
            dst = {0: (a3, 0), 1: (a3, 512), 2: (a4, 0), 3: (a3, 1024), 4: (a3, 1536), 5: (a4, 512), 6: (a4, 1024),
                   7: (a5, 0), 8: (a5, 512)}
            for j in range(9):
                head(l, j + 2)
                if j == 1:
                    act.wait_ge(rel_ready, 1)
                    act.dma_start(scratch[:, 0:REL], rel).then_inc(rel_stored, 16)
                a, o = dst[j]
                A(a[:, o:o + 512], ps[:, j % 4, :], ACT.Copy).then_inc(b["proj_ready"], 1)
            act.wait_ge(b["proj_ready"], 3)
            act.dma_start(a4[64:128, 1536:1536 + S], a4[0:64, 0:S]).then_inc(b["ka_swapped"], 16)
            act.dma_start(a4[0:64, 1536:1536 + S], a4[64:128, 0:S]).then_inc(b["ka_swapped"], 16)
            act.wait_ge(b["v_turned"], 1)
            A(v_rows[0][:, 0:512], ps[:, 4, :], ACT.Copy).then_inc(b["v_rows_a"], 1)
            A(v_rows[0][:, 640:640 + 512], ps[:, 5, :], ACT.Copy).then_inc(b["v_rows_a"], 1)
            def exps_columns(h):
                act.wait_ge(b["turned"], h + 1)
                if h >= 2:
                    act.wait_ge(b["attended"], h - 1)
                A(mul2[:, h % 2, :], ps[:, 2 + h % 2, :], ACT.Copy).then_inc(b["exps_t"], 1)
            for h in range(NHEAD):
                act.wait_ge(b["row_max"], h + 1)
                for tt in range(TT):
                    c = 4 * (h % 2) + tt
                    A(act2[:, h % 2, S * tt:S * tt + S], act2[:, h % 2, S * tt:S * tt + S], ACT.Exp,
                      bias=small[:, 24 + c:25 + c], accum_out=probs[:, 0, 2 * h + tt:2 * h + tt + 1])\
                      .then_inc(b["exps"], 1)
                if h < 8:
                    for tt in range(TT):
                        c = 4 * (h % 2) + tt
                        A(probs[:, 1, 2 * h + tt:2 * h + tt + 1], sink[:, h:h + 1], ACT.Exp,
                          bias=small[:, 24 + c:25 + c]).then_inc(b["exps"], 1)
                if h >= 1:
                    exps_columns(h - 1)
            exps_columns(NHEAD - 1)
            for tt in range(TT):
                for kind in range(2):
                    i = 2 * tt + kind
                    act.wait_ge(b["attn_rows"], i + 1)
                    own.done(A(a5[:, 0:512], a1[:, D * tt + 512 * kind:D * tt + 512 * kind + 512], ACT.Square,
                               accum_out=pre_ss[:, i:i + 1]))
                    act.sem_inc(b["attn_sum"], 1)
            u_heads(l, 1, vec, V2_GOUT)
            for j in range(B_O, B_UP - 1):
                head(l, j + 2)
            post(l, 0, B_UP)
            pre(l, 1, vec, V2_GMLP, B_UP, t=2)
            for part in range(2):
                for j in range(16 + part):
                    n = (B_UP if part == 0 else B_UP2) + j
                    if n < B_GATE - 1:
                        head(l, n + 2)
                    if n == B_DN2 + 4:
                        act.wait_ge(b["p_turned"], 1)
                        A(u_hi[:, 0:2, :], ps[:, 0, :].rearrange("p (a n) -> p a n", a=2), ACT.Copy).then_inc(b["p_head"], 1)
                    if n == B_PLE:
                        act.wait_ge(slot_used.sem, slot_used.at(l, n + 1))
                        for tt in range(TT):
                            A(ple[:, tt, :], ps[:, 2 * tt:2 * tt + 2, :].rearrange("p a n -> p (a n)"), ACT.Copy)\
                             .then_inc(b["ple_rows"], 1)
                    if j < 8:
                        p = 8 * part + j
                        act.wait_ge(slot_used.sem, slot_used.at(l, n + 1))
                        if p >= 2:
                            act.wait_ge(b["sq_ready"], p - 1)
                        A(act2[:, p % 2, :], ps[:, (9 + p) % 4, :], ACT.Relu).then_inc(b["relu_ready"], 1)
            post(l, 1, B_GATE)
            for k in range(KD):
                act.wait_ge(u_turned.sem, u_turned.at(l, KD * 3 + (k | 1) + 1))
                A(u_hi[:, k, :], turned(l, 3, k), ACT.Copy).then_inc(u_head.sem, 1)
            for n in range(B_GATE - 1, B_SLOTS - 2):
                head(l, n + 2)
            for tt in range(TT):
                for q in (2 * tt, 2 * tt + 1):
                    act.wait_ge(b["gate_in"], q + 1)
                    A(a3[:, 512 * q:512 * q + 512], a3[:, 512 * q:512 * q + 512], ACT.Sigmoid).then_inc(b["gate_ready"], 1)
                for q in (2 * tt, 2 * tt + 1):
                    act.wait_ge(b["gated"], q + 1)
                    A(a5[:, 512 * q:512 * q + 512], a3[:, 512 * q:512 * q + 512], ACT.Square, scale=D ** -0.5,
                      accum_out=post_ss[:, q:q + 1]).then_inc(b["ple_sum"], 1)

        @block.vector
        def _(dve):
            V = nc.vector
            own = Chain(dve, dve_own)

            def rest(l, n, size=2048, it=0):
                for i in range(2):
                    half_rest(l, n, i, size, it)

            def half_rest(l, n, i, size=2048, it=0):
                part = slice(i * size // 2, (i + 1) * size // 2)
                dve.wait_ge(heads_done.sem, heads_done.at(l, 2 * n + i + 1) + it * 8)
                ins = V.tensor_tensor(w_lo[n % SPLIT][:, part], raw[n % RAW][:, part], w_hi[n % SPLIT][:, part],
                                      ALU.subtract)
                if i == 1:
                    ins.then_inc(split_done.sem, 1)

            def pre(l, i, gains, col, base, t=None):
                for tt in range(TT):
                    scales(l, i, tt)
                    half_rest(l, base, tt)
                u_rests(l, i if t is None else t, gains, col)
                rest(l, base + 1)

            def scales(l, i, tt):
                for q in (2 * tt, 2 * tt + 1):
                    half = slice(512 * (q % 2), 512 * (q % 2) + 512)
                    dve.wait_ge(pre_scale.sem, pre_scale.at(l, TT * i + tt + 1))
                    V.tensor_scalar(scaled[:, tt, half], x[:, tt, half], pre_rs[:, tt:tt + 1], None, ALU.mult)\
                     .then_inc(pre_scaled.sem, 1)

            def u_rests(l, i, gains, col):
                for k in range(KD):
                    dve.wait_ge(u_head.sem, u_head.at(l, KD * i + (k | 1) + 1))
                    V.scalar_tensor_tensor(u_lo[:, k, :], turned(l, i, k), gains[:, k, col:col + 1], u_hi[:, k, :], ALU.mult, ALU.subtract)\
                     .then_inc(u_ready.sem, 1)

            def post(l, i, end):
                def gain_halves(tt):
                    if tt == 0:
                        dve.wait_ge(rows_done.sem, rows_done.at(l, i + 1))
                    else:
                        dve.wait_ge(slot_used.sem, slot_used.at(l, end))
                    for q in (2 * tt + 1, 2 * tt):
                        half = slice(512 * (q % 2), 512 * (q % 2) + 512)
                        if q == 2 * tt:
                            dve.wait_ge(post_sum.sem, post_sum.at(l, 4 * i + q + 1))
                        V.tensor_tensor(rescaled[:, tt, half], ps[:, 4 + q, :], gain_row[:, half], ALU.mult)\
                         .then_inc(gained.sem, 1)
                    dve.wait_ge(gained.sem, gained.at(l, 4 * i + 2 * tt + 2))

                def add(q):
                    tt, half = q // 2, slice(512 * (q % 2), 512 * (q % 2) + 512)
                    dve.wait_ge(post_scale.sem, post_scale.at(l, TT * i + tt + 1))
                    V.scalar_tensor_tensor(x[:, tt, half], rescaled[:, tt, half], post_rs[:, tt:tt + 1], x[:, tt, half],
                                           ALU.mult, ALU.add).then_inc(x_ready.sem, 1)

                dve.wait_ge(gain_loaded.sem, gain_loaded.at(l, 16 * (i + 1)))
                gain_halves(0)
                add(0)
                gain_halves(1)
                for q in (1, 2, 3):
                    add(q)

            def split(src, hi, lo, sig):
                own.done(V.tensor_copy(hi, src))
                V.tensor_tensor(lo, src, hi, ALU.subtract).then_inc(sig, 1)

            def hidden(l, which, base, p, it=0):
                pair = FFN_PAIRS * which + p
                n = base + (2 * p if p < FIRST_PAIRS else FFN_IN2 + 2 * (p - FIRST_PAIRS)) + 1
                bank = (2 * which + 2 * p) % 4 + 1
                dve.wait_ge(slot_used.sem, slot_used.at(l, n + 1) + it * 4)
                dve.wait_ge(act_ready.sem, act_ready.at(l, pair + 1) + it * 2)
                V.tensor_tensor(mul2[:, pair % 2, :], ps[:, bank, :], act2[:, pair % 2, :], ALU.mult)\
                 .then_inc(mul_ready.sem, 1)
                dve.wait_ge(mul_ready.sem, mul_ready.at(l, pair + 1) + it * 2)
                k = ds(2 * p + it * 4, 2) if p < FIRST_PAIRS else slice(2 * (p - FIRST_PAIRS), 2 * (p - FIRST_PAIRS) + 2)
                split(mul2[:, pair % 2, :].rearrange("p (a n) -> p a n", a=2), h_hi[:, k, :], h_lo[:, k, :], h_ready.sem)

            def feed_forward(l, which, base):
                own.restart()
                with dve.Fori(0, FIRST_PAIRS // 2) as it:
                    for j in range(4):
                        rest(l, base + j + 2, it=it)
                        if j % 2 == 1:
                            hidden(l, which, base, j // 2, it)
                    own.restart()
                for n in range(base + 2 * FIRST_PAIRS, base + FFN_SLOTS - 2):
                    at = n - base
                    rest(l, n + 2, 1024 if FFN_OUT2 <= at + 2 < FFN_OUT2 + 2 else 2048)
                    if which == 0 and at == 2 * FIRST_PAIRS + FIRST_PAIRS - 2:
                        dve.wait_ge(vec_turned.sem, vec_turned.at(l, 1))
                        own.done(V.tensor_copy(vec[:, :, 0:NVEC],
                                               ps[:, 0, 0:KD * NVEC].rearrange("p (k v) -> p k v", v=NVEC)))
                        V.tensor_copy(lv[:, :, :], vec[:, :, ds(l * NV, NV)]).then_inc(lv_ready.sem, 1)
                    if FFN_IN2 <= at < FFN_OUT2 and (at - FFN_IN2) % 2 == 1:
                        hidden(l, which, base, FIRST_PAIRS + (at - FFN_IN2) // 2)
                post(l, 2 * which, base + FFN_SLOTS)

            def rope(l, j, bank, dst, sig):
                pv = ps[:, bank, :].rearrange("p (a n) -> p a n", a=2)
                c3 = cos2[:, :].unsqueeze(1).broadcast_to([P, 2, S])
                s3 = sin2[:, :].unsqueeze(1).broadcast_to([P, 2, S])
                V.tensor_tensor(mul2[:, 0, :].rearrange("p (a n) -> p a n", a=2), pv, c3, ALU.mult)
                own.done(V.tensor_tensor(mul2[:, 1, :].rearrange("p (a n) -> p a n", a=2), pv, s3, ALU.mult))
                V.tensor_tensor(dst[:, 2 * j, :], mul2[:, 0, 0:S], mul2[:, 1, S:2 * S], ALU.subtract)
                own.done(V.tensor_tensor(dst[:, 2 * j + 1, :], mul2[:, 0, S:2 * S], mul2[:, 1, 0:S], ALU.add))
                dve.sem_inc(sig.sem, 1)

            def recurrence(l, j):
                f = slice(512 * j, 512 * j + 512)
                own.done(V.scalar_tensor_tensor(a0[:, f], a5[:, f], 1.0, a0[:, f], ALU.add, ALU.mult))
                own.done(V.tensor_tensor(a1[:, f], a0[:, f], a1[:, f], ALU.mult))
                for c in (2 * j, 2 * j + 1):
                    g = slice(S * c, S * c + S)
                    own.done(V.tensor_tensor_scan(a0[:, g], a5[:, g], a1[:, g], 0.0, ALU.mult, ALU.add))
                dve.wait_ge(gelu_ready.sem, gelu_ready.at(l, j + 1))
                own.done(V.tensor_tensor(a0[:, f], a0[:, f], a2[:, f], ALU.mult))
                split(tiles(a0)[:, 2 * j:2 * j + 2, :], h_hi[:, 2 * j:2 * j + 2, :], h_lo[:, 2 * j:2 * j + 2, :], oa_ready.sem)

            def mixer(l):
                own.done(V.memset(xa_pad[:, :, 0:3], 0.0))
                for name, count in STAGES:
                    for j in range(count):
                        n = AT[name] + j
                        m = n - MIX0
                        bank = (2 + j) % 4
                        pair = slice(2 * j, 2 * j + 2)
                        pv = ps[:, bank, :].rearrange("p (a n) -> p a n", a=2)
                        c = m - GATE0
                        if 0 <= c < KD:
                            dve.wait_ge(lru_acts.sem, lru_acts.at(l, c + 1))
                            V.tensor_tensor(tiles(a1)[:, c, :], tiles(a1)[:, c, :], act2[:, 0, S * (c % 2):S * (c % 2) + S],
                                            ALU.mult).then_inc(gated_x.sem, 1)
                            dve.wait_ge(gated_x.sem, gated_x.at(l, c + 1))
                        if name == "g" and j % 2 == 0:
                            h = j // 2
                            dve.wait_ge(ret_scores.sem, ret_scores.at(l, h + 1))
                            if h >= 2:
                                dve.wait_ge(ret_out.sem, ret_out.at(l, h - 1))
                            V.tensor_tensor(probs[:, h % 2, :], ps[:, 4, 0:384], decay[:, h, :], ALU.mult)\
                             .then_inc(ret_probs.sem, 1)
                        if name in ("g", "sc") and (m - 34) % 2 == 0 and 0 <= (m - 34) // 2 < HEADS:
                            h = (m - 34) // 2
                            dve.wait_ge(ret_turned.sem, ret_turned.at(l, h + 1))
                            dve.wait_ge(g_ready.sem, g_ready.at(l, 2 * h + 2))
                            sg = a2[:, D * (h % 2):D * (h % 2) + D]
                            own.done(V.tensor_tensor(sg, ps[:, 6:8, :].rearrange("p a n -> p (a n)"), sg, ALU.mult))
                            split(sg.rearrange("p (k n) -> p k n", n=S), h_hi[:, 4 * h:4 * h + 4, :],
                                  h_lo[:, 4 * h:4 * h + 4, :], ret_ready.sem)
                        if name == "g" and j % 2 == 1:
                            h = j // 2
                            dve.wait_ge(ret_scale.sem, ret_scale.at(l, h + 1))
                            V.tensor_scalar(mul2[:, 0, :], ps[:, 5, :], ret_rs[:, 0:1], None, ALU.mult)
                            V.tensor_scalar(mul2[:, 1, :], ps[:, 6, :], ret_rs[:, 1:2], None, ALU.mult)\
                             .then_inc(ret_scaled.sem, 1)
                        if n < FFN2 - 2:
                            rest(l, n + 2)
                        if name == "xa":
                            dve.wait_ge(xa_ready.sem, xa_ready.at(l, j + 1))
                            for c in (2 * j, 2 * j + 1):
                                own.done(V.tensor_scalar(tiles(a1)[:, c, :], xa_pad[:, c, 3:3 + S],
                                                         lv[:, c, V_CW + 3:V_CW + 4], lv[:, c, V_CB:V_CB + 1],
                                                         ALU.mult, ALU.add))
                                for tap in (2, 1, 0):
                                    ins = V.scalar_tensor_tensor(tiles(a1)[:, c, :], xa_pad[:, c, tap:tap + S],
                                                                 lv[:, c, V_CW + tap:V_CW + tap + 1], tiles(a1)[:, c, :],
                                                                 ALU.mult, ALU.add)
                                    if tap:
                                        own.done(ins)
                                ins.then_inc(xc_ready.sem, 1)
                        elif name == "q":
                            if j == 0:
                                dve.wait_ge(sines.sem, sines.at(l, 2))
                            dve.wait_ge(slot_used.sem, slot_used.at(l, n + 1))
                            rope(l, j, bank, q_t, q_ready)
                        elif name == "k":
                            dve.wait_ge(slot_used.sem, slot_used.at(l, n + 1))
                            rope(l, j, bank, k_t, k_ready)
                        if REC0 <= m < REC0 + 4:
                            if m == REC0:
                                dve.wait_ge(decays_ready.sem, decays_ready.at(l, 1))
                                dve.wait_ge(roots_ready.sem, roots_ready.at(l, 1))
                            recurrence(l, m - REC0)
                        if name == "lru_out":
                            dve.wait_ge(slot_used.sem, slot_used.at(l, n + 1))
                            dve.wait_ge(ga_ready.sem, ga_ready.at(l, j + 1))
                            V.tensor_tensor(tiles(a5)[:, pair, :], pv, tiles(a5)[:, pair, :], ALU.mult)\
                             .then_inc(acc_ready.sem, 1)
                        elif name in V_HALF and j == 3:
                            dve.wait_ge(slot_used.sem, slot_used.at(l, n + 1))
                            V.tensor_copy(v_rows[1][:, D * V_HALF[name]:D * V_HALF[name] + D],
                                          ps[:, 6:8, :].rearrange("p a n -> p (a n)")).then_inc(v_ready1.sem, 1)
                        elif name == "sh":
                            dve.wait_ge(slot_used.sem, slot_used.at(l, n + 1))
                            if j == 0:
                                own.done(V.memset(prod_pad[:, :, 0:2], 0.0))
                            dve.wait_ge(sc_ready.sem, sc_ready.at(l, j + 1))
                            V.tensor_tensor(prod_pad[:, pair, 2:2 + S], pv, tiles(a1)[:, pair, :], ALU.mult)\
                             .then_inc(sh_ready.sem, 1)
                            dve.wait_ge(sh_ready.sem, sh_ready.at(l, j + 1))
                            for c in (2 * j, 2 * j + 1):
                                own.done(V.tensor_scalar(tiles(a1)[:, c, :], prod_pad[:, c, 2:2 + S],
                                                         lv[:, c, V_SW + 2:V_SW + 3], None, ALU.mult))
                                for tap in (1, 0):
                                    own.done(V.scalar_tensor_tensor(
                                        tiles(a1)[:, c, :], prod_pad[:, c, tap:tap + S],
                                        lv[:, c, V_SW + tap:V_SW + tap + 1], tiles(a1)[:, c, :], ALU.mult, ALU.add))
                        elif name == "ret_out" and j % 2 == 1:
                            g = j // 2
                            bb = (2 + 2 * g) % 4
                            dve.wait_ge(slot_used.sem, slot_used.at(l, n + 1))
                            dve.wait_ge(gb_ready.sem, gb_ready.at(l, g + 1))
                            tmp = mul2[:, g % 2, :].rearrange("p (a n) -> p a n", a=2)
                            own.done(V.tensor_tensor(tmp, ps[:, bb:bb + 2, 0:S], tiles(a4)[:, 2 * g:2 * g + 2, :], ALU.mult))
                            V.tensor_tensor(tiles(a5)[:, 2 * g:2 * g + 2, :], tiles(a5)[:, 2 * g:2 * g + 2, :], tmp,
                                            ALU.add).then_inc(ret_added.sem, 1)
                        elif name == "sb":
                            dve.wait_ge(slot_used.sem, slot_used.at(l, n + 1))
                            own.done(V.tensor_tensor(tiles(a1)[:, pair, :], pv, tiles(a1)[:, pair, :], ALU.mult))
                            split(tiles(a1)[:, pair, :], h_hi[:, pair, :], h_lo[:, pair, :], oc_ready.sem)
                        elif name == "sc_out":
                            dve.wait_ge(slot_used.sem, slot_used.at(l, n + 1))
                            dve.wait_ge(gc_ready.sem, gc_ready.at(l, j + 1))
                            tmp = mul2[:, j % 2, :].rearrange("p (a n) -> p a n", a=2)
                            own.done(V.tensor_tensor(tmp, pv, tiles(a4)[:, pair, :], ALU.mult))
                            own.done(V.tensor_tensor(tmp, tmp, tiles(a5)[:, pair, :], ALU.add))
                            split(tmp, u_hi[:, pair, :], u_lo[:, pair, :], mix_ready.sem)
                post(l, 1, FFN2)

            TWO_PI = 2 * np.pi
            C1 = 6.28125
            C2 = float(np.float32(np.round((TWO_PI - C1) * 2 ** 21) / 2 ** 21))
            C3 = float(np.float32(TWO_PI - C1 - C2))
            MAGIC = 1.5 * 2 ** 23
            PI_IN = float(np.nextafter(np.float32(np.pi), np.float32(0)))
            dve.sem_inc(ret_ready.sem, ret_ready.primed)
            dve.sem_inc(mul_ready.sem, mul_ready.primed)
            dve.sem_inc(act_ready.sem, act_ready.primed)
            dve.sem_inc(gated_x.sem, gated_x.primed)
            dve.wait_ge(pos_loaded, 32)
            ang, turns = a1[:, 0:S], a1[:, S:2 * S]
            own.done(V.tensor_copy(ang, a0[:, 0:S].bitcast(I32)))
            own.done(V.tensor_scalar(ang, ang, inv_freq[:, 0:1], None, ALU.mult))
            for r, shift in enumerate((0.0, 0.25)):
                arg = angle[:, r, :]
                own.done(V.tensor_scalar(turns, ang, 1.0 / TWO_PI, shift, ALU.mult, ALU.add))
                own.done(V.tensor_scalar(turns, turns, MAGIC, None, ALU.add))
                own.done(V.tensor_scalar(turns, turns, MAGIC, None, ALU.subtract))
                own.done(V.scalar_tensor_tensor(arg, turns, -C1, ang, ALU.mult, ALU.add))
                own.done(V.scalar_tensor_tensor(arg, turns, -C2, arg, ALU.mult, ALU.add))
                own.done(V.scalar_tensor_tensor(arg, turns, -C3, arg, ALU.mult, ALU.add))
                if shift:
                    own.done(V.tensor_scalar(arg, arg, float(np.pi / 2), None, ALU.add))
                own.done(V.tensor_scalar(arg, arg, PI_IN, -PI_IN, ALU.min, ALU.max))
            dve.sem_inc(angles, 1)
            dve.wait_ge(first_turned, 1)
            V.tensor_copy(first_gain[:, :], ps[:, 4, 0:KD]).then_inc(first_ready.sem, 1)
            dve.wait_ge(first_ready.sem, 1)
            for tt in range(TT):
                scales(0, 0, tt)
                half_rest(0, 0, tt)
            u_rests(0, 0, first, 0)
            rest(0, 1)
            own.restart()
            with dve.Fori(0, DEPTH) as l:
                feed_forward(l, 0, 0)
                dve.wait_ge(lv_ready.sem, lv_ready.at(l, 1))
                pre(l, 1, lv, V_GM, MIX0)
                mixer(l)
                pre(l, 2, lv, V_G2, FFN2)
                feed_forward(l, 1, FFN2)
                V.tensor_copy(first, vec[:, :, ds((l + 1) * NV, 1)]).then_inc(first_ready.sem, 1)
                dve.wait_ge(first_ready.sem, first_ready.at(l, 1))
                pre(l, 3, first, 0, SLOTS)
                own.restart()

            l = DEPTH
            for j in range(9):
                rest(l, j + 2)
                if j == 0:
                    dve.wait_ge(rel_done, 1)
                    V.tensor_tensor(rel, ps[0:NHEAD, 4, 0:REL], allowed, ALU.add).then_inc(rel_ready, 1)
            dve.wait_ge(b["v_turned"], 1)
            V.tensor_copy(a0[:, 512:640], ps[:, 6, 0:128]).then_inc(b["v_rows_b"], 1)
            V.tensor_copy(a0[:, 1152:1280], ps[:, 6, 128:256]).then_inc(b["v_rows_b"], 1)
            dve.wait_ge(b["sink_loaded"], 16)
            for h in range(NHEAD):
                band = (a1 if h % 10 < 5 else a2)
                s0 = (h % 5) * BIASW
                dve.wait_ge(b["scored"], h + 1)
                dve.wait_ge(b["bias_loaded0" if h % 2 == 0 else "bias_loaded1"], 16 * (h // 2 + 1))
                if h >= 2:
                    dve.wait_ge(b["turned"], h - 1)
                for tt in range(TT):
                    o = s0 + P * tt + S - 1
                    bias = band[:, o:o - S if o >= S else None:-1]
                    ins = V.scalar_tensor_tensor(act2[:, h % 2, S * tt:S * tt + S], ps[:, h % 2, S * tt:S * tt + S], 0.125,
                                                 bias, ALU.mult, ALU.add)
                ins.then_inc(b["logits"], 1)
                dve.wait_ge(b["logits"], h + 1)
                c = 4 * (h % 2)
                own.done(V.tensor_reduce(small[:, 24 + c:26 + c], act2[:, h % 2, :].rearrange("p (t n) -> p t n", t=2),
                                         AX_X, ALU.max))
                if h < 8:
                    own.done(V.tensor_scalar(small[:, 24 + c:26 + c], small[:, 24 + c:26 + c], sink[:, h:h + 1], -1.0,
                                             ALU.max, ALU.mult))
                else:
                    own.done(V.tensor_scalar(small[:, 24 + c:26 + c], small[:, 24 + c:26 + c], -1.0, None, ALU.mult))
                dve.sem_inc(b["row_max"], 1)
            dve.wait_ge(b["exps"], 2 * NHEAD + 16)
            own.done(V.tensor_tensor(probs[:, 0, 0:16], probs[:, 0, 0:16], probs[:, 1, 0:16], ALU.add))
            own.done(V.reciprocal(probs[:, 0, 0:32], probs[:, 0, 0:32]))
            dve.wait_ge(b["attended"], NHEAD)
            for tt in range(TT):
                for kind in range(2):
                    r = probs[:, 0, 16 * kind + tt:16 * kind + tt + 15:2].unsqueeze(2).broadcast_to([P, 8, 64])
                    o = a1[:, D * tt + 512 * kind:D * tt + 512 * kind + 512]
                    V.tensor_tensor(o.rearrange("p (h e) -> p h e", e=64),
                                    ps[:, 4 + 2 * tt + kind, :].rearrange("p (h e) -> p h e", e=64), r, ALU.mult)\
                     .then_inc(b["attn_rows"], 1)
            dve.wait_ge(b["attn_scale"], 1)
            for tt in range(TT):
                for kind in range(2):
                    ins = V.tensor_scalar(scaled[:, tt, 512 * kind:512 * kind + 512],
                                          a1[:, D * tt + 512 * kind:D * tt + 512 * kind + 512],
                                          pre_rs[:, 2 * tt + kind:2 * tt + kind + 1], None, ALU.mult)
                ins.then_inc(b["den_ready"], 1)
            u_rests(l, 1, vec, V2_GOUT)
            for j in range(B_O, B_UP - 2):
                rest(l, j + 2)
            post(l, 0, B_UP)
            pre(l, 1, vec, V2_GMLP, B_UP, t=2)
            for part in range(2):
                for j in range(16 + part):
                    n = (B_UP if part == 0 else B_UP2) + j
                    if n < B_GATE - 2:
                        rest(l, n + 2)
                    if n == B_DN2 + 4:
                        dve.wait_ge(b["p_head"], 1)
                        V.tensor_tensor(u_lo[:, 0:2, :], ps[:, 0, :].rearrange("p (a n) -> p a n", a=2), u_hi[:, 0:2, :],
                                        ALU.subtract).then_inc(b["p_ready"], 1)
                    if j < 8:
                        p = 8 * part + j
                        dve.wait_ge(b["relu_ready"], p + 1)
                        V.tensor_tensor(mul2[:, p % 2, :], act2[:, p % 2, :], act2[:, p % 2, :], ALU.mult)\
                         .then_inc(b["sq_ready"], 1)
                        dve.wait_ge(b["sq_ready"], p + 1)
                        split(mul2[:, p % 2, :].rearrange("p (a n) -> p a n", a=2), h_hi[:, 2 * j:2 * j + 2, :],
                              h_lo[:, 2 * j:2 * j + 2, :], b["hid_ready"])
            post(l, 1, B_GATE)
            rest(l, B_GATE)
            for k in range(KD):
                dve.wait_ge(u_head.sem, u_head.at(l, KD * 3 + (k | 1) + 1))
                V.tensor_tensor(u_lo[:, k, :], turned(l, 3, k), u_hi[:, k, :], ALU.subtract)\
                 .then_inc(u_ready.sem, 1)
            for n in range(B_GATE - 1, B_SLOTS - 2):
                rest(l, n + 2)
            dve.wait_ge(b["brow_loaded"], 16)
            dve.wait_ge(gain_loaded.sem, gain_loaded.at(l, 48))
            dve.wait_ge(b["ple_rows"], TT)

            def columns(a, q):
                return a[:, 512 * q:512 * q + 512]

            def gate_sums(tt):
                if tt == 0:
                    dve.wait_ge(rows_done.sem, rows_done.at(l, 3))
                else:
                    dve.wait_ge(slot_used.sem, slot_used.at(l, B_SLOTS))
                for q in (2 * tt, 2 * tt + 1):
                    V.tensor_tensor(columns(a3, q), ps[:, 4 + q, :], columns(a2, q % 2), ALU.add).then_inc(b["gate_in"], 1)

            def products(tt):
                for q in (2 * tt, 2 * tt + 1):
                    dve.wait_ge(b["gate_ready"], q + 1)
                    V.tensor_tensor(columns(a3, q), columns(a0, q), columns(a3, q), ALU.mult).then_inc(b["gated"], 1)
                for q in (2 * tt, 2 * tt + 1):
                    dve.wait_ge(b["gated"], q + 1)
                    V.tensor_tensor(columns(a4, q), columns(a3, q), columns(gain_row, q % 2), ALU.mult)\
                     .then_inc(b["ple_gained"], 1)

            def add(q):
                half = slice(512 * (q % 2), 512 * (q % 2) + 512)
                dve.wait_ge(b["ple_gained"], q + 1)
                dve.wait_ge(b["ple_scale"], q // 2 + 1)
                V.scalar_tensor_tensor(x[:, q // 2, half], columns(a4, q), post_rs[:, q // 2:q // 2 + 1],
                                       x[:, q // 2, half], ALU.mult, ALU.add).then_inc(b["out_ready"], 1)

            gate_sums(0)
            products(0)
            gate_sums(1)
            add(0)
            products(1)
            for q in (1, 2, 3):
                add(q)

        @block.tensor
        def _(pe):
            M = nc.tensor.matmul

            def column_slot(l, n, dst, act_hi, act_lo, k0=0, first=True, last=True, it=0, u_from=None):
                pe.wait_ge(split_done.sem, split_done.at(l, n + 1) + it * 4)
                hi, lo = col_view(w_hi, n % SPLIT), col_view(w_lo, n % SPLIT)
                for a, k in [(a, k) for a in range(2) for k in range(KD)]:
                    if a == 0 and u_from is not None:
                        pe.wait_ge(u_ready.sem, u_ready.at(l, u_from + k + 1))
                    c = slice(P * a, P * a + P)
                    M(dst[a], hi[:, k, c], act_hi[:, k0 + k, :], start=first and k == 0, stop=False)
                    M(dst[a], hi[:, k, c], act_lo[:, k0 + k, :], start=False, stop=False)
                    ins = M(dst[a], lo[:, k, c], act_hi[:, k0 + k, :], start=False, stop=last and k == KD - 1)
                ins.then_inc(slot_used.sem, 1)

            def row_slot(l, n, ks, act_hi, act_lo, first, last, bank0=4):
                pe.wait_ge(split_done.sem, split_done.at(l, n + 1))
                hi, lo = row_view(w_hi, n % SPLIT), row_view(w_lo, n % SPLIT)
                for i, k in enumerate(ks):
                    for tt in range(TT):
                        tok = slice(P * tt, P * tt + P)
                        f, e = first and i == 0, last and i == len(ks) - 1
                        for a, (stat, mov) in enumerate(((act_hi, hi), (act_hi, lo), (act_lo, hi))):
                            for half in range(2):
                                ins = M(ps[:, bank0 + 2 * tt + half, :], stat[:, k, tok],
                                        mov[:, i, 512 * half:512 * half + 512], start=f and a == 0, stop=e and a == 2)
                ins.then_inc(slot_used.sem, 1)

            def last_rows(l, i, n, ks, act_hi, act_lo):
                pe.wait_ge(split_done.sem, split_done.at(l, n + 1))
                hi, lo = row_view(w_hi, n % SPLIT), row_view(w_lo, n % SPLIT)
                for tt in range(TT):
                    tok = slice(P * tt, P * tt + P)
                    for r, k in enumerate(ks):
                        for a, (stat, mov) in enumerate(((act_hi, hi), (act_hi, lo), (act_lo, hi))):
                            for half in range(2):
                                ins = M(ps[:, 4 + 2 * tt + half, :], stat[:, k, tok],
                                        mov[:, r, 512 * half:512 * half + 512], start=False,
                                        stop=k == ks[-1] and a == 2)
                    ins.then_inc(rows_done.sem if tt == 0 else slot_used.sem, 1)

            def bank(i):
                return [ps[:, i, 0:S], ps[:, i, S:2 * S]]

            def keep_warm(n, bank=3):
                for _ in range(n):
                    M(ps[:, bank, 0:P], ident[:, :], ident[:, :], start=True, stop=True)

            def turn(l, i, src, sig, count):
                for tt in range(TT):
                    for k in range(KD):
                        if k % 4 == 0:
                            pe.wait_ge(sig, count(2 * tt + k // 4))
                        ins = nc.tensor.transpose(turned(l, i, k)[:, P * tt:P * tt + P], src[:, tt, P * k:P * k + P], ident[:, :])
                        if tt == TT - 1:
                            ins.then_inc(u_turned.sem, 1)

            def pre(l, i):
                keep_warm(WARM)
                turn(l, i, scaled, pre_scaled.sem, lambda q: pre_scaled.at(l, 4 * i + q + 1))

            def pair_slots(l, which, base, p, it=0):
                pair = FFN_PAIRS * which + p
                n = base + (2 * p if p < FIRST_PAIRS else FFN_IN2 + 2 * (p - FIRST_PAIRS))
                bk = (2 * which + 2 * p) % 4
                norm = 2 * which
                pe.wait_ge(act_ready.sem, act_ready.at(l, pair - 1) + it * 2)
                column_slot(l, n, bank(bk), u_hi, u_lo, it=it, u_from=KD * norm if p == 0 else None)
                pe.wait_ge(mul_ready.sem, mul_ready.at(l, pair - 1) + it * 2)
                column_slot(l, n + 1, bank(bk + 1), u_hi, u_lo, it=it)

            def feed_forward(l, which, base):
                with pe.Fori(0, FIRST_PAIRS // 2) as it:
                    for p in range(2):
                        pair_slots(l, which, base, p, it)
                for p in range(FIRST_PAIRS):
                    pe.wait_ge(h_ready.sem, h_ready.at(l, FFN_PAIRS * which + p + 1))
                    row_slot(l, base + 2 * FIRST_PAIRS + p, (2 * p, 2 * p + 1), h_hi, h_lo, p == 0, False)
                    if which == 0 and p == FIRST_PAIRS - 2:
                        for loaded, count in zip(vec_loaded, (1, 3, len(VECTORS) - 4)):
                            pe.wait_ge(loaded, 16 * count)
                        for k in range(KD):
                            ins = nc.tensor.transpose(ps[:, 0, NVEC * k:NVEC * k + NVEC], rows[0:NVEC, P * k:P * k + P],
                                                      ident[0:NVEC, 0:NVEC])
                        ins.then_inc(vec_turned.sem, 1)
                if which == 0:
                    pe.wait_ge(lv_ready.sem, lv_ready.at(l, 1))
                for p in range(FIRST_PAIRS, FFN_PAIRS):
                    pair_slots(l, which, base, p)
                for p in range(FIRST_PAIRS, FFN_PAIRS):
                    k = 2 * (p - FIRST_PAIRS)
                    pe.wait_ge(h_ready.sem, h_ready.at(l, FFN_PAIRS * which + p + 1))
                    n = base + FFN_OUT2 + 1 + p - FIRST_PAIRS
                    if p == FIRST_PAIRS:
                        row_slot(l, n - 1, (k,), h_hi, h_lo, False, False)
                        row_slot(l, n, (k + 1,), h_hi, h_lo, False, False)
                    elif p < FFN_PAIRS - 1:
                        row_slot(l, n, (k, k + 1), h_hi, h_lo, False, False)
                    else:
                        last_rows(l, 2 * which, n, (k, k + 1), h_hi, h_lo)

            def lru_gate(l, c):
                pe.wait_ge(xc_ready.sem, xc_ready.at(l, c + 1))
                pe.wait_ge(lru_w_loaded.sem, lru_w_loaded.at(l, 64))
                if c >= 4:
                    pe.wait_ge(lru_acts.sem, lru_acts.at(l, c - 3))
                for m in range(2):
                    ins = M(ps[:, 4 + c % 4, S * m:S * m + S], lru_w[:, m, c, :], tiles(a1)[:, c, :], start=True, stop=True)
                ins.then_inc(lru_gates.sem, 1)

            def scores(l, h):
                if h == 0:
                    pe.wait_ge(v_ready0.sem, v_ready0.at(l, 2))
                    pe.wait_ge(v_ready1.sem, v_ready1.at(l, 2))
                    pe.wait_ge(q_ready.sem, q_ready.at(l, 4))
                    pe.wait_ge(k_ready.sem, k_ready.at(l, 4))
                else:
                    pe.wait_ge(ret_probs.sem, ret_probs.at(l, h))
                for c in range(2):
                    M(ps[:, 4, 0:S], k_t[:, 2 * h + c, 0:P], q_t[:, 2 * h + c, :], start=c == 0, stop=c == 1)
                for c in range(2):
                    ins = M(ps[:, 4, S:S + P], k_t[:, 2 * h + c, P:S], q_t[:, 2 * h + c, P:S], start=c == 0, stop=c == 1)
                ins.then_inc(ret_scores.sem, 1)

            def attend(l, h):
                pe.wait_ge(ret_probs.sem, ret_probs.at(l, h + 1))
                if h >= 1:
                    pe.wait_ge(ret_ready.sem, ret_ready.at(l, h))
                pr, vs = probs[:, h % 2, :], slice(HV * h, HV * h + HV)
                M(ps[:, 5, :], pr[:, 0:P], v_rows[0][:, vs], start=True, stop=True)
                M(ps[:, 6, :], pr[:, P:S], v_rows[0][:, vs], start=True, stop=False)
                M(ps[:, 6, :], pr[:, S:S + P], v_rows[1][:, vs], start=False, stop=True).then_inc(ret_out.sem, 1)

            def turn_head(l, h):
                pe.wait_ge(ret_scaled.sem, ret_scaled.at(l, h + 1))
                for e in range(4):
                    for tt in range(TT):
                        o = S * (e % 2) + P * tt
                        ins = nc.tensor.transpose(ps[:, 6 + e // 2, o:o + P], mul2[:, tt, P * e:P * e + P], ident[:, :])
                ins.then_inc(ret_turned.sem, 1)

            EMPTIED = {"xa": xa_ready, "q": q_ready, "k": k_ready, "ya": gelu_ready, "ga": ga_ready, "lru_out": acc_ready,
                       "g": g_ready, "sc": sc_ready, "sh": sh_ready, "gb": gb_ready, "ret_out": ret_added,
                       "sb": oc_ready, "gc": gc_ready}
            BEFORE = {"q": "xa", "k": "q", "ya": "k", "ga": "ya", "lru_out": "ga", "g": "lru_out", "sc": "g",
                      "sh": "sc", "gb": "sh", "ret_out": "gb", "sb": "ret_out", "gc": "sb", "sc_out": "gc"}

            def mixer(l):
                for name, count in STAGES:
                    for j in range(count):
                        n = AT[name] + j
                        m = n - MIX0
                        if 0 <= m - GATE0 < KD:
                            lru_gate(l, m - GATE0)
                        if name == "g":
                            (scores if j % 2 == 0 else attend)(l, j // 2)
                        if name in V_HALF:
                            if name == "v0" and j == 0:
                                pe.wait_ge(lru_acts.sem, lru_acts.at(l, KD))
                            if name == "v1" and j == 0:
                                pe.wait_ge(v_ready0.sem, v_ready0.at(l, 1))
                                pe.wait_ge(v_ready1.sem, v_ready1.at(l, 1))
                            row_slot(l, n, (2 * j, 2 * j + 1), u_hi, u_lo, j == 0, j == 3)
                            continue
                        if name == "mix_out":
                            pe.wait_ge(mix_ready.sem, mix_ready.at(l, j + 1))
                            if j == 0:
                                pe.wait_ge(ret_ready.sem, ret_ready.at(l, HEADS))
                            if j < 3:
                                row_slot(l, n, (2 * j, 2 * j + 1), u_hi, u_lo, j == 0, False)
                            else:
                                last_rows(l, 1, n, (6, 7), u_hi, u_lo)
                            continue
                        if name == "ret_out":
                            g = j // 2
                            if j % 2 == 0:
                                if g < 2:
                                    pe.wait_ge(gb_ready.sem, gb_ready.at(l, 2 * g + 2))
                                else:
                                    pe.wait_ge(ret_added.sem, ret_added.at(l, g - 1))
                            if j == 0:
                                pe.wait_ge(ret_ready.sem, ret_ready.at(l, HEADS))
                            bb = (2 + 2 * g) % 4
                            column_slot(l, n, [ps[:, bb, 0:S], ps[:, bb + 1, 0:S]], h_hi, h_lo, KD * (j % 2),
                                        j % 2 == 0, j % 2 == 1)
                            continue
                        if name == "sb":
                            pe.wait_ge(ret_added.sem, ret_added.at(l, 3 + j // 2))
                        elif name == "g" and j >= 4:
                            pe.wait_ge(g_ready.sem, g_ready.at(l, j - 3))
                        elif name == "sc":
                            pe.wait_ge(g_ready.sem, g_ready.at(l, j + 5))
                        elif name != "xa":
                            before = EMPTIED[BEFORE[name]]
                            pe.wait_ge(before.sem, before.at(l, j + 1))
                        ah, al = u_hi, u_lo
                        if name == "lru_out":
                            ah, al = h_hi, h_lo
                            pe.wait_ge(oa_ready.sem, oa_ready.at(l, 4))
                        if name == "sc_out":
                            ah, al = h_hi, h_lo
                            pe.wait_ge(oc_ready.sem, oc_ready.at(l, 4))
                        column_slot(l, n, bank((2 + j) % 4), ah, al, u_from=KD if name == "xa" and j == 0 else None)
                        if name == "g" and j % 2 == 1:
                            turn_head(l, j // 2)

            pe.wait_ge(ident_ready, 1)
            pe.wait_ge(vec_loaded[0], 16)
            for k in range(KD):
                ins = nc.tensor.transpose(ps[:, 4, k:k + 1], rows[0:1, P * k:P * k + P], ident[0:1, 0:1])
            ins.then_inc(first_turned, 1)
            pre(0, 0)
            with pe.Fori(0, DEPTH) as l:
                feed_forward(l, 0, 0)
                pre(l, 1)
                mixer(l)
                pre(l, 2)
                feed_forward(l, 1, FFN2)
                pre(l, 3)

            l = DEPTH
            for j in range(9):
                if j >= 4:
                    pe.wait_ge(b["proj_ready"], j - 3)
                column_slot(l, j, bank(j % 4), u_hi, u_lo, u_from=0 if j == 0 else None)
                if j == 0:
                    pe.wait_ge(consts_loaded, 64)
                    M(ps[0:NHEAD, 4, 0:REL], table, onehot, start=True, stop=True).then_inc(rel_done, 1)
            pe.wait_ge(b["proj_ready"], 9)
            pe.wait_ge(rel_ready, 1)
            for tt in range(TT):
                for c in range(4):
                    nc.tensor.transpose(ps[:, 4 + tt, P * c:P * c + P], a5[:, S * c + P * tt:S * c + P * tt + P], ident[:, :])
            for tt in range(TT):
                ins = nc.tensor.transpose(ps[:, 6, P * tt:P * tt + P], a4[:, S + P * tt:S + P * tt + P], ident[:, :])
            ins.then_inc(b["v_turned"], 1)
            keep_warm(16, 7)
            pe.wait_ge(b["ka_swapped"], 32)
            pe.wait_ge(b["v_rows_a"], 2)
            pe.wait_ge(b["v_rows_b"], 2)

            def logits(h):
                part = slice(64 * (h % 2), 64 * (h % 2) + 64)
                if h < 8:
                    q_off = S * (h // 2)
                    k_off = 0 if h // 4 == h % 2 else 1536
                else:
                    q_off = 1024 + S * ((h - 8) // 2)
                    k_off = 512 + S * ((h - 8) // 2)
                if h >= 2:
                    pe.wait_ge(b["logits"], h - 1)
                keep_warm(WARM_HEAD, h % 2)
                for tt in range(TT):
                    ins = M(ps[:, h % 2, S * tt:S * tt + S], a3[part, q_off + P * tt:q_off + P * tt + P],
                            a4[part, k_off:k_off + S], start=True, stop=True)
                ins.then_inc(b["scored"], 1)

            def turn_exps(h):
                pe.wait_ge(b["exps"], 4 * (h + 1) if h < 8 else 32 + 2 * (h - 7))
                if h >= 2:
                    pe.wait_ge(b["exps_t"], h - 1)
                for kt in range(2):
                    for tt in range(TT):
                        ins = nc.tensor.transpose(ps[:, 2 + h % 2, S * kt + P * tt:S * kt + P * tt + P],
                                                  act2[:, h % 2, S * tt + P * kt:S * tt + P * kt + P], ident[:, :])
                ins.then_inc(b["turned"], 1)

            def weigh(h):
                pe.wait_ge(b["exps_t"], h + 1)
                kind = h // 8
                v_off = 512 + 64 * (h // 4) if kind == 0 else 64 * (h - 8)
                for tt in range(TT):
                    for kt in range(2):
                        ins = M(ps[:, 4 + 2 * tt + kind, 64 * (h % 8):64 * (h % 8) + 64],
                                mul2[:, h % 2, S * kt + P * tt:S * kt + P * tt + P],
                                a0[:, 640 * kt + v_off:640 * kt + v_off + 64], start=kt == 0, stop=kt == 1)
                ins.then_inc(b["attended"], 1)

            for h in range(NHEAD + 2):
                if h < NHEAD:
                    logits(h)
                if 1 <= h <= NHEAD:
                    turn_exps(h - 1)
                if h >= 2:
                    weigh(h - 2)
            keep_warm(WARM)
            turn(l, 1, scaled, b["den_ready"], lambda q: q // 2 + 1)
            for j in range(4):
                for k in (2 * j, 2 * j + 1):
                    pe.wait_ge(u_ready.sem, u_ready.at(l, KD + k + 1))
                if j < 3:
                    row_slot(l, B_O + j, (2 * j, 2 * j + 1), u_hi, u_lo, j == 0, False)
                else:
                    last_rows(l, 0, B_O + 3, (6, 7), u_hi, u_lo)
            keep_warm(WARM)
            turn(l, 2, scaled, pre_scaled.sem, lambda q: pre_scaled.at(l, 4 + q + 1))
            for part in range(2):
                for j in range(8):
                    p = 8 * part + j
                    if p >= 4:
                        pe.wait_ge(b["relu_ready"], p - 3)
                    column_slot(l, (B_UP if part == 0 else B_UP2) + j, bank((9 + p) % 4), u_hi, u_lo,
                                u_from=2 * KD if p == 0 else None)
                for j in range(8):
                    pe.wait_ge(b["hid_ready"], 8 * part + j + 1)
                    n = (B_DN if part == 0 else B_DN2) + j
                    if n == B_DN2 + 4:
                        pe.wait_ge(b["relu_ready"], 16)
                        pe.wait_ge(b["p_loaded"], 16)
                        for c in range(2):
                            for tt in range(TT):
                                ins = nc.tensor.transpose(ps[:, 0, S * c + P * tt:S * c + P * tt + P],
                                                          a1[:, S * tt + P * c:S * tt + P * c + P], ident[:, :])
                        ins.then_inc(b["p_turned"], 1)
                    if n == B_PLE:
                        pe.wait_ge(b["p_ready"], 1)
                        row_slot(l, B_PLE, (0, 1), u_hi, u_lo, True, True, bank0=0)
                    if j < 7 or part == 0:
                        row_slot(l, n + (n >= B_PLE), (2 * j, 2 * j + 1), h_hi, h_lo, part == 0 and j == 0, False)
                    else:
                        last_rows(l, 1, n + 1, (14, 15), h_hi, h_lo)
            pe.wait_ge(b["ple_rows"], TT)
            turn(l, 3, x, x_ready.sem, lambda q: x_ready.at(l, 4 + q + 1))
            for j in range(4):
                for k in (2 * j, 2 * j + 1):
                    pe.wait_ge(u_ready.sem, u_ready.at(l, 3 * KD + k + 1))
                if j < 3:
                    row_slot(l, B_GATE + j, (2 * j, 2 * j + 1), u_hi, u_lo, j == 0, False)
                else:
                    last_rows(l, 2, B_GATE + 3, (6, 7), u_hi, u_lo)


_INS = ["x", "positions", "ffn1_pre_g", "ffn1_w_in", "ffn1_w_out", "ffn1_post_g", "mix_pre_g", "w_mix_in",
        "lru_conv_w", "lru_conv_b", "lru_w_a", "lru_b_a", "lru_w_x", "lru_b_x", "lru_lambda", "w_lru_out",
        "w_ret_out", "sc_conv_w", "w_sc_out", "w_mix_out", "mix_post_g", "ffn2_pre_g", "ffn2_w_in", "ffn2_w_out",
        "ffn2_post_g", "p_2", "rel_bias_table_2", "g_pre_mix_2", "w_in_2", "sink_a_2", "g_out_a_2", "g_out_b_2",
        "w_o_2", "g_post_mix_2", "g_pre_mlp_2", "w_up_2", "w_down_2", "g_post_mlp_2", "w_ple_proj_2",
        "w_ple_gate_2", "b_ple_gate_2", "g_post_ple_2"]


def kernel(**inputs):
    import concourse.bacc as _bacc
    from concourse.bass_utils import run_bass_kernel_spmd as _run

    nc = _bacc.Bacc("TRN2", target_bir_lowering=False, num_devices=1)
    arrays, args = {}, {}

    def declare(name, a):
        arrays[f"in_{name}_dram"] = a
        args[name] = nc.dram_tensor(f"in_{name}_dram", a.shape, mybir.dt.from_np(a.dtype), kind="ExternalInput").ap()

    for name in _INS:
        declare(name, np.ascontiguousarray(inputs[name]))
    for name, a in constants().items():
        declare(name, a)
    out = nc.dram_tensor("out_0_dram", (1, S, D), F32, kind="ExternalOutput").ap()
    scratch = nc.dram_tensor("rel_scratch_dram", (NHEAD, 512), F32).ap()
    build(nc, args, out, scratch)
    r = _run(nc, [arrays], core_ids=[0])
    return r.results[0]["out_0_dram"]
```
